# Optimizing a Trainium2 kernel written in Bass

```python
import math
import jax, jax.numpy as jnp
from jax import lax
import numpy as np

D_MODEL = 1024
BATCH = 1
SEQ = 512
DEPTH = 2

EPS = 1e-6
NEG = -1e30
FORCE = 1e4

GDN_DK = 128
GDN_DV = 128
GDN_HEADS = (D_MODEL // 2) // GDN_DV
GDN_QK = GDN_HEADS * GDN_DK
GDN_V = GDN_HEADS * GDN_DV
GDN_CONV = 4
GDN_CHUNK = 64

NSA_DH = 64
NSA_HEADS = (D_MODEL // 2) // NSA_DH
NSA_GROUPS = 2
NSA_Q = NSA_HEADS * NSA_DH
NSA_KV = NSA_GROUPS * NSA_DH
CMP_LEN = 32
CMP_STRIDE = 16
CMP_HIDDEN = 2 * NSA_DH
SLC_LEN = 64
SLC_TOPK = 8
WINDOW = 512
Q_BLOCK = 128

GLA_HEADS = 4
GLA_DK = (D_MODEL // 2) // GLA_HEADS
GLA_DV = D_MODEL // GLA_HEADS
GLA_QK = GLA_HEADS * GLA_DK
GLA_V = GLA_HEADS * GLA_DV
GLA_RANK = 16
GLA_TAU = 16.0
GLA_CHUNK = 64

D_FF = ((8 * D_MODEL // 3 + 127) // 128) * 128
FFN_CONV = 3

EVEN_SPLITS = (2 * GDN_QK + GDN_V, GDN_HEADS, GDN_HEADS, GDN_V, NSA_Q, 6 * NSA_KV, 3 * NSA_HEADS)
EVEN_IN = 2 * GDN_QK + GDN_V + 2 * GDN_HEADS + GDN_V + NSA_Q + 6 * NSA_KV + 3 * NSA_HEADS
EVEN_OUT = GDN_V + NSA_Q
ODD_SPLITS = (GLA_QK, GLA_QK, GLA_V, GLA_V, GLA_RANK)
ODD_IN = 2 * GLA_QK + 2 * GLA_V + GLA_RANK

kernel_name = "hybrid_gdn_nsa_gla_convffn"

def split_last(x, sizes):
    idx = np.cumsum(sizes)[:-1].tolist()
    return jnp.split(x, idx, axis=-1)

def rms_norm(x, g):
    xf = x.astype(jnp.float32)
    y = xf * lax.rsqrt(jnp.mean(xf * xf, axis=-1, keepdims=True) + EPS)
    return (y * g.astype(jnp.float32)).astype(x.dtype)

def l2norm(x):
    xf = x.astype(jnp.float32)
    return xf * lax.rsqrt(jnp.sum(xf * xf, axis=-1, keepdims=True) + EPS)

def causal_dwconv(x, w):
    K, C = w.shape
    xp = jnp.pad(x, ((0, 0), (K - 1, 0), (0, 0)))
    return lax.conv_general_dilated(xp, w.astype(x.dtype)[:, None, :], window_strides=(1,), padding='VALID',
                                    dimension_numbers=('NWC', 'WIO', 'NWC'), feature_group_count=C)

def gated_delta_rule(q, k, v, beta, g):
    Bn, S, H, Dk = q.shape
    Dv = v.shape[-1]
    C = GDN_CHUNK
    N = S // C

    def chunks(a):
        a = a.astype(jnp.float32).reshape((Bn, N, C, H) + a.shape[3:])
        return jnp.moveaxis(a, 3, 1)

    q = chunks(q) * (Dk ** -0.5)
    k, v, beta, g = chunks(k), chunks(v), chunks(beta), chunks(g)
    G = jnp.cumsum(g, axis=-1)
    causal = jnp.tril(jnp.ones((C, C), dtype=bool))
    strict = jnp.tril(jnp.ones((C, C), dtype=bool), -1)
    decay = jnp.exp(jnp.where(causal, G[..., :, None] - G[..., None, :], -jnp.inf))
    kb = k * beta[..., None]
    a_kk = jnp.where(strict, jnp.einsum('bhncd,bhnmd->bhncm', kb, k) * decay, 0.0)
    rhs = jnp.concatenate([v * beta[..., None], kb * jnp.exp(G)[..., None]], axis=-1)
    sol = lax.linalg.triangular_solve(a_kk, rhs, left_side=True, lower=True, unit_diagonal=True)
    u, w = sol[..., :Dv], sol[..., Dv:]
    a_qk = jnp.einsum('bhncd,bhnmd->bhncm', q, k) * decay
    qg = q * jnp.exp(G)[..., None]
    g_last = G[..., -1]
    kd = k * jnp.exp(g_last[..., None] - G)[..., None]

    def step(state, inp):
        qg_n, kd_n, u_n, w_n, aqk_n, gl_n = inp
        v_new = u_n - jnp.einsum('bhcd,bhde->bhce', w_n, state)
        o = jnp.einsum('bhcd,bhde->bhce', qg_n, state) + jnp.einsum('bhcm,bhme->bhce', aqk_n, v_new)
        state = state * jnp.exp(gl_n)[..., None, None] + jnp.einsum('bhcd,bhce->bhde', kd_n, v_new)
        return state, o

    xs = tuple(jnp.moveaxis(a, 2, 0) for a in (qg, kd, u, w, a_qk, g_last))
    s0 = jnp.zeros((Bn, H, Dk, Dv), jnp.float32)
    _, o = lax.scan(step, s0, xs)
    return o.transpose(1, 0, 3, 2, 4).reshape(Bn, S, H, Dv)

def compress_blocks(x, pe, w1, b1, w2):
    Bn, G, S, dh = x.shape
    R = CMP_LEN // CMP_STRIDE
    P = x.reshape(Bn, G, S // CMP_STRIDE, CMP_STRIDE, dh)
    Nc = P.shape[2] - R + 1
    blocks = jnp.concatenate([P[:, :, i:i + Nc] for i in range(R)], axis=3)
    flat = (blocks + pe).reshape(Bn, G, Nc, CMP_LEN * dh)
    return jax.nn.silu(flat @ w1 + b1) @ w2

def nsa_attention(q, kc, vc, ks, vs, kw, vw, gate_logits, cmp_pe, cmp_w1, cmp_b1, cmp_w2):
    Bn, S, _ = q.shape
    G, Hg, dh = NSA_GROUPS, NSA_HEADS // NSA_GROUPS, NSA_DH
    scale = dh ** -0.5
    f32 = jnp.float32
    qh = q.astype(f32).reshape(Bn, S, G, Hg, dh).transpose(0, 2, 3, 1, 4)

    def kvh(a):
        return a.astype(f32).reshape(Bn, S, G, dh).transpose(0, 2, 1, 3)

    kc, vc, ks, vs, kw, vw = kvh(kc), kvh(vc), kvh(ks), kvh(vs), kvh(kw), kvh(vw)
    t = jnp.arange(S)

    k_cmp = compress_blocks(kc, cmp_pe[0], cmp_w1[0], cmp_b1[0], cmp_w2[0])
    v_cmp = compress_blocks(vc, cmp_pe[1], cmp_w1[1], cmp_b1[1], cmp_w2[1])
    Nc = k_cmp.shape[2]
    cmp_end = jnp.arange(Nc) * CMP_STRIDE + CMP_LEN - 1
    cmp_valid = cmp_end[None, :] <= t[:, None]
    s = jnp.einsum('bghsd,bgcd->bghsc', qh, k_cmp) * scale
    p_cmp = jnp.where(cmp_valid, jax.nn.softmax(jnp.where(cmp_valid, s, NEG), axis=-1), 0.0)
    o_cmp = jnp.einsum('bghsc,bgcd->bghsd', p_cmp, v_cmp)

    Ns = S // SLC_LEN
    c0 = np.arange(Nc)[:, None] * CMP_STRIDE
    s0 = np.arange(Ns)[None, :] * SLC_LEN
    overlap = np.clip(np.minimum(c0 + CMP_LEN, s0 + SLC_LEN) - np.maximum(c0, s0), 0, None) / CMP_STRIDE
    imp = jnp.einsum('bgsc,cj->bgsj', p_cmp.sum(axis=2), jnp.asarray(overlap, f32))
    blk = jnp.arange(Ns)[None, :]
    cur = (t // SLC_LEN)[:, None]
    slc_valid = blk <= cur
    forced = (blk == 0) | (blk == cur) | (blk == cur - 1)
    score = jnp.where(slc_valid, imp + jnp.where(forced, FORCE, 0.0), NEG)
    n_top = min(SLC_TOPK, Ns)
    _, sel = lax.top_k(score, n_top)

    QB = Q_BLOCK
    NQ = S // QB
    ksb = ks.reshape(Bn, G, Ns, SLC_LEN, dh)
    vsb = vs.reshape(Bn, G, Ns, SLC_LEN, dh)
    kw_pad = jnp.pad(kw, ((0, 0), (0, 0), (WINDOW, 0), (0, 0)))
    vw_pad = jnp.pad(vw, ((0, 0), (0, 0), (WINDOW, 0), (0, 0)))
    take = jax.vmap(jax.vmap(lambda blocks, ix: blocks[ix]))

    def block(args):
        i, q_i, sel_i = args
        t_i = i * QB + jnp.arange(QB)
        kg = take(ksb, sel_i).reshape(Bn, G, QB, n_top * SLC_LEN, dh)
        vg = take(vsb, sel_i).reshape(Bn, G, QB, n_top * SLC_LEN, dh)
        pos = (sel_i[..., None] * SLC_LEN + jnp.arange(SLC_LEN)).reshape(Bn, G, QB, n_top * SLC_LEN)
        m = (pos <= t_i[:, None])[:, :, None]
        s_sel = jnp.einsum('bghqd,bgqnd->bghqn', q_i, kg) * scale
        o_s = jnp.einsum('bghqn,bgqnd->bghqd', jax.nn.softmax(jnp.where(m, s_sel, NEG), axis=-1), vg)
        kwin = lax.dynamic_slice_in_dim(kw_pad, i * QB, WINDOW + QB, axis=2)
        vwin = lax.dynamic_slice_in_dim(vw_pad, i * QB, WINDOW + QB, axis=2)
        kpos = i * QB - WINDOW + jnp.arange(WINDOW + QB)
        mw = (kpos[None, :] <= t_i[:, None]) & (kpos[None, :] > t_i[:, None] - WINDOW) & (kpos[None, :] >= 0)
        s_win = jnp.einsum('bghqd,bgnd->bghqn', q_i, kwin) * scale
        o_w = jnp.einsum('bghqn,bgnd->bghqd', jax.nn.softmax(jnp.where(mw, s_win, NEG), axis=-1), vwin)
        return o_s, o_w

    q_blocks = jnp.moveaxis(qh.reshape(Bn, G, Hg, NQ, QB, dh), 3, 0)
    sel_blocks = jnp.moveaxis(sel.reshape(Bn, G, NQ, QB, n_top), 2, 0)
    o_s, o_w = lax.map(block, (jnp.arange(NQ), q_blocks, sel_blocks))
    o_s = jnp.moveaxis(o_s, 0, 3).reshape(Bn, G, Hg, S, dh)
    o_w = jnp.moveaxis(o_w, 0, 3).reshape(Bn, G, Hg, S, dh)

    gates = jax.nn.sigmoid(gate_logits.astype(f32)).reshape(Bn, S, 3, G, Hg).transpose(2, 0, 3, 4, 1)[..., None]
    o = gates[0] * o_cmp + gates[1] * o_s + gates[2] * o_w
    return o.transpose(0, 3, 1, 2, 4).reshape(Bn, S, NSA_Q)

def even_mixer(h, w_in, w_out, conv_w, A_log, dt_bias, o_norm, cmp_pe, cmp_w1, cmp_b1, cmp_w2):
    Bn, S, _ = h.shape
    qkv_a, beta_l, a_l, gate_a, q_b, kv_b, gate_b = split_last(h @ w_in, EVEN_SPLITS)
    qkv = jax.nn.silu(causal_dwconv(qkv_a, conv_w))
    qa, ka, va = split_last(qkv, (GDN_QK, GDN_QK, GDN_V))
    qa = l2norm(qa.reshape(Bn, S, GDN_HEADS, GDN_DK))
    ka = l2norm(ka.reshape(Bn, S, GDN_HEADS, GDN_DK))
    va = va.reshape(Bn, S, GDN_HEADS, GDN_DV)
    beta = jax.nn.sigmoid(beta_l.astype(jnp.float32))
    g = -jnp.exp(A_log.astype(jnp.float32)) * jax.nn.softplus(a_l.astype(jnp.float32) + dt_bias.astype(jnp.float32))
    oa = gated_delta_rule(qa, ka, va, beta, g)
    oa = rms_norm(oa, o_norm) * jax.nn.silu(gate_a.astype(jnp.float32).reshape(Bn, S, GDN_HEADS, GDN_DV))
    kc, vc, ks, vs, kw, vw = split_last(kv_b, (NSA_KV,) * 6)
    ob = nsa_attention(q_b, kc, vc, ks, vs, kw, vw, gate_b, cmp_pe, cmp_w1, cmp_b1, cmp_w2)
    o = jnp.concatenate([oa.reshape(Bn, S, GDN_V), ob], axis=-1).astype(h.dtype)
    return o @ w_out

def gla_chunked(q, k, v, log_a):
    Bn, S, H, Dk = q.shape
    Dv = v.shape[-1]
    C = GLA_CHUNK
    N = S // C

    def chunks(a):
        a = a.astype(jnp.float32).reshape(Bn, N, C, H, a.shape[-1])
        return jnp.moveaxis(a, 3, 1)

    q = chunks(q) * (Dk ** -0.5)
    k, v, log_a = chunks(k), chunks(v), chunks(log_a)
    b = jnp.cumsum(log_a, axis=3)
    b_last = b[..., -1:, :]
    qt = q * jnp.exp(b)
    kt = k * jnp.exp(-b)
    kh = k * jnp.exp(b_last - b)
    causal = jnp.tril(jnp.ones((C, C), dtype=bool))
    intra = jnp.where(causal, jnp.einsum('bhncd,bhnmd->bhncm', qt, kt), 0.0)
    o_intra = jnp.einsum('bhncm,bhnme->bhnce', intra, v)

    def step(state, inp):
        qt_n, kh_n, v_n, dl_n = inp
        o = jnp.einsum('bhcd,bhde->bhce', qt_n, state)
        state = state * jnp.exp(dl_n)[..., None] + jnp.einsum('bhcd,bhce->bhde', kh_n, v_n)
        return state, o

    xs = tuple(jnp.moveaxis(a, 2, 0) for a in (qt, kh, v, b_last[..., 0, :]))
    s0 = jnp.zeros((Bn, H, Dk, Dv), jnp.float32)
    _, o_inter = lax.scan(step, s0, xs)
    o = o_intra + jnp.moveaxis(o_inter, 0, 2)
    return o.transpose(0, 2, 3, 1, 4).reshape(Bn, S, H, Dv)

def odd_mixer(h, w_in, a_w2, a_b, o_norm, w_out):
    Bn, S, _ = h.shape
    q, k, v, r, a_lr = split_last(h @ w_in, ODD_SPLITS)
    log_a = jax.nn.log_sigmoid((a_lr @ a_w2 + a_b).astype(jnp.float32)) / GLA_TAU
    hd = lambda a, d: a.reshape(Bn, S, GLA_HEADS, d)
    o = gla_chunked(hd(q, GLA_DK), hd(k, GLA_DK), hd(v, GLA_DV), hd(log_a, GLA_DK))
    o = rms_norm(o, o_norm) * jax.nn.silu(hd(r, GLA_DV).astype(jnp.float32))
    return o.reshape(Bn, S, GLA_V).astype(h.dtype) @ w_out

def conv_ffn(h, w_in, conv_w, conv_b, w_out):
    u = causal_dwconv(h @ w_in, conv_w) + conv_b
    gate, val = jnp.split(u, 2, axis=-1)
    return (jax.nn.silu(gate) * val) @ w_out

def setup_inputs(seed: int = 0) -> dict:
    key = jax.random.key(seed)
    ks = jax.random.split(key, 24)
    NE = (DEPTH + 1) // 2
    NO = DEPTH // 2
    f32 = jnp.float32

    def dense(k, shape, fan_in):
        return jax.random.normal(k, shape, f32) * (fan_in ** -0.5)

    def gain(k, shape):
        return 1.0 + 0.05 * jax.random.normal(k, shape, f32)

    def small(k, shape, s=0.02):
        return s * jax.random.normal(k, shape, f32)

    dt = jnp.exp(jax.random.uniform(ks[10], (NE, GDN_HEADS), f32, math.log(1e-3), math.log(1e-1)))
    return {
        "x": jax.random.normal(ks[0], (BATCH, SEQ, D_MODEL), f32),
        "norm_gains": gain(ks[1], (DEPTH, 4, D_MODEL)),
        "ffn_w_in": dense(ks[2], (DEPTH, D_MODEL, 2 * D_FF), D_MODEL),
        "ffn_conv_w": dense(ks[3], (DEPTH, FFN_CONV, 2 * D_FF), FFN_CONV),
        "ffn_conv_b": small(ks[4], (DEPTH, 2 * D_FF)),
        "ffn_w_out": dense(ks[5], (DEPTH, D_FF, D_MODEL), D_FF),
        "hyb_w_in": dense(ks[6], (NE, D_MODEL, EVEN_IN), D_MODEL),
        "hyb_w_out": dense(ks[7], (NE, EVEN_OUT, D_MODEL), EVEN_OUT),
        "gdn_conv_w": dense(ks[8], (NE, GDN_CONV, 2 * GDN_QK + GDN_V), GDN_CONV),
        "gdn_A_log": jnp.log(jax.random.uniform(ks[9], (NE, GDN_HEADS), f32, 1.0, 16.0)),
        "gdn_dt_bias": dt + jnp.log(-jnp.expm1(-dt)),
        "gdn_o_norm": gain(ks[11], (NE, GDN_DV)),
        "nsa_cmp_pe": small(ks[12], (NE, 2, CMP_LEN, NSA_DH)),
        "nsa_cmp_w1": dense(ks[13], (NE, 2, CMP_LEN * NSA_DH, CMP_HIDDEN), CMP_LEN * NSA_DH),
        "nsa_cmp_b1": small(ks[14], (NE, 2, CMP_HIDDEN)),
        "nsa_cmp_w2": dense(ks[15], (NE, 2, CMP_HIDDEN, NSA_DH), CMP_HIDDEN),
        "gla_w_in": dense(ks[16], (NO, D_MODEL, ODD_IN), D_MODEL),
        "gla_a_w2": dense(ks[17], (NO, GLA_RANK, GLA_QK), GLA_RANK),
        "gla_a_b": small(ks[18], (NO, GLA_QK), 0.1),
        "gla_o_norm": gain(ks[19], (NO, GLA_DV)),
        "gla_w_out": dense(ks[20], (NO, GLA_V, D_MODEL), GLA_V),
    }

def reference(x, norm_gains, ffn_w_in, ffn_conv_w, ffn_conv_b, ffn_w_out,
              hyb_w_in, hyb_w_out, gdn_conv_w, gdn_A_log, gdn_dt_bias, gdn_o_norm,
              nsa_cmp_pe, nsa_cmp_w1, nsa_cmp_b1, nsa_cmp_w2,
              gla_w_in, gla_a_w2, gla_a_b, gla_o_norm, gla_w_out):
    for layer in range(DEPTH):
        h = rms_norm(x, norm_gains[layer, 0])
        if layer % 2 == 0:
            e = layer // 2
            mix = even_mixer(h, hyb_w_in[e], hyb_w_out[e], gdn_conv_w[e], gdn_A_log[e], gdn_dt_bias[e],
                             gdn_o_norm[e], nsa_cmp_pe[e], nsa_cmp_w1[e], nsa_cmp_b1[e], nsa_cmp_w2[e])
        else:
            o = layer // 2
            mix = odd_mixer(h, gla_w_in[o], gla_a_w2[o], gla_a_b[o], gla_o_norm[o], gla_w_out[o])
        x = x + rms_norm(mix, norm_gains[layer, 1])
        h = rms_norm(x, norm_gains[layer, 2])
        x = x + rms_norm(conv_ffn(h, ffn_w_in[layer], ffn_conv_w[layer], ffn_conv_b[layer], ffn_w_out[layer]),
                         norm_gains[layer, 3])
    return x


_drawn_inputs = setup_inputs


def setup_inputs(seed=0):
    import zlib

    import numpy as np

    out = dict(_drawn_inputs(seed))
    spreads = {}
    factors = {'nsa_cmp_pe': 4.612, 'nsa_cmp_b1': 4.79}
    for name, (base, spread) in spreads.items():
        noise = np.random.default_rng([zlib.crc32(name.encode()), seed]).standard_normal(out[name].shape)
        drawn = base * np.exp(spread * noise) if base else spread * noise
        out[name] = __import__('jax').numpy.asarray(drawn.astype(out[name].dtype))
    for name, factor in factors.items():
        out[name] = (out[name] * factor).astype(out[name].dtype)
    return out
```

```python
from contextlib import ExitStack

import concourse.bass as bass
from concourse import mybir

F32 = mybir.dt.float32
F16 = mybir.dt.float16
ALU = mybir.AluOpType
ACT = mybir.ActivationFunctionType
AX_X = mybir.AxisListType.X

P = 128
D = 1024
S = 512
DB = D // P
NT = S // P
EPS = 1e-6
NEG = -1e30
WS = 16.0
SLOTS = 4

H = 4
GC = 4
NH = 8
DH = 64
NC = 31
NCP = 32
CL, CS = 32, 16

DFF = 2816
FB = DFF // P
FC = 3
OUT_SUB = (8, 8, 6)

HIN, OUTB, FIN, GIN = 27, DB, 2 * FB, 25
C_HIN, O_HIN = 0, 0
C_HOUT, O_HOUT = C_HIN + HIN, O_HIN + HIN
C_F0, O_F0 = C_HOUT + OUTB, O_HOUT + OUTB
C_FO0, O_FO0 = C_F0 + FIN, O_F0 + FIN
C_GIN, O_GIN = C_FO0 + 3 * OUTB, O_FO0 + OUTB
C_GOUT, O_GOUT = C_GIN + GIN, O_GIN + GIN
C_F1, O_F1 = C_GOUT + OUTB, O_GOUT + OUTB
C_FO1, O_FO1 = C_F1 + FIN, O_F1 + FIN
C_END = C_FO1 + 3 * OUTB
C_FIN, O_FIN = (C_F0, C_F1), (O_F0, O_F1)
C_FOUT, O_FOUT = (C_FO0, C_FO1), (O_FO0, O_FO1)

W_HIN, W_HOUT, W_F0 = 0, HIN, HIN + OUTB
W_GIN = W_F0 + FIN
W_GOUT = W_GIN + GIN
W_F1 = W_GOUT + OUTB
W_FIN = (W_F0, W_F1)

ROWS, QKV, QB, KC, VC, KSW, VSW, GA = 0, 1, 13, 17, 18, 19, 21, 23
ALR, GQ, GK, GV, GR = 0, 1, 5, 9, 17

PARAM = {}
_at = 0
for _n, _w in (("gain", 8 * DB), ("fcw", 2 * FIN * FC), ("fcb", 2 * FIN), ("gcw", 12 * GC), ("alog", 1), ("dtb", 1),
               ("gon", 1), ("b1", 2), ("pe", 2 * CL), ("lon", 2), ("lab", 4)):
    PARAM[_n] = (_at, _at + _w)
    _at += _w
NPAR = _at

MASKS = {}
_at = 0
for _n, _w in (("ident", P), ("ones", P), ("strict", P), ("incl", P), ("lev", 7 * P), ("neg", S), ("seg", S),
               ("cadd", NT * NCP), ("c01", NT * NCP), ("sel", H * P)):
    MASKS[_n] = (_at, _at + _w)
    _at += _w
NMASK = _at


def build(nc, out_x, in_x, in_par, in_msk, in_w, in_fo, in_w1, in_w2, in_aw2):
    with ExitStack() as ctx:
        def sb(name, shape, dt=F32):
            return ctx.enter_context(nc.sbuf_tensor(name, shape, dt))

        def sem(name):
            return ctx.enter_context(nc.semaphore(name))

        bank = [ctx.enter_context(nc.psum_tensor(f"bank{i}", [P, S], F32)) for i in range(8)]

        x = sb("x", [P, DB, S])
        hh = sb("hh", [P, DB, S], F16)
        hl = sb("hl", [P, DB, S], F16)
        raw = sb("raw", [P, SLOTS, D])
        whi = sb("whi", [P, SLOTS, D], F16)
        wlo = sb("wlo", [P, SLOTS, D], F16)
        par = sb("par", [P, NPAR])
        msk = sb("msk", [P, NMASK])
        gain = sb("gain", [P, 8 * DB])
        fcw = sb("fcw", [P, 2 * FIN * FC])
        gcw = sb("gcw", [P, 12 * GC])
        hon = sb("hon", [P, 3])
        hf = sb("hf", [P, 2, S])
        rln = sb("rln", [P, S])
        rstd = sb("rstd", [P, S])
        epsc = sb("epsc", [P, 4])
        onec = sb("onec", [P, 1])
        CONSTS = 10
        ARENA = 29472
        arena = sb("arena", [P, ARENA])

        def pr(name, i=0, n=1):
            a = PARAM[name][0] + i
            return par[:, a:a + n]

        def mk(name):
            return msk[:, MASKS[name][0]:MASKS[name][1]]

        ident, ones = mk("ident"), mk("ones")

        def view(at, *dims):
            n = 1
            for d in dims:
                n *= d
            assert at + n <= ARENA, (at, n)
            v = arena[:, at:at + n]
            if len(dims) == 1:
                return v
            if len(dims) == 2:
                return v.rearrange("p (a b) -> p a b", b=dims[1])
            return v.rearrange("p (a b c) -> p a b c", b=dims[1], c=dims[2])

        y = view(0, DB, S)
        sq = view(4096, DB, S)
        gh = view(8192, FB * S // 2).bitcast(F16).rearrange("p (f s) -> p f s", s=S)
        gl = view(8192 + FB * S // 2, FB * S // 2).bitcast(F16).rearrange("p (f s) -> p f s", s=S)
        cu = view(19456, 4, S)
        gf = view(21504, S)

        QKVS = view(0, 12, S)
        AK = view(6144, H, NT, P)
        AQ = view(8192, H, NT, P)
        TT = view(10240, H, NT, P)
        UU = view(12288, H, NT, P)
        XX = view(14336, H, NT, P)
        BM = view(16384, H, NT, P)
        KD = view(18432, H, NT, P)
        EE = view(20480, 3, S)
        GAT = view(22016, H, S)
        QBS = view(24064, 4, S)
        KSWS = view(26112, 2, S)
        VTK = view(27136, 2, NT, P)
        VBD = view(28160, 2, 4 * DH)
        KCM = view(28672, NCP)
        SIG = view(28704, NT, 64)
        G = view(28960, S)[0:H]
        ROWT = view(20480, S)
        GZ = view(18944, 3, S)[0:H]
        BLK = view(6144, 2, CL, NC)
        HS = view(8192, 2, 2, NCP)
        KCF = view(8448, 2, S)
        VF = view(9472, 2, S)
        W1 = view(10496, 2, CL, P)
        W2 = view(18688, 2, P)
        SM = view(10496, 2, S)
        PP = view(11520, 2, S)
        PT = view(12544, 2, S)
        ACC = view(13568, NT, S)
        TMP = view(15616, S)
        CSC = view(16128, NT, NH * NCP)
        CPT = view(17152, NT, 2 * P)
        US, WT, OA = AK, XX, TT
        VN, SS, SD = BM[:, 0], BM[:, 1], BM[:, 2]

        small = sb("small", [P, 512])
        GT, BT, GLB, EGT, BEG, EKD, EGL = (small[:, 16 * i:16 * i + 16] for i in range(7))
        NMX = small[:, 112:114]
        LS = small[:, 128:144]
        RC = small[:, 144:152]
        CMX, CLS, CRC = small[:, 160:192], small[:, 192:224], small[:, 224:256]
        NA = small[:, 256:257]
        EBL = small[:, 288:320]
        DEC = small[:, 320:336]

        LQ = view(0, H, S)
        LK = view(2048, H, S)
        VTT = view(4096, NT, D)
        RS = view(8192, DB, S)
        LB = view(12288, H, S)
        VFF = view(14336, DB, S)
        KDT = view(14336, H, NT, P)
        LA = view(16384, H, NT, P)
        KKT = view(18432, 2, 1024)
        EX = view(20736, 3, S)
        QT = view(22272, 2, S)
        OO = view(23296, DB, S)
        LST = view(27392, H, 2 * P)
        ALRS = view(28416, S)
        LZ = view(18432, 4, S)
        AW2 = view(28928, S)

        s_par = sem("params_loaded")
        s_x = sem("x_loaded")
        s_w1 = sem("cmp_weights_loaded")
        s_aw = sem("gla_weights_loaded")
        s_cst = sem("constants_ready")
        w_dma = [sem(f"chunk_loaded{i}") for i in range(SLOTS)]
        w_hi = sem("chunk_high_ready")
        w_lo = sem("chunk_low_ready")
        w_used = sem("chunk_used")
        b_free = [sem(f"bank_read{i}") for i in range(SLOTS)]
        s_sq = sem("square_ready")
        s_sum = sem("sum_of_squares_ready")
        s_ln = sem("log_ready")
        s_rstd = sem("rstd_ready")
        s_yn = sem("y_normed")
        s_xr = sem("x_updated")
        s_hf = sem("h32_ready")
        s_hh = sem("h_high_ready")
        s_h = sem("h_ready")
        s_cv = sem("conv_started")
        s_c1 = sem("conv_stepped")
        s_silu = sem("gate_silu_ready")
        s_prod = sem("products_ready")
        s_gh = sem("g_high_ready")
        s_g = sem("g_ready")
        s_out = sem("output_stored")
        s_om = sem("mixer_output_ready")
        s_omh = sem("mixer_output_high_ready")
        v_link = sem("vector_step")
        a_link = sem("scalar_step")
        g_link = sem("pool_step")
        (s_qs, s_blk, s_hid, s_hs, s_kv, s_kcm, s_vt, s_vtk, s_rt, s_se, s_sg, s_cs, s_cm, s_ce, s_cp, s_ct, s_cpt,
         s_co, s_ca, s_s, s_m, s_e, s_t, s_pc, s_pv, s_o, s_cb, s_acc, s_at) = (sem(n) for n in (
             "qkv_ready", "cmp_blocks_ready", "cmp_hidden_summed", "cmp_hidden_ready", "cmp_kv_summed", "cmp_kv_ready",
             "v_transposed", "v_tokens_ready", "rows_transposed", "gate_exp_ready", "gates_ready",
             "cmp_scores", "cmp_scores_masked", "cmp_exp_ready", "cmp_probs_ready", "cmp_probs_transposed",
             "cmp_probs_t_ready", "cmp_out_summed", "cmp_out_ready", "scores_summed", "scores_masked", "probs_ready",
             "probs_transposed", "probs_t_ready", "pv_summed", "attention_summed", "attention_bank_read",
             "attention_ready", "attention_transposed"))
        (s_ga, s_g1, s_gg, s_gtr, s_gt, s_ge, s_gk, s_nq, s_ns, s_nl, s_nr, s_nn, s_gb, s_dd, s_d, s_ex, s_eg, s_e1,
         s_e2, s_qg, s_kk, s_qk, s_kt, s_vr, s_ak, s_aq, s_kd, s_bv) = (sem(n) for n in (
             "decay_exp_ready", "softplus_ready", "decays_cumulated", "decay_columns_summed", "decay_columns_ready",
             "decay_exps_ready", "decay_products_ready", "qk_square_ready", "qk_sum_ready", "qk_log_ready",
             "qk_rstd_ready", "qk_normed", "decay_row_spread", "decay_differences_ready", "decay_row_read",
             "decay_pair_exp_ready", "decay_row_exp_ready", "kk_decay_ready", "qk_decay_ready", "q_decayed",
             "kk_summed", "qk_summed", "k_transposed", "v_heads_transposed", "kk_ready", "qk_t_ready",
             "k_tokens_ready", "v_beta_ready"))
        (s_b, s_tt, s_ut, s_uu, s_xp, s_xx, s_zu, s_zt, s_u, s_w, s_us, s_wt, s_p2, s_vn, s_oo, s_ds, s_ss, s_oa,
         s_hq, s_hsum, s_hln, s_hr, s_on) = (sem(n) for n in (
             "level_blocks_ready", "inverse_ready", "inverse_transposed", "inverse_t_ready", "x_summed", "x_ready",
             "u_update_summed", "t_update_summed", "u_summed", "w_summed", "u_ready", "w_ready", "old_value_summed",
             "new_value_ready", "head_out_summed", "state_update_summed", "state_ready", "head_out_ready",
             "head_square_ready", "head_sum_ready", "head_log_ready", "head_rstd_ready", "head_out_gated"))
        (s_z, s_zl, s_zc, s_lb, s_bl, s_lx, s_le, s_lk, s_lg, s_lap, s_la, s_kp, s_kdt, s_vp, s_vv, s_lo, s_lds,
         s_lss, s_loo, s_lm) = (sem(n) for n in (
             "decay_logit_summed", "decay_log_ready", "decay_log_joined", "log_decays_cumulated", "chunk_decays_ready",
             "decay_to_end_ready", "gla_exps_ready", "gla_k_ready", "gla_decayed", "gla_kq_summed", "gla_kq_ready",
             "gla_k_transposed", "gla_k_tokens_ready", "gla_v_transposed", "gla_v_tokens_ready", "gla_out_summed",
             "gla_state_summed", "gla_state_ready", "gla_out_ready", "gla_k_mixed_ready"))

        vl, al, gl_ = [0], [0], [0]

        def link(eng, ins, signal, at):
            ins.then_inc(signal, 1)
            at[0] += 1
            eng.wait_ge(signal, at[0])

        def tiles(a):
            return a.rearrange("p (n c) -> p n c", c=P)

        def spread(a, n):
            return a.unsqueeze(1).to_broadcast([a.shape[0], n, a.shape[1]])

        def along(a, n):
            return a.unsqueeze(2).to_broadcast([a.shape[0], a.shape[1], n])

        def kb_of(c):
            for a in C_FOUT:
                if a <= c < a + 3 * OUTB:
                    return OUT_SUB[(c - a) % 3]
            return DB

        def load(sp, c, src, it=0, n=0):
            if c >= SLOTS:
                sp.wait_ge(w_lo, it * n + (c - SLOTS + 1))
            sp.dma_start(raw[:, c % SLOTS, 0:kb_of(c) * P], src).then_inc(w_dma[c % SLOTS], 16)

        def split_hi(act, c, it=0, n=0):
            if c >= C_END:
                return
            act.wait_ge(w_dma[c % SLOTS], it * (n // SLOTS * 16) + 16 * (c // SLOTS + 1))
            if c >= SLOTS:
                act.wait_ge(w_used, it * n + (c - SLOTS + 1))
            k = kb_of(c) * P
            act.activation(whi[:, c % SLOTS, 0:k], raw[:, c % SLOTS, 0:k], ACT.Copy, scale=WS).then_inc(w_hi, 1)

        def split_lo(dve, c, it=0, n=0):
            if c >= C_END:
                return
            dve.wait_ge(w_hi, it * n + (c + 1))
            k = kb_of(c) * P
            dve.scalar_tensor_tensor(out=wlo[:, c % SLOTS, 0:k], in0=raw[:, c % SLOTS, 0:k], scalar=WS,
                                     in1=whi[:, c % SLOTS, 0:k], op0=ALU.mult, op1=ALU.subtract).then_inc(w_lo, 1)

        def chunk(pe, c, o, mh, ml, k0=0, first=True, last=True, it=0, n=0):
            pe.wait_ge(w_lo, it * n + (c + 1))
            if first and o >= SLOTS:
                no = n if kb_of(c) == DB and n != 12 else 4
                pe.wait_ge(b_free[o % SLOTS], it * (no // SLOTS) + o // SLOTS)
            s, nk = c % SLOTS, kb_of(c)
            for k in range(nk):
                wh, wl = whi[:, s, k * P:(k + 1) * P], wlo[:, s, k * P:(k + 1) * P]
                pe.matmul(bank[o % SLOTS][:, :], wh, mh[:, k0 + k, :], start=(first and k == 0), stop=False)
                pe.matmul(bank[o % SLOTS][:, :], wh, ml[:, k0 + k, :], start=False, stop=False)
                m = pe.matmul(bank[o % SLOTS][:, :], wl, mh[:, k0 + k, :], start=False, stop=(last and k == nk - 1))
            m.then_inc(w_used, 1)

        def project(pe, c, o, count, peel=0):
            for i in range(peel):
                chunk(pe, c + i, o + i, hh, hl)
            with pe.Fori(0, (count - peel) // SLOTS) as it:
                for j in range(SLOTS):
                    chunk(pe, c + peel + j, o + peel + j, hh, hl, it=it, n=SLOTS)

        def summed(eng, c, it=0, n=0):
            eng.wait_ge(w_used, it * n + (c + 1))

        def was_read(eng, o, it=0, n=0):
            eng.wait_ge(b_free[o % SLOTS], it * (n // SLOTS) + (o // SLOTS + 1))

        def pe_sum(pe, e):
            if e:
                pe.wait_ge(s_ln, e)
            for d in range(DB):
                pe.wait_ge(s_sq, DB * e + d + 1)
                m = pe.matmul(bank[4][:, :], ones, sq[:, d, :], start=(d == 0), stop=(d == DB - 1))
            m.then_inc(s_sum, 1)

        def act_rstd(act, e):
            act.preload_act_table_set("natural_log_exp_and_others")
            act.wait_ge(s_sum, e + 1)
            act.activation(rln[:, :], bank[4][:, :], ACT.Ln, bias=epsc[:, 0:1]).then_inc(s_ln, 1)
            act.wait_ge(s_ln, e + 1)
            act.activation(rstd[:, :], rln[:, :], ACT.Exp, scale=-0.5).then_inc(s_rstd, 1)

        def act_pre(act, e):
            base = DB * (e // 2)
            if e == 0:
                act.wait_ge(s_x, 16)
            for d in range(DB):
                if e:
                    act.wait_ge(s_xr, base - DB + d + 1)
                act.activation(sq[:, d, :], x[:, d, :], ACT.Square).then_inc(s_sq, 1)
            act_rstd(act, e)
            for d in range(DB):
                act.wait_ge(s_hf, base + d + 1)
                act.activation(hh[:, d, :], hf[:, d % 2, :], ACT.Copy).then_inc(s_hh, 1)

        def dve_pre(dve, e):
            base = DB * (e // 2)

            def low(d):
                dve.wait_ge(s_hh, base + d + 1)
                dve.tensor_tensor(hl[:, d, :], hf[:, d % 2, :], hh[:, d, :], ALU.subtract).then_inc(s_h, 1)

            dve.wait_ge(s_rstd, e + 1)
            for d in range(DB):
                if d >= 2:
                    dve.wait_ge(s_h, base + d - 1)
                dve.scalar_tensor_tensor(out=hf[:, d % 2, :], in0=x[:, d, :], scalar=gain[:, e * DB + d:e * DB + d + 1],
                                         in1=rstd[:, :], op0=ALU.mult, op1=ALU.mult).then_inc(s_hf, 1)
                if d:
                    low(d - 1)
            low(DB - 1)

        def dve_post(dve, e):
            base = DB * (e // 2)

            def add(d):
                dve.wait_ge(s_yn, base + d + 1)
                dve.tensor_tensor(x[:, d, :], x[:, d, :], y[:, d, :], ALU.add).then_inc(s_xr, 1)

            dve.wait_ge(s_rstd, e + 1)
            for d in range(DB):
                dve.scalar_tensor_tensor(out=y[:, d, :], in0=y[:, d, :], scalar=gain[:, e * DB + d:e * DB + d + 1],
                                         in1=rstd[:, :], op0=ALU.mult, op1=ALU.mult).then_inc(s_yn, 1)
                if d:
                    add(d - 1)
            add(DB - 1)

        def act_output(act, c, o, d, it=0, nc_=0, no=0):
            summed(act, c, it, nc_)
            at = bass.ds(it * no + d, 1)
            src = bank[o % SLOTS][:, :].unsqueeze(1)
            act.activation(sq[:, at, :], src, ACT.Square, scale=1 / WS).then_inc(s_sq, 1)
            act.activation(y[:, at, :], src, ACT.Copy, scale=1 / WS).then_inc(b_free[o % SLOTS], 1)

        def act_outproj(act, c, o):
            with act.Fori(0, DB // SLOTS) as it:
                for j in range(SLOTS):
                    split_hi(act, c + j + 2, it, SLOTS)
                    act_output(act, c + j, o + j, j, it, SLOTS, SLOTS)

        def dve_outproj(dve, c):
            with dve.Fori(0, DB // SLOTS) as it:
                for j in range(SLOTS):
                    split_lo(dve, c + j + 2, it, SLOTS)

        def pe_ffn(pe, L):
            pe.wait_ge(s_h, DB * (2 * L + 2))
            project(pe, C_FIN[L], O_FIN[L], FIN)
            pe.wait_ge(s_g, FB * (L + 1))
            with pe.Fori(0, 2) as it:
                for j in range(SLOTS):
                    for u in range(3):
                        chunk(pe, C_FOUT[L] + 3 * j + u, O_FOUT[L] + j, gh, gl, 8 * u, u == 0, u == 2, it, 12)

        def act_ffn(act, L):
            act.preload_act_table_set("silu_and_others")
            c0, o0 = C_FIN[L], O_FIN[L]
            with act.Fori(0, FIN // SLOTS) as it:
                for j in range(SLOTS):
                    split_hi(act, c0 + j + 2, it, SLOTS)
                    summed(act, c0 + j, it, SLOTS)
                    if j % 2 == 0:
                        act.wait_ge(s_prod, it * 2 + (FB * L + j // 2 + 1))
                    k = it * SLOTS + (L * FIN + j)
                    act.activation(cu[:, j, :], bank[(o0 + j) % SLOTS][:, :], ACT.Identity,
                                   scale=fcw[:, bass.ds(k + 2 * 2 * FIN, 1)], bias=par[:, bass.ds(k + PARAM["fcb"][0], 1)]
                                   ).then_inc(s_cv, 1)
                    if j % 2 == 0:
                        was_read(act, o0 + j, it, SLOTS)
                        act.activation(cu[:, j, :], cu[:, j, :], ACT.Silu).then_inc(s_silu, 1)
            if L == 0:
                with act.Fori(0, 2) as it:
                    act_ffn_out(act, L, it)
            else:
                for it in range(2):
                    act_ffn_out(act, L, it)

        def act_ffn_out(act, L, it):
            for j in range(12):
                c = C_FOUT[L] + j
                if L == 0:
                    split_hi(act, c + 2, it, 12)
                else:
                    split_hi(act, c + 2 + 12 * it)
                if j % 3 == 2:
                    act_output(act, c, O_FOUT[L] + j // 3, j // 3, it, 12, 4)

        def dve_ffn(dve, L):
            c0, o0 = C_FIN[L], O_FIN[L]
            with dve.Fori(0, FIN // SLOTS) as it:
                for j in range(SLOTS):
                    split_lo(dve, c0 + j + 2, it, SLOTS)
                    k = it * SLOTS + (L * FIN + j)
                    b = bank[(o0 + j) % SLOTS]
                    dve.wait_ge(s_cv, it * SLOTS + (12 + L * FIN + j + 1))
                    dve.scalar_tensor_tensor(out=cu[:, j, 1:S], in0=b[:, 0:S - 1],
                                             scalar=fcw[:, bass.ds(k + 2 * FIN, 1)], in1=cu[:, j, 1:S],
                                             op0=ALU.mult, op1=ALU.add).then_inc(s_c1, 1)
                    dve.wait_ge(s_c1, it * SLOTS + (24 + L * FIN + j + 1))
                    dve.scalar_tensor_tensor(out=cu[:, j, 2:S], in0=b[:, 0:S - 2],
                                             scalar=fcw[:, bass.ds(k, 1)], in1=cu[:, j, 2:S],
                                             op0=ALU.mult, op1=ALU.add).then_inc(b_free[(o0 + j) % SLOTS], 1)
                    if j % 2:
                        p = it * 2 + (FB * L + j // 2 + 1)
                        at = bass.ds(it * 2 + j // 2, 1)
                        g32 = gf.unsqueeze(1)
                        dve.wait_ge(s_silu, p)
                        was_read(dve, o0 + j, it, SLOTS)
                        dve.tensor_tensor(gf, cu[:, j - 1, :], cu[:, j, :], ALU.mult).then_inc(s_prod, 1)
                        dve.wait_ge(s_prod, p + 2)
                        dve.tensor_copy(gh[:, at, :], g32).then_inc(s_gh, 1)
                        dve.wait_ge(s_gh, p)
                        dve.tensor_tensor(gl[:, at, :], g32, gh[:, at, :], ALU.subtract).then_inc(s_g, 1)
            if L == 0:
                with dve.Fori(0, 2) as it:
                    for j in range(12):
                        split_lo(dve, C_FOUT[L] + j + 2, it, 12)
            else:
                for c in range(C_FOUT[L], C_END):
                    split_lo(dve, c + 2)

        def act_hybrid_in(act):
            act.preload_act_table_set("silu_and_others")

            def silu(i):
                was_read(act, O_HIN + QKV + i)
                act.activation(QKVS[:, i, :], QKVS[:, i, :], ACT.Silu).then_inc(s_qs, 1)

            def leave(o, out, func=ACT.Copy, scale=1 / WS):
                act.activation(out, bank[o % SLOTS][:, :], func, scale=scale).then_inc(b_free[o % SLOTS], 1)

            split_hi(act, 0)
            split_hi(act, 1)
            for o in range(HIN):
                split_hi(act, o + 2)
                summed(act, o)
                if o == ROWS:
                    leave(o, ROWT)
                elif o < QB:
                    i = o - QKV
                    act.activation(QKVS[:, i, :], bank[o % SLOTS][:, :], ACT.Identity,
                                   scale=gcw[:, i * GC + 3:i * GC + 4]).then_inc(s_cv, 1)
                    if i:
                        silu(i - 1)
                elif o < KC:
                    if o == QB:
                        silu(11)
                    leave(o, QBS[:, o - QB, :], scale=DH ** -0.5 / WS)
                elif o < KSW:
                    leave(o, KCF[:, o - KC, :])
                elif o < VSW:
                    leave(o, KSWS[:, o - KSW, :])
                elif o < GA:
                    leave(o, VF[:, o - VSW, :])
                else:
                    leave(o, GAT[:, o - GA, :], ACT.Silu)

        def dve_hybrid_in(dve):
            split_lo(dve, 0)
            split_lo(dve, 1)
            for o in range(HIN):
                split_lo(dve, o + 2)
                if QKV <= o < QB:
                    i = o - QKV
                    dve.wait_ge(s_cv, i + 1)
                    for t in (1, 2, 3):
                        m = dve.scalar_tensor_tensor(
                            out=QKVS[:, i, t:S], in0=bank[o % SLOTS][:, 0:S - t], scalar=gcw[:, i * GC + 3 - t:i * GC + 4 - t],
                            in1=QKVS[:, i, t:S], op0=ALU.mult, op1=ALU.add)
                        if t < 3:
                            m.then_inc(s_c1, 1)
                            dve.wait_ge(s_c1, 2 * i + t)
                    m.then_inc(b_free[o % SLOTS], 1)

        def pe_compress(pe):
            for o in range(HIN - SLOTS, HIN):
                was_read(pe, o)
            pe.wait_ge(s_w1, 16 * 6)
            pe.wait_ge(s_blk, 4)
            for t in range(2):
                for g in range(2):
                    r = slice(g * DH, (g + 1) * DH)
                    for q in range(CL):
                        m = pe.matmul(bank[4 + g][:, t * NCP:t * NCP + NC], W1[r, t, q, :], BLK[r, t, q, :],
                                      start=(q == 0), stop=(q == CL - 1))
            m.then_inc(s_hid, 1)
            for b in range(2):
                for n in range(NT):
                    m = pe.transpose(bank[6 + b][:, n * P:(n + 1) * P], VF[:, b, n * P:(n + 1) * P], ident)
                m.then_inc(s_vt, 1)
            for n in range(NT):
                m = pe.transpose(bank[0][:, n * P:(n + 1) * P], ROWT[:, n * P:(n + 1) * P], ident)
            m.then_inc(s_rt, 1)
            pe.wait_ge(s_hs, 4)
            pe.matmul(bank[5][:, 0:2 * NCP], W2[:, 0, :], HS[:, 0, :, :].rearrange("p g c -> p (g c)"), start=True, stop=True)
            for g in range(2):
                m = pe.matmul(bank[5][0:NCP, 64 + g * DH:64 + (g + 1) * DH], HS[:, 1, g, :], W2[:, 1, 0:DH],
                              start=True, stop=True)
            m.then_inc(s_kv, 1)

        def dve_compress(dve):
            link(dve, dve.memset(HS[:, :, :, :], 0.0), v_link, vl)
            link(dve, dve.memset(VBD[:, :, :], 0.0), v_link, vl)
            pe_ = PARAM["pe"][0]
            for t in range(2):
                was_read(dve, O_HIN + KC + t)
                src = KCF[:, t, :].rearrange("p (c r) -> p r c", r=CS)
                for a in range(2):
                    dve.tensor_tensor(BLK[:, t, a * CS:(a + 1) * CS, :], src[:, :, a:a + NC],
                                      along(par[:, pe_ + t * CL + a * CS:pe_ + t * CL + (a + 1) * CS], NC),
                                      ALU.add).then_inc(s_blk, 1)
            for b in range(2):
                dve.wait_ge(s_vt, b + 1)
                dve.tensor_copy(VTK[:, b, :, :], tiles(bank[6 + b][:, :])).then_inc(s_vtk, 1)
            dve.wait_ge(s_se, 1)
            link(dve, dve.tensor_scalar(SIG[:, :, 0:56], SIG[:, :, 0:56], 1.0, None, ALU.add), v_link, vl)
            dve.reciprocal(SIG[:, :, 0:56], SIG[:, :, 0:56]).then_inc(s_sg, 1)
            dve.wait_ge(s_kv, 1)
            for g in range(2):
                r = slice(g * DH, (g + 1) * DH)
                dve.tensor_copy(KCM[r, :], bank[5][r, g * NCP:(g + 1) * NCP]).then_inc(s_kcm, 1)
            for i in range(4):
                dve.tensor_copy(VBD[i * NCP:(i + 1) * NCP, :, i * DH:(i + 1) * DH],
                                bank[5][0:NCP, 64:64 + 2 * DH].rearrange("p (g d) -> p g d", g=2)).then_inc(s_kcm, 1)

        def act_compress(act):
            act.wait_ge(s_hid, 1)
            act.wait_ge(v_link, 1)
            for t in range(2):
                for g in range(2):
                    act.activation(HS[:, t, g, 0:NC], bank[4 + g][:, t * NCP:t * NCP + NC], ACT.Silu,
                                   bias=pr("b1", t)).then_inc(s_hs, 1)
            act.preload_act_table_set("natural_log_exp_and_others")
            act.wait_ge(s_rt, 1)
            act.activation(SIG[:, :, 0:56], tiles(bank[0][:, :])[:, :, 32:88], ACT.Exp, scale=-1.0).then_inc(s_se, 1)
            link(act, act.activation(GZ[:, 0, :], ROWT[0:H, :], ACT.Identity, bias=pr("dtb")[0:H]), a_link, al)
            link(act, act.activation(GZ[:, 1, :], GZ[:, 0, :], ACT.Abs), a_link, al)
            link(act, act.activation(GZ[:, 1, :], GZ[:, 1, :], ACT.Exp, scale=-1.0), a_link, al)
            act.activation(GZ[:, 1, :], GZ[:, 1, :], ACT.Ln, bias=onec[0:H, 0:1]).then_inc(s_ga, 1)
            act.activation(NA[0:H, :], pr("alog")[0:H], ACT.Exp).then_inc(s_ga, 1)

        def dve_decays(dve):
            dve.wait_ge(s_ga, 2)
            link(dve, dve.scalar_tensor_tensor(out=GZ[:, 2, :], in0=GZ[:, 0, :], scalar=0.0, in1=GZ[:, 1, :],
                                               op0=ALU.max, op1=ALU.add), v_link, vl)
            link(dve, dve.tensor_scalar(GZ[:, 2, :], GZ[:, 2, :], NA[0:H, :], -1.0, ALU.mult, ALU.mult), v_link, vl)
            for n in range(NT):
                t = slice(n * P, (n + 1) * P)
                dve.tensor_tensor_scan(G[:, t], ones[0:H, :], GZ[:, 2, t], 0.0, ALU.mult, ALU.add).then_inc(s_gg, 1)

        def pe_cmp(pe):
            pe.wait_ge(s_kcm, 6)
            for g in range(2):
                r = slice(g * DH, (g + 1) * DH)
                for n in range(NT):
                    for h in range(4):
                        a = (n * 4 + h) * NCP
                        m = pe.matmul(bank[2 + g][:, a:a + NCP], QBS[r, h, n * P:(n + 1) * P], KCM[r, :],
                                      start=True, stop=True)
                m.then_inc(s_cs, 1)
            pe.wait_ge(s_cp, 1)
            for n in range(NT):
                for g in range(2):
                    m = pe.transpose(bank[2 + n // 2][:, (n % 2 * 2 + g) * P:(n % 2 * 2 + g + 1) * P],
                                     CSC[:, n, g * P:(g + 1) * P], ident)
                if n % 2:
                    m.then_inc(s_ct, 1)
            for n in range(NT):
                pe.wait_ge(s_cpt, n // 2 + 1)
                if n >= 2:
                    pe.wait_ge(s_ca, n - 1)
                for g in range(2):
                    m = pe.matmul(bank[6 + n % 2][:, g * 4 * DH:(g + 1) * 4 * DH], CPT[:, n, g * P:(g + 1) * P],
                                  VBD[:, g, :], start=True, stop=True)
                m.then_inc(s_co, 1)

        def heads(a):
            return a.rearrange("p n (h c) -> p n h c", c=NCP)

        def dve_cmp(dve):
            rows = CSC.rearrange("p n (h c) -> p (n h) c", c=NCP)
            cadd, c01 = mk("cadd").rearrange("p (n c) -> p n c", c=NCP), mk("c01").rearrange("p (n c) -> p n c", c=NCP)
            for a in range(2):
                dve.wait_ge(s_cs, a + 1)
                link(dve, dve.tensor_tensor(heads(CSC)[:, :, 4 * a:4 * a + 4, :],
                                            bank[2 + a][:, :].rearrange("p (n h c) -> p n h c", h=4, c=NCP),
                                            cadd.unsqueeze(2).to_broadcast([P, NT, 4, NCP]), ALU.add), v_link, vl)
            link(dve, dve.tensor_reduce(CMX, rows, AX_X, ALU.max), v_link, vl)
            dve.tensor_tensor(rows, rows, along(CMX, NCP), ALU.subtract).then_inc(s_cm, 1)
            dve.wait_ge(s_ce, 1)
            link(dve, dve.tensor_reduce(CLS, rows, AX_X, ALU.add), v_link, vl)
            link(dve, dve.reciprocal(CRC, CLS), v_link, vl)
            link(dve, dve.tensor_tensor(CRC.rearrange("p (n h) -> p n h", h=NH), CRC.rearrange("p (n h) -> p n h", h=NH),
                                        SIG[:, :, 32:40], ALU.mult), v_link, vl)
            link(dve, dve.tensor_tensor(rows, rows, along(CRC, NCP), ALU.mult), v_link, vl)
            dve.tensor_tensor(heads(CSC), heads(CSC), c01.unsqueeze(2).to_broadcast([P, NT, NH, NCP]),
                              ALU.mult).then_inc(s_cp, 1)
            for a in range(2):
                dve.wait_ge(s_ct, a + 1)
                dve.tensor_copy(CPT[:, 2 * a:2 * a + 2, :], bank[2 + a][:, :].rearrange("p (n c) -> p n c", n=2)
                                ).then_inc(s_cpt, 1)
            for n in range(NT):
                dve.wait_ge(s_co, n + 1)
                dve.tensor_copy(ACC[:, n, :], bank[6 + n % 2][:, :]).then_inc(s_ca, 1)

        UNITS = NT * 2 * NH

        def unit(u):
            return u // (2 * NH), u // NH % 2, u % NH, (u // (2 * NH) + 1) * P

        def pe_attention(pe):
            pe.wait_ge(s_vtk, 2)
            for u in range(UNITS + 2):
                if u < UNITS:
                    i, b, h, keys = unit(u)
                    r = slice(h // 4 * DH, h // 4 * DH + DH)
                    if u >= 2:
                        pe.wait_ge(s_m, u - 1)
                    pe.matmul(bank[4 + u % 2][:, 0:keys], QBS[r, h % 4, i * P:(i + 1) * P], KSWS[r, b, 0:keys],
                              start=True, stop=True).then_inc(s_s, 1)
                if 1 <= u <= UNITS:
                    w = u - 1
                    i = unit(w)[0]
                    pe.wait_ge(s_e, w + 1)
                    if w >= 2:
                        pe.wait_ge(s_pc, w - 1)
                    else:
                        pe.wait_ge(s_ca, NT)
                    for k in range(i + 1):
                        m = pe.transpose(bank[6 if w % 2 else 2][:, k * P:(k + 1) * P], PP[:, w % 2, k * P:(k + 1) * P], ident)
                    m.then_inc(s_t, 1)
                if u >= 2:
                    w = u - 2
                    i, b, h, keys = unit(w)
                    v = w // NH
                    pe.wait_ge(s_pc, w + 1)
                    if h == 0 and v >= 2:
                        pe.wait_ge(s_cb, v - 1)
                    for k in range(i + 1):
                        m = pe.matmul(bank[v % 2][:, h * DH:(h + 1) * DH], PT[:, w % 2, k * P:(k + 1) * P],
                                      VTK[:, b, k, h // 4 * DH:h // 4 * DH + DH], start=(k == 0), stop=(k == i))
                    m.then_inc(s_pv, 1)
                    if w % (2 * NH) == 6 and i:
                        pe_attention_out(pe, i - 1)
            pe_attention_out(pe, NT - 1)

        def pe_attention_out(pe, i):
            pe.wait_ge(s_acc, i + 1)
            if i:
                pe.wait_ge(s_om, i)
            for k in range(4):
                m = pe.transpose(bank[3][:, k * P:(k + 1) * P], ACC[:, i, k * P:(k + 1) * P], ident)
            m.then_inc(s_at, 1)

        def act_attention(act):
            act.wait_ge(s_cm, 1)
            act.activation(CSC[:, :, :], CSC[:, :, :], ACT.Exp).then_inc(s_ce, 1)

            def high(i):
                act.wait_ge(s_at, i + 1)
                act.activation(hh[:, 4:8, i * P:(i + 1) * P], tiles(bank[3][:, :]), ACT.Copy).then_inc(s_omh, 1)

            for u in range(UNITS):
                i, b, h, keys = unit(u)
                v = u // NH
                act.wait_ge(s_m, u + 1)
                if u >= 2:
                    act.wait_ge(s_t, u - 1)
                if h == 0 and v >= 2:
                    act.wait_ge(s_cb, v - 1)
                act.activation(PP[:, u % 2, 0:keys], SM[:, u % 2, 0:keys], ACT.Exp, scale=-1.0,
                               bias=NMX[:, u % 2:u % 2 + 1], accum_out=LS[:, v % 2 * NH + h:v % 2 * NH + h + 1]
                               ).then_inc(s_e, 1)
                if u % (2 * NH) == 12 and i:
                    high(i - 1)
            high(NT - 1)

        def dve_attention(dve):
            def low(i):
                dve.wait_ge(s_omh, i + 1)
                t = slice(i * P, (i + 1) * P)
                dve.tensor_tensor(hl[:, 4:8, t], tiles(bank[3][:, :]), hh[:, 4:8, t], ALU.subtract).then_inc(s_om, 1)

            def combine(v):
                i, b = v // 2, v % 2
                dve.wait_ge(s_pv, NH * (v + 1))
                link(dve, dve.reciprocal(RC, LS[:, b * NH:(b + 1) * NH]), v_link, vl)
                link(dve, dve.tensor_tensor(RC, RC, SIG[:, i, 40 + NH * b:48 + NH * b], ALU.mult), v_link, vl)
                dve.tensor_tensor(TMP.rearrange("p (h d) -> p h d", d=DH), bank[v % 2][:, :].rearrange("p (h d) -> p h d", d=DH),
                                  along(RC, DH), ALU.mult).then_inc(s_cb, 1)
                dve.wait_ge(s_cb, v + 1)
                m = dve.tensor_tensor(ACC[:, i, :], ACC[:, i, :], TMP, ALU.add)
                if b:
                    m.then_inc(s_acc, 1)
                else:
                    link(dve, m, v_link, vl)

            for u in range(UNITS + 1):
                if u < UNITS:
                    i, b, h, keys = unit(u)
                    dve.wait_ge(s_s, u + 1)
                    if u >= 2:
                        dve.wait_ge(s_e, u - 1)
                    dve.tensor_tensor_reduce(out=SM[:, u % 2, 0:keys], in0=bank[4 + u % 2][:, 0:keys],
                                             in1=mk("neg")[:, S - keys:S], scale=-1.0, scalar=3e38, op0=ALU.add,
                                             op1=ALU.min, accum_out=NMX[:, u % 2:u % 2 + 1]).then_inc(s_m, 1)
                if u >= 1:
                    w = u - 1
                    keys = unit(w)[3]
                    dve.wait_ge(s_t, w + 1)
                    if w >= 2:
                        dve.wait_ge(s_pv, w - 1)
                    dve.tensor_copy(PT[:, w % 2, 0:keys], bank[6 if w % 2 else 2][:, 0:keys]).then_inc(s_pc, 1)
                if u % NH == 3 and u >= NH:
                    combine(u // NH - 1)
                if u % (2 * NH) == 14 and u > 2 * NH:
                    low(u // (2 * NH) - 1)
            combine(2 * NT - 1)
            low(NT - 1)

        def pe_gdn_prep(pe):
            for n in range(NT):
                pe.wait_ge(s_gg, n + 1)
                pe.transpose(bank[6][:, n * H:(n + 1) * H], G[:, n * P:(n + 1) * P], ident[0:H, 0:H])
            for h in range(H):
                m = pe.matmul(bank[6][:, 16 + h * NT:16 + (h + 1) * NT], mk("sel")[0:H, h * P:(h + 1) * P],
                              G[:, P - 1:S:P], start=True, stop=True)
            m.then_inc(s_gtr, 1)
            for i in range(8):
                pe.wait_ge(s_nq, i + 1)
                if i >= 2:
                    pe.wait_ge(s_nl, i - 1)
                pe.matmul(bank[i % 2][:, :], ones, EE[:, i % 2, :], start=True, stop=True).then_inc(s_ns, 1)
            for h in range(H):
                if h:
                    pe.wait_ge(s_eg, h)
                pe.matmul(bank[4][:, :], mk("sel")[0:H, h * P:(h + 1) * P], G[:, :], start=True, stop=True).then_inc(s_gb, 1)
                pe.wait_ge(s_nn, 5 + h)
                if h:
                    pe.wait_ge(s_ak, h)
                else:
                    pe.wait_ge(s_gt, 2)
                q, k, v = (tiles(QKVS[:, a + h, :]) for a in (0, 4, 8))
                for n in range(NT):
                    m = pe.matmul(bank[5][:, n * P:(n + 1) * P], k[:, n, :], k[:, n, :], start=True, stop=True)
                m.then_inc(s_kk, 1)
                if h:
                    pe.wait_ge(s_aq, h)
                for n in range(NT):
                    m = pe.matmul(bank[6][:, n * P:(n + 1) * P], k[:, n, :], q[:, n, :], start=True, stop=True)
                m.then_inc(s_qk, 1)
                if h:
                    pe.wait_ge(s_kd, h)
                for n in range(NT):
                    m = pe.transpose(bank[7][:, n * P:(n + 1) * P], k[:, n, :], ident)
                m.then_inc(s_kt, 1)
                if h:
                    pe.wait_ge(s_bv, h)
                else:
                    pe.wait_ge(s_nl, 8)
                for n in range(NT):
                    m = pe.transpose(bank[0][:, n * P:(n + 1) * P], v[:, n, :], ident)
                m.then_inc(s_vr, 1)

        def act_gdn_prep(act):
            act.wait_ge(s_gt, 2)
            act.activation(EGT, GT, ACT.Exp).then_inc(s_ge, 1)
            act.activation(EGL, GLB, ACT.Exp).then_inc(s_ge, 1)
            act.wait_ge(s_gk, 1)
            act.activation(EKD, EKD, ACT.Exp).then_inc(s_ge, 1)

            def rst(i):
                act.wait_ge(s_ns, i + 1)
                if i >= 2:
                    act.wait_ge(s_nn, i - 1)
                act.activation(hf[:, i % 2, :], bank[i % 2][:, :], ACT.Ln, bias=epsc[:, 1:2]).then_inc(s_nl, 1)
                act.wait_ge(s_nl, i + 1)
                act.activation(hf[:, i % 2, :], hf[:, i % 2, :], ACT.Exp, scale=-0.5).then_inc(s_nr, 1)

            for i in range(8):
                act.wait_ge(s_qs, i + 1)
                if i >= 2:
                    act.wait_ge(s_ns, i - 1)
                act.activation(EE[:, i % 2, :], QKVS[:, i, :], ACT.Square).then_inc(s_nq, 1)
                if i:
                    rst(i - 1)
            rst(7)
            for h in range(H):
                act.wait_ge(s_dd, 2 * (h + 1))
                act.activation(EE[:, 0, :], EE[:, 0, :], ACT.Exp, scale=-1.0).then_inc(s_ex, 1)
                act.activation(EE[:, 1, :], EE[:, 1, :], ACT.Exp).then_inc(s_ex, 1)
                if h:
                    act.wait_ge(s_qg, h)
                act.activation(EE[:, 2, :], bank[4][:, :], ACT.Exp).then_inc(s_eg, 1)

        def pool_gdn(pool):
            for h in range(H):
                pool.wait_ge(s_ex, 2 * h + 1)
                link(pool, pool.tensor_tensor(tiles(EE[:, 0, :]), tiles(EE[:, 0, :]), spread(mk("strict"), NT), ALU.mult),
                     g_link, gl_)
                pool.tensor_tensor(tiles(EE[:, 0, :]), tiles(EE[:, 0, :]), along(BT[:, h * NT:(h + 1) * NT], P),
                                   ALU.mult).then_inc(s_e1, 1)
                pool.wait_ge(s_ex, 2 * h + 2)
                pool.tensor_tensor(tiles(EE[:, 1, :]), tiles(EE[:, 1, :]), spread(mk("incl"), NT),
                                   ALU.mult).then_inc(s_e2, 1)
                pool.wait_ge(s_eg, h + 1)
                pool.wait_ge(s_qk, h + 1)
                pool.tensor_tensor(QKVS[:, h, :], QKVS[:, h, :], EE[:, 2, :], ALU.mult).then_inc(s_qg, 1)
            for lv in range(7):
                for h in range(H):
                    if lv == 0:
                        pool.wait_ge(s_ak, h + 1)
                    elif lv == 1:
                        pool.wait_ge(s_tt, h + 1)
                    else:
                        pool.wait_ge(s_xp, (lv - 2) * H + h + 1)
                    m = mk("lev")[:, lv * P:(lv + 1) * P]
                    pool.tensor_tensor(BM[:, h, :, :], AK[:, h, :, :], spread(m, NT), ALU.mult).then_inc(s_b, 1)

        def dve_gdn_prep(dve):
            dve.wait_ge(s_gtr, 1)
            dve.wait_ge(s_sg, 1)
            dve.tensor_copy(GT.rearrange("p (h n) -> p n h", n=NT), bank[6][:, 0:16].rearrange("p (n h) -> p n h", n=NT)
                            ).then_inc(s_gt, 1)
            dve.tensor_copy(GLB, bank[6][:, 16:32]).then_inc(s_gt, 1)
            link(dve, dve.tensor_copy(BT.rearrange("p (h n) -> p n h", n=NT), SIG[:, :, 0:H]), v_link, vl)
            dve.wait_ge(s_gt, 2)
            dve.tensor_tensor(EKD, GLB, GT, ALU.subtract).then_inc(s_gk, 1)
            dve.wait_ge(s_ge, 1)
            dve.tensor_tensor(BEG, BT, EGT, ALU.mult).then_inc(s_gk, 1)
            for i in range(8):
                dve.wait_ge(s_nr, i + 1)
                if i < 4:
                    dve.scalar_tensor_tensor(out=QKVS[:, i, :], in0=QKVS[:, i, :], scalar=P ** -0.5, in1=hf[:, i % 2, :],
                                             op0=ALU.mult, op1=ALU.mult).then_inc(s_nn, 1)
                else:
                    dve.tensor_tensor(QKVS[:, i, :], QKVS[:, i, :], hf[:, i % 2, :], ALU.mult).then_inc(s_nn, 1)
            dve.wait_ge(s_ge, 3)
            dve.wait_ge(s_gk, 2)
            for h in range(H):
                c = slice(h * NT, (h + 1) * NT)
                dve.wait_ge(s_gb, h + 1)
                if h:
                    dve.wait_ge(s_aq, h)
                dve.tensor_tensor(tiles(EE[:, 0, :]), tiles(bank[4][:, :]), along(GT[:, c], P), ALU.subtract).then_inc(s_d, 1)
                dve.wait_ge(s_d, h + 1)
                dve.tensor_scalar(EE[:, 1, :], EE[:, 0, :], 0.0, None, ALU.min).then_inc(s_dd, 1)
                dve.tensor_scalar(EE[:, 0, :], EE[:, 0, :], 0.0, None, ALU.max).then_inc(s_dd, 1)
                dve.wait_ge(s_kt, h + 1)
                dve.tensor_tensor(KD[:, h, :, :], tiles(bank[7][:, :]), along(EKD[:, c], P), ALU.mult)
                dve.tensor_tensor(tiles(QKVS[:, 4 + h, :]), tiles(bank[7][:, :]), along(BEG[:, c], P),
                                  ALU.mult).then_inc(s_kd, 1)
                dve.wait_ge(s_vr, h + 1)
                dve.tensor_tensor(tiles(QKVS[:, 8 + h, :]), tiles(bank[0][:, :]), along(BT[:, c], P),
                                  ALU.mult).then_inc(s_bv, 1)
                dve.wait_ge(s_e1, h + 1)
                dve.tensor_tensor(AK[:, h, :, :], tiles(bank[5][:, :]), tiles(EE[:, 0, :]), ALU.mult).then_inc(s_ak, 1)
                dve.wait_ge(s_e2, h + 1)
                dve.tensor_tensor(AQ[:, h, :, :], tiles(bank[6][:, :]), tiles(EE[:, 1, :]), ALU.mult).then_inc(s_aq, 1)

        def pe_inverse(pe):
            for h in range(H):
                pe.wait_ge(s_tt, h + 1)
                if h == 0:
                    pe.wait_ge(s_bv, H)
                for n in range(NT):
                    m = pe.transpose(bank[h][:, n * P:(n + 1) * P], TT[:, h, n, :], ident)
                m.then_inc(s_ut, 1)
            for lv in range(1, 7):
                for h in range(H):
                    pe.wait_ge(s_uu, (lv - 1) * H + h + 1)
                    pe.wait_ge(s_b, lv * H + h + 1)
                    pe.wait_ge(s_tt, (lv - 1) * H + h + 1)
                    for n in range(NT):
                        m = pe.matmul(bank[h][:, n * P:(n + 1) * P], BM[:, h, n, :], UU[:, h, n, :], start=True, stop=True)
                    m.then_inc(s_xp, 1)
                for h in range(H):
                    pe.wait_ge(s_xx, (lv - 1) * H + h + 1)
                    if lv == 1:
                        pe.wait_ge(s_aq, H)
                    for n in range(NT):
                        m = pe.matmul(bank[4 + h][:, n * P:(n + 1) * P], TT[:, h, n, :], XX[:, h, n, :], start=True, stop=True)
                    m.then_inc(s_zu, 1)
                for h in range(H):
                    if lv == 6:
                        break
                    for n in range(NT):
                        m = pe.matmul(bank[h][:, n * P:(n + 1) * P], XX[:, h, n, :], TT[:, h, n, :], start=True, stop=True)
                    m.then_inc(s_zt, 1)

        def dve_inverse(dve):
            for h in range(H):
                dve.wait_ge(s_b, h + 1)
                dve.tensor_tensor(TT[:, h, :, :], spread(ident, NT), BM[:, h, :, :], ALU.subtract).then_inc(s_tt, 1)
            for h in range(H):
                dve.wait_ge(s_ut, h + 1)
                dve.tensor_copy(UU[:, h, :, :], tiles(bank[h][:, :])).then_inc(s_uu, 1)
            for lv in range(1, 7):
                for h in range(H):
                    dve.wait_ge(s_zu, (lv - 1) * H + h + 1)
                    dve.tensor_tensor(UU[:, h, :, :], UU[:, h, :, :], tiles(bank[4 + h][:, :]), ALU.subtract).then_inc(s_uu, 1)
                for h in range(H):
                    if lv == 6:
                        break
                    dve.wait_ge(s_zt, (lv - 1) * H + h + 1)
                    dve.tensor_tensor(TT[:, h, :, :], TT[:, h, :, :], tiles(bank[h][:, :]), ALU.subtract).then_inc(s_tt, 1)

        def act_inverse(act):
            for i in range(6 * H):
                act.wait_ge(s_xp, i + 1)
                act.activation(XX[:, i % H, :, :], tiles(bank[i % H][:, :]), ACT.Copy).then_inc(s_xx, 1)

        def pe_gdn_scan(pe):
            for h in range(H):
                pe.wait_ge(s_uu, 6 * H + h + 1)
                for n in range(NT):
                    m = pe.matmul(bank[h][:, n * P:(n + 1) * P], UU[:, h, n, :], QKVS[:, 8 + h, n * P:(n + 1) * P],
                                  start=True, stop=True)
                m.then_inc(s_u, 1)
                for n in range(NT):
                    m = pe.matmul(bank[4 + h][:, n * P:(n + 1) * P], QKVS[:, 4 + h, n * P:(n + 1) * P], UU[:, h, n, :],
                                  start=True, stop=True)
                m.then_inc(s_w, 1)
            for n in range(NT):
                if n:
                    pe.wait_ge(s_ss, n)
                    for h in range(H):
                        m = pe.matmul(bank[0][:, h * P:(h + 1) * P], WT[:, h, n, :], SS[:, h, :],
                                      start=True, stop=True)
                    m.then_inc(s_p2, 1)
                pe.wait_ge(s_vn, n + 1)
                if n == 0:
                    pe.wait_ge(s_wt, H)
                if n < NT - 1:
                    for h in range(H):
                        m = pe.matmul(bank[1][:, h * P:(h + 1) * P], KD[:, h, n, :], VN[:, h, :], start=True, stop=True)
                    m.then_inc(s_ds, 1)
                for h in range(H):
                    o = bank[4 + n][:, h * P:(h + 1) * P]
                    if n:
                        pe.matmul(o, SS[:, h, :], QKVS[:, h, n * P:(n + 1) * P], start=True, stop=False)
                    m = pe.matmul(o, VN[:, h, :], AQ[:, h, n, :], start=(n == 0), stop=True)
                m.then_inc(s_oo, 1)
            for h in range(H):
                pe.wait_ge(s_hq, h + 1)
                pe.matmul(bank[h][:, :], ones, EE[:, h % 2, :], start=True, stop=True).then_inc(s_hsum, 1)

        def act_gdn_scan(act):
            for h in range(H):
                act.wait_ge(s_u, h + 1)
                act.activation(US[:, h, :, :], tiles(bank[h][:, :]), ACT.Copy).then_inc(s_us, 1)
                act.wait_ge(s_w, h + 1)
                act.activation(WT[:, h, :, :], tiles(bank[4 + h][:, :]), ACT.Copy).then_inc(s_wt, 1)
            for n in range(NT):
                act.wait_ge(s_oo, n + 1)
                act.activation(OA[:, :, n, :], tiles(bank[4 + n][:, :]), ACT.Copy).then_inc(s_oa, 1)
            act.wait_ge(s_oa, NT)

            def rst(h):
                act.wait_ge(s_hsum, h + 1)
                if h >= 2:
                    act.wait_ge(s_on, h - 1)
                act.activation(hf[:, h % 2, :], bank[h][:, :], ACT.Ln, bias=epsc[:, 2:3]).then_inc(s_hln, 1)
                act.wait_ge(s_hln, h + 1)
                act.activation(hf[:, h % 2, :], hf[:, h % 2, :], ACT.Exp, scale=-0.5).then_inc(s_hr, 1)

            for h in range(H):
                if h >= 2:
                    act.wait_ge(s_hsum, h - 1)
                act.activation(tiles(EE[:, h % 2, :]), OA[:, h, :, :], ACT.Square).then_inc(s_hq, 1)
                if h:
                    rst(h - 1)
            rst(H - 1)
            for h in range(H):
                act.wait_ge(s_on, h + 1)
                act.activation(tiles(hh[:, h, :]), OA[:, h, :, :], ACT.Copy).then_inc(s_omh, 1)

        def dve_gdn_scan(dve):
            dve.wait_ge(s_us, H)
            dve.wait_ge(s_wt, H)
            for n in range(NT):
                if n == 0:
                    dve.tensor_copy(VN, US[:, :, 0, :]).then_inc(s_vn, 1)
                else:
                    link(dve, dve.tensor_tensor(SD, SS, along(EGL[:, n:4 * H:NT], P), ALU.mult), v_link, vl)
                    dve.wait_ge(s_p2, n)
                    dve.tensor_tensor(VN, US[:, :, n, :], tiles(bank[0][:, :]), ALU.subtract).then_inc(s_vn, 1)
                if n < NT - 1:
                    dve.wait_ge(s_ds, n + 1)
                    if n == 0:
                        dve.tensor_copy(SS, tiles(bank[1][:, :])).then_inc(s_ss, 1)
                    else:
                        dve.wait_ge(s_oo, n + 1)
                        dve.tensor_tensor(SS, SD, tiles(bank[1][:, :]), ALU.add).then_inc(s_ss, 1)
                    dve.wait_ge(s_ss, n + 1)
            for h in range(H):
                dve.wait_ge(s_hr, h + 1)
                link(dve, dve.scalar_tensor_tensor(out=OA[:, h, :, :], in0=OA[:, h, :, :], scalar=hon[:, 0:1],
                                                   in1=tiles(hf[:, h % 2, :]), op0=ALU.mult, op1=ALU.mult), v_link, vl)
                dve.tensor_tensor(OA[:, h, :, :], OA[:, h, :, :], tiles(GAT[:, h, :]), ALU.mult).then_inc(s_on, 1)
            for h in range(H):
                dve.wait_ge(s_omh, NT + h + 1)
                dve.tensor_tensor(tiles(hl[:, h, :]), OA[:, h, :, :], tiles(hh[:, h, :]), ALU.subtract).then_inc(s_om, 1)

        def act_gla_in(act):
            act.preload_act_table_set("silu_and_others")
            for i in range(GIN):
                o = O_GIN + i
                split_hi(act, C_GIN + i + 2)
                summed(act, C_GIN + i)
                src = bank[o % SLOTS][:, :]
                if i == ALR:
                    m = act.activation(ALRS, src, ACT.Copy, scale=1 / WS)
                elif i < GK:
                    m = act.activation(LQ[:, i - GQ, :], src, ACT.Copy, scale=P ** -0.5 / WS)
                elif i < GV:
                    m = act.activation(LK[:, i - GK, :], src, ACT.Copy, scale=1 / WS)
                elif i < GR:
                    m = act.activation(VFF[:, i - GV, :], src, ACT.Copy, scale=1 / WS)
                else:
                    m = act.activation(RS[:, i - GR, :], src, ACT.Silu, scale=1 / WS)
                m.then_inc(b_free[o % SLOTS], 1)

        def dve_gla_in(dve):
            for i in range(GIN):
                split_lo(dve, C_GIN + i + 2)

        HB = DH

        def pe_gla(pe):
            for i in range(GIN - SLOTS, GIN):
                was_read(pe, O_GIN + i)
            pe.wait_ge(s_aw, 16)
            for h in range(H):
                pe.matmul(bank[h][:, :], AW2[0:16, h * P:(h + 1) * P], ALRS[0:16, :], start=True, stop=True).then_inc(s_z, 1)
            for j in range(8):
                n, a = j // 2, j % 2
                if j >= 4:
                    pe.wait_ge(s_vv, j - 3)
                for k in range(4):
                    m = pe.transpose(bank[4 + j % 4][:, k * P:(k + 1) * P], VFF[:, 4 * a + k, n * P:(n + 1) * P], ident)
                m.then_inc(s_vp, 1)
            for h in range(H):
                kk = KKT[:, h % 2, :]
                qt = QT[:, h % 2, :].rearrange("p (n a r) -> p n a r", a=2, r=HB)
                pe.wait_ge(s_lm, h + 1)
                if h >= 2:
                    pe.wait_ge(s_la, h - 1)
                else:
                    pe.wait_ge(s_vv, 8)
                    pe.wait_ge(s_zl, H)
                for n in range(NT):
                    pe.matmul(bank[h % 2][:, n * P + HB:(n + 1) * P], kk[:, n * P:(n + 1) * P], qt[:, n, 1, :],
                              start=True, stop=True)
                    m = pe.matmul(bank[h % 2][:, n * P:n * P + HB], kk[:, S + n * P:S + (n + 1) * P], qt[:, n, 0, :],
                                  start=True, stop=True)
                m.then_inc(s_lap, 1)
                pe.wait_ge(s_lg, h + 1)
                if h >= 2:
                    pe.wait_ge(s_kdt, h - 1)
                for n in range(NT):
                    m = pe.transpose(bank[2 + h % 2][:, n * P:(n + 1) * P], LK[:, h, n * P:(n + 1) * P], ident)
                m.then_inc(s_kp, 1)
            for n in range(NT):
                if n == 0:
                    pe.wait_ge(s_kdt, H)
                    pe.wait_ge(s_la, H)
                if n < NT - 1:
                    if n >= 2:
                        pe.wait_ge(s_lss, n - 1)
                    for h in range(H):
                        m = pe.matmul(bank[4 + n % 2 * 2 + h // 2][:, h % 2 * 2 * P:(h % 2 + 1) * 2 * P], KDT[:, h, n, :],
                                      VTT[:, n, h * 2 * P:(h + 1) * 2 * P], start=True, stop=True)
                    m.then_inc(s_lds, 1)
                if n:
                    pe.wait_ge(s_lss, n)
                if n >= 2:
                    pe.wait_ge(s_loo, 2 * (n - 1))
                for i in range(DB):
                    h = i // 2
                    o = bank[n % 2 * 2 + i // 4][:, i % 4 * P:(i % 4 + 1) * P]
                    if n:
                        pe.matmul(o, LST[:, h, i % 2 * P:(i % 2 + 1) * P], LQ[:, h, n * P:(n + 1) * P], start=True, stop=False)
                    m = pe.matmul(o, VTT[:, n, i * P:(i + 1) * P], LA[:, h, n, :], start=(n == 0), stop=True)
                m.then_inc(s_lo, 1)
            for h in range(H):
                for a in range(2):
                    pe.wait_ge(s_hq, H + 2 * h + a + 1)
                    m = pe.matmul(bank[4 + h][:, :], ones, EX[:, a, :], start=(a == 0), stop=(a == 1))
                m.then_inc(s_hsum, 1)

        def act_gla(act):
            act.preload_act_table_set("natural_log_exp_and_others")

            def v_out(j):
                act.wait_ge(s_vp, j + 1)
                act.activation(VTT[:, j // 2, j % 2 * S:(j % 2 + 1) * S], bank[4 + j % 4][:, :], ACT.Copy).then_inc(s_vv, 1)

            for h in range(H):
                z, t = LZ[:, h % 2, :], LZ[:, 2 + h % 2, :]
                act.wait_ge(s_z, h + 1)
                if h >= 2:
                    act.wait_ge(s_lb, h - 1)
                link(act, act.activation(z, bank[h][:, :], ACT.Identity, bias=pr("lab", h)), a_link, al)
                link(act, act.activation(t, z, ACT.Abs), a_link, al)
                link(act, act.activation(t, t, ACT.Exp, scale=-1.0), a_link, al)
                act.activation(t, t, ACT.Ln, bias=onec[:, 0:1]).then_inc(s_zl, 1)
                v_out(2 * h)
                v_out(2 * h + 1)
            act.wait_ge(s_lb, H)
            act.activation(EBL.rearrange("p (h c) -> p h c", h=H), LB[:, :, HB - 1:S:HB], ACT.Exp, scale=1 / 16).then_inc(s_bl, 1)
            for h in range(H):
                act.wait_ge(s_lx, h + 1)
                act.activation(EX[:, 0, :], EX[:, 0, :], ACT.Exp, scale=1 / 16).then_inc(s_le, 1)
                act.activation(EX[:, 1, :], LB[:, h, :], ACT.Exp, scale=1 / 16).then_inc(s_le, 1)
                act.activation(EX[:, 2, :], LB[:, h, :], ACT.Exp, scale=-1 / 16).then_inc(s_le, 1)
                if h:
                    act.wait_ge(s_kp, h)
                    act.activation(KDT[:, h - 1, :, :], tiles(bank[2 + (h - 1) % 2][:, :]), ACT.Copy).then_inc(s_kdt, 1)
            act.wait_ge(s_kp, H)
            act.activation(KDT[:, H - 1, :, :], tiles(bank[2 + (H - 1) % 2][:, :]), ACT.Copy).then_inc(s_kdt, 1)
            for n in range(NT):
                act.wait_ge(s_lo, n + 1)
                for a in range(2):
                    act.activation(OO[:, 4 * a:4 * a + 4, n * P:(n + 1) * P], tiles(bank[n % 2 * 2 + a][:, :]),
                                   ACT.Copy).then_inc(s_loo, 1)
            act.wait_ge(s_loo, 2 * NT)

            def rst(h):
                act.wait_ge(s_hsum, H + h + 1)
                if h >= 2:
                    act.wait_ge(s_on, H + 2 * (h - 1))
                act.activation(hf[:, h % 2, :], bank[4 + h][:, :], ACT.Ln, bias=epsc[:, 3:4]).then_inc(s_hln, 1)
                act.wait_ge(s_hln, H + h + 1)
                act.activation(hf[:, h % 2, :], hf[:, h % 2, :], ACT.Exp, scale=-0.5).then_inc(s_hr, 1)

            for h in range(H):
                if h:
                    act.wait_ge(s_hsum, H + h)
                for a in range(2):
                    act.activation(EX[:, a, :], OO[:, 2 * h + a, :], ACT.Square).then_inc(s_hq, 1)
                if h:
                    rst(h - 1)
            rst(H - 1)
            for i in range(DB):
                act.wait_ge(s_on, H + i + 1)
                act.activation(hh[:, i, :], OO[:, i, :], ACT.Copy).then_inc(s_omh, 1)

        def pool_gla(pool):
            for h in range(H):
                qt = QT[:, h % 2, :].rearrange("p (n a r) -> p n a r", a=2, r=HB)
                mixed, kt = (KKT[:, h % 2, a:a + S].rearrange("p (n a r) -> p n a r", a=2, r=HB) for a in (0, S))
                q, k = (a[:, h, :].rearrange("p (n a r) -> p n a r", a=2, r=HB) for a in (LQ, LK))
                e = EBL[:, 8 * h:8 * h + 8].rearrange("p (n a) -> p n a", a=2)
                pool.wait_ge(s_bl, 1)
                pool.wait_ge(s_lk, h + 1)
                pool.tensor_copy(mixed[:, :, 0, :], k[:, :, 0, :])
                pool.tensor_copy(mixed[:, :, 1, :], kt[:, :, 1, :]).then_inc(s_lm, 1)
                pool.tensor_copy(q[:, :, 0, :], qt[:, :, 0, :])
                pool.tensor_tensor(q[:, :, 1, :], qt[:, :, 1, :], along(e[:, :, 0], HB), ALU.mult)
                pool.tensor_tensor(k[:, :, 0, :], k[:, :, 0, :], along(e[:, :, 1], HB), ALU.mult).then_inc(s_lg, 1)

        def dve_gla(dve):
            for h in range(H):
                z, t = LZ[:, h % 2, :], LZ[:, 2 + h % 2, :]
                dve.wait_ge(s_zl, h + 1)
                dve.scalar_tensor_tensor(out=z, in0=z, scalar=0.0, in1=t, op0=ALU.min, op1=ALU.subtract).then_inc(s_zc, 1)
                dve.wait_ge(s_zc, h + 1)
                dve.tensor_tensor_scan(LB[:, h, :], mk("seg"), z, 0.0, ALU.mult, ALU.add).then_inc(s_lb, 1)
            dve.wait_ge(s_bl, 1)
            dve.wait_ge(s_lb, H)
            link(dve, dve.tensor_tensor(DEC, EBL[:, 0:32:2], EBL[:, 1:32:2], ALU.mult), v_link, vl)

            def mask(h):
                dve.wait_ge(s_lap, h + 1)
                dve.tensor_tensor(LA[:, h, :, :], tiles(bank[h % 2][:, :]), spread(mk("incl"), NT), ALU.mult).then_inc(s_la, 1)

            for h in range(H):
                b = LB[:, h, :].rearrange("p (c r) -> p c r", r=HB)
                if h:
                    dve.wait_ge(s_lk, h)
                dve.tensor_tensor(EX[:, 0, :].rearrange("p (c r) -> p c r", r=HB), along(LB[:, h, HB - 1:S:HB], HB), b,
                                  ALU.subtract).then_inc(s_lx, 1)
                dve.wait_ge(s_le, 3 * (h + 1))
                if h >= 2:
                    dve.wait_ge(s_lg, h - 1)
                    dve.wait_ge(s_lap, h - 1)
                dve.tensor_tensor(QT[:, h % 2, :], LQ[:, h, :], EX[:, 1, :], ALU.mult)
                dve.tensor_tensor(KKT[:, h % 2, S:2 * S], LK[:, h, :], EX[:, 2, :], ALU.mult)
                dve.tensor_tensor(LK[:, h, :], LK[:, h, :], EX[:, 0, :], ALU.mult).then_inc(s_lk, 1)
                if h:
                    mask(h - 1)
            mask(H - 1)
            for n in range(NT - 1):
                if n:
                    dve.wait_ge(s_lo, n + 1)
                    link(dve, dve.tensor_tensor(LST, LST, along(DEC[:, n:4 * H:NT], 2 * P), ALU.mult), v_link, vl)
                dve.wait_ge(s_lds, n + 1)
                for a in range(2):
                    src = bank[4 + n % 2 * 2 + a][:, :].rearrange("p (h d) -> p h d", h=2)
                    dst = LST[:, 2 * a:2 * a + 2, :]
                    if n == 0:
                        m = dve.tensor_copy(dst, src)
                    else:
                        m = dve.tensor_tensor(dst, dst, src, ALU.add)
                m.then_inc(s_lss, 1)
                dve.wait_ge(s_lss, n + 1)
            for h in range(H):
                dve.wait_ge(s_hr, H + h + 1)
                for a in range(2):
                    i = 2 * h + a
                    link(dve, dve.scalar_tensor_tensor(out=OO[:, i, :], in0=OO[:, i, :], scalar=hon[:, 1 + a:2 + a],
                                                       in1=hf[:, h % 2, :], op0=ALU.mult, op1=ALU.mult), v_link, vl)
                    dve.tensor_tensor(OO[:, i, :], OO[:, i, :], RS[:, i, :], ALU.mult).then_inc(s_on, 1)
            for i in range(DB):
                dve.wait_ge(s_omh, DB + i + 1)
                dve.tensor_tensor(hl[:, i, :], OO[:, i, :], hh[:, i, :], ALU.subtract).then_inc(s_om, 1)

        block = ctx.enter_context(nc.Block())

        @block.sync
        def _(sp):
            sp.dma_start(x[:, :, :], in_x).then_inc(s_x, 16)
            sp.dma_start(par[:, :], in_par).then_inc(s_par, 16)
            sp.dma_start(msk[:, :], in_msk).then_inc(s_par, 16)

            def flow(c, w, count, peel=0):
                for i in range(peel):
                    load(sp, c + i, in_w[w + i])
                with sp.Fori(0, (count - peel) // SLOTS) as it:
                    for j in range(SLOTS):
                        src = in_w[bass.ds(it * SLOTS + (w + peel + j), 1)].rearrange("a p n -> (a p) n")
                        load(sp, c + peel + j, src, it, SLOTS)

            def flow_out(L):
                with sp.Fori(0, 2) as it:
                    for j in range(12):
                        a = j % 3
                        src = in_fo[bass.ds(it * 4 + (DB * L + j // 3), 1), :, a * D:a * D + OUT_SUB[a] * P]
                        load(sp, C_FOUT[L] + j, src.rearrange("a p n -> (a p) n"), it, 12)

            for i in range(SLOTS):
                load(sp, i, in_w[i])
            for t in range(2):
                for g in range(2):
                    sp.dma_start(W1[g * DH:(g + 1) * DH, t, :, :], in_w1[t]).then_inc(s_w1, 16)
                sp.dma_start(W2[:, t, :], in_w2[t]).then_inc(s_w1, 16)
            for i in range(SLOTS, 7):
                load(sp, i, in_w[i])
            flow(C_HIN + 7, W_HIN + 7, HIN - 7)
            flow(C_HOUT, W_HOUT, OUTB)
            flow(C_F0, W_F0, FIN)
            flow_out(0)
            flow(C_GIN, W_GIN, GIN, 1)
            sp.wait_ge(s_g, FB)
            sp.dma_start(AW2[0:16, :], in_aw2).then_inc(s_aw, 16)
            flow(C_GOUT, W_GOUT, OUTB)
            flow(C_F1, W_F1, FIN)
            flow_out(1)
            for d in range(DB):
                sp.wait_ge(s_xr, 3 * DB + d + 1)
                sp.dma_start(out_x[:, d, :], x[:, d, :]).then_inc(s_out, 16)
            sp.wait_ge(s_out, 16 * DB)

        @block.tensor
        def _(pe):
            pe.wait_ge(s_par, 32)
            pe_sum(pe, 0)
            pe.wait_ge(s_h, DB)
            project(pe, C_HIN, O_HIN, HIN, 7)
            pe_compress(pe)
            pe_cmp(pe)
            pe_attention(pe)
            pe_gdn_prep(pe)
            pe_inverse(pe)
            pe_gdn_scan(pe)
            pe.wait_ge(s_om, DB)
            project(pe, C_HOUT, O_HOUT, OUTB)
            pe_sum(pe, 1)
            pe_sum(pe, 2)
            pe_ffn(pe, 0)
            pe_sum(pe, 3)
            pe_sum(pe, 4)
            pe.wait_ge(s_h, 3 * DB)
            project(pe, C_GIN, O_GIN, GIN, 1)
            pe_gla(pe)
            pe.wait_ge(s_om, 2 * DB)
            project(pe, C_GOUT, O_GOUT, OUTB)
            pe_sum(pe, 5)
            pe_sum(pe, 6)
            pe_ffn(pe, 1)
            pe_sum(pe, 7)

        @block.scalar
        def _(act):
            act.wait_ge(s_cst, CONSTS)
            act_pre(act, 0)
            act_hybrid_in(act)
            act_compress(act)
            act_attention(act)
            act_gdn_prep(act)
            act_inverse(act)
            act_gdn_scan(act)
            act_outproj(act, C_HOUT, O_HOUT)
            act_rstd(act, 1)
            act_pre(act, 2)
            act_ffn(act, 0)
            act_rstd(act, 3)
            act_pre(act, 4)
            act_gla_in(act)
            act_gla(act)
            act_outproj(act, C_GOUT, O_GOUT)
            act_rstd(act, 5)
            act_pre(act, 6)
            act_ffn(act, 1)
            act_rstd(act, 7)

        @block.gpsimd
        def _(pool):
            pool_gdn(pool)
            pool_gla(pool)

        @block.vector
        def _(dve):
            dve.memset(epsc[:, 0:1], D * EPS).then_inc(s_cst, 1)
            dve.memset(epsc[:, 1:2], EPS).then_inc(s_cst, 1)
            dve.memset(epsc[:, 2:3], P * EPS).then_inc(s_cst, 1)
            dve.memset(epsc[:, 3:4], 2 * P * EPS).then_inc(s_cst, 1)
            dve.memset(onec[:, :], 1.0).then_inc(s_cst, 1)
            dve.wait_ge(s_par, 32)
            dve.tensor_scalar(gain[:, :], pr("gain", 0, 8 * DB), D ** 0.5, None, ALU.mult).then_inc(s_cst, 1)
            dve.tensor_scalar(fcw[:, :], pr("fcw", 0, 2 * FIN * FC), 1 / WS, None, ALU.mult).then_inc(s_cst, 1)
            dve.tensor_scalar(gcw[:, :], pr("gcw", 0, 12 * GC), 1 / WS, None, ALU.mult).then_inc(s_cst, 1)
            dve.tensor_scalar(hon[:, 0:1], pr("gon"), P ** 0.5, None, ALU.mult).then_inc(s_cst, 1)
            dve.tensor_scalar(hon[:, 1:3], pr("lon", 0, 2), (2 * P) ** 0.5, None, ALU.mult).then_inc(s_cst, 1)
            dve.memset(cu[:, 0, 0:1], 0.0).then_inc(s_prod, 1)
            dve.memset(cu[:, 0, 1:2], 0.0).then_inc(s_prod, 1)
            dve.wait_ge(s_cst, CONSTS)
            dve_pre(dve, 0)
            dve_hybrid_in(dve)
            dve_compress(dve)
            dve_decays(dve)
            dve_cmp(dve)
            dve_attention(dve)
            dve_gdn_prep(dve)
            dve_inverse(dve)
            dve_gdn_scan(dve)
            dve_outproj(dve, C_HOUT)
            dve_post(dve, 1)
            dve_pre(dve, 2)
            dve_ffn(dve, 0)
            dve_post(dve, 3)
            dve_pre(dve, 4)
            dve_gla_in(dve)
            dve_gla(dve)
            dve_outproj(dve, C_GOUT)
            dve_post(dve, 5)
            dve_pre(dve, 6)
            dve_ffn(dve, 1)
            dve_post(dve, 7)


def host_layout(i):
    import numpy as np

    i = {k: np.asarray(v) for k, v in i.items()}

    def cols(w):
        k, n = w.shape
        return w.reshape(k // P, P, n // P, P).transpose(2, 1, 0, 3).reshape(n // P, P, k)

    def rows(a):
        return a.reshape(-1, P).T

    w = i["hyb_w_in"][0]
    at = np.cumsum([0, 3 * H * P, H, H, H * P, NH * DH, 6 * 2 * DH, 3 * NH])
    qkv, beta, dec, gate, qb, kv, gb = (w[:, at[j]:at[j + 1]] for j in range(7))
    small = np.zeros((D, P), w.dtype)
    small[:, 0:H], small[:, 32:32 + H], small[:, 64:64 + 3 * NH] = dec, beta, gb
    qb = qb.reshape(D, 2, 4, DH).transpose(0, 2, 1, 3).reshape(D, NH * DH)
    kv = kv.reshape(D, 6, 2 * DH)[:, [0, 1, 2, 4, 3, 5]].reshape(D, 12 * DH)
    hin = np.concatenate([small, qkv, qb, kv, gate], 1)
    g = i["gla_w_in"][0]
    alr = np.zeros((D, P), g.dtype)
    alr[:, 0:16] = g[:, 3 * D:]
    gin = np.concatenate([alr, g[:, 0:3 * D]], 1)

    def pairs(a):
        return a.reshape(a.shape[:-1] + (2, FB, P)).swapaxes(-3, -2).reshape(a.shape)

    fin = pairs(i["ffn_w_in"])
    in_w = np.concatenate([cols(hin), cols(i["hyb_w_out"][0]), cols(fin[0]), cols(gin), cols(i["gla_w_out"][0]), cols(fin[1])])
    in_fo = np.concatenate([cols(i["ffn_w_out"][0]), cols(i["ffn_w_out"][1])])
    par = np.zeros((P, NPAR), np.float32)

    def put(name, a):
        a = a.reshape(a.shape[0], -1)
        par[0:a.shape[0], PARAM[name][0]:PARAM[name][0] + a.shape[1]] = a

    put("gain", rows(i["norm_gains"]))
    put("fcw", rows(pairs(i["ffn_conv_w"]).transpose(1, 0, 2)))
    put("fcb", rows(pairs(i["ffn_conv_b"])))
    put("gcw", i["gdn_conv_w"][0].reshape(GC, 12, P).transpose(2, 1, 0))
    put("alog", i["gdn_A_log"][0][:, None])
    put("dtb", i["gdn_dt_bias"][0][:, None])
    put("gon", rows(i["gdn_o_norm"]))
    put("b1", rows(i["nsa_cmp_b1"]))
    put("pe", np.concatenate([i["nsa_cmp_pe"][0].transpose(2, 0, 1)] * 2))
    put("lon", rows(i["gla_o_norm"]))
    put("lab", rows(i["gla_a_b"]))
    w2 = i["nsa_cmp_w2"][0]
    return {
        "in_x": i["x"][0].T.reshape(DB, P, S).transpose(1, 0, 2),
        "in_par": par, "in_msk": masks(), "in_w": in_w, "in_fo": in_fo,
        "in_w1": i["nsa_cmp_w1"][0].reshape(2, CL, DH, P).transpose(0, 2, 1, 3),
        "in_w2": np.concatenate([w2, w2], 2),
        "in_aw2": i["gla_a_w2"][0],
    }


def masks():
    import numpy as np

    m = np.zeros((P, NMASK), np.float32)

    def put(name, a):
        m[0:a.shape[0], MASKS[name][0]:MASKS[name][1]] = a

    r = np.arange(P)
    put("ident", np.eye(P))
    put("ones", np.ones((P, P)))
    put("strict", r[:, None] > r[None, :])
    put("incl", r[:, None] <= r[None, :])
    put("lev", np.concatenate([(r[:, None] >> l + 1 == r[None, :] >> l + 1) & (r[:, None] >> l & 1 == 1)
                               & (r[None, :] >> l & 1 == 0) for l in range(7)], 1))
    neg = np.zeros((P, S))
    neg[:, S - P:] = np.where(r[None, :] > r[:, None], NEG, 0.0)
    put("neg", neg)
    put("seg", np.tile(np.arange(S) % DH != 0, (P, 1)))
    t = r[:, None, None] + P * np.arange(NT)[None, :, None]
    c = np.arange(NCP)[None, None, :]
    ok = ((c * CS + CL - 1 <= t) & (c < NC)).reshape(P, -1)
    put("cadd", np.where(ok, 0.0, NEG))
    put("c01", ok)
    put("sel", np.kron(np.eye(H), np.ones((1, P))))
    return m


def kernel(**inputs):
    import numpy as np
    import concourse.bacc as bacc
    from concourse.bass_utils import run_bass_kernel_spmd

    nc = bacc.Bacc("TRN2", target_bir_lowering=False, num_devices=1)
    arrays = {k: np.ascontiguousarray(a) for k, a in host_layout(inputs).items()}
    aps = {k: nc.dram_tensor(k, a.shape, mybir.dt.from_np(a.dtype), kind="ExternalInput").ap() for k, a in arrays.items()}
    out = nc.dram_tensor("out_x", (P, DB, S), F32, kind="ExternalOutput").ap()
    build(nc, out, **aps)
    r = run_bass_kernel_spmd(nc, [arrays], core_ids=[0])
    o = np.asarray(r.results[0]["out_x"])
    return o.transpose(2, 1, 0).reshape(1, S, D)
```

```python
from contextlib import ExitStack

import concourse.bass as bass
from concourse import mybir

F32 = mybir.dt.float32
F16 = mybir.dt.float16
ALU = mybir.AluOpType
ACT = mybir.ActivationFunctionType
AX_X = mybir.AxisListType.X

P = 128
D = 1024
S = 512
DB = D // P
NT = S // P
EPS = 1e-6
NEG = -1e30
WS = 16.0
SLOTS = 4

H = 4
GC = 4
NH = 8
DH = 64
NC = 31
NCP = 32
CL, CS = 32, 16

DFF = 2816
FB = DFF // P
FC = 3
OUT_SUB = (8, 8, 6)

HIN, OUTB, FIN, GIN = 27, DB, 2 * FB, 25
C_HIN, O_HIN = 0, 0
C_HOUT, O_HOUT = C_HIN + HIN, O_HIN + HIN
C_F0, O_F0 = C_HOUT + OUTB, O_HOUT + OUTB
C_FO0, O_FO0 = C_F0 + FIN, O_F0 + FIN
C_GIN, O_GIN = C_FO0 + 3 * OUTB, O_FO0 + OUTB
C_GOUT, O_GOUT = C_GIN + GIN, O_GIN + GIN
C_F1, O_F1 = C_GOUT + OUTB, O_GOUT + OUTB
C_FO1, O_FO1 = C_F1 + FIN, O_F1 + FIN
C_END = C_FO1 + 3 * OUTB
C_FIN, O_FIN = (C_F0, C_F1), (O_F0, O_F1)
C_FOUT, O_FOUT = (C_FO0, C_FO1), (O_FO0, O_FO1)

W_HIN, W_HOUT, W_F0 = 0, HIN, HIN + OUTB
W_GIN = W_F0 + FIN
W_GOUT = W_GIN + GIN
W_F1 = W_GOUT + OUTB
W_FIN = (W_F0, W_F1)

ROWS, QKV, QB, KC, VC, KSW, VSW, GA = 0, 1, 13, 17, 18, 19, 21, 23
ALR, GQ, GK, GV, GR = 0, 1, 5, 9, 17

PARAM = {}
_at = 0
for _n, _w in (("gain", 8 * DB), ("fcw", 2 * FIN * FC), ("fcb", 2 * FIN), ("gcw", 12 * GC), ("alog", 1), ("dtb", 1),
               ("gon", 1), ("b1", 2), ("pe", 2 * CL), ("lon", 2), ("lab", 4)):
    PARAM[_n] = (_at, _at + _w)
    _at += _w
NPAR = _at

MASKS = {}
_at = 0
for _n, _w in (("ident", P), ("strict", P), ("incl", P), ("lev", 7 * P), ("neg", S), ("seg", S),
               ("cadd", NT * NCP), ("c01", NT * NCP), ("sel", H * P)):
    MASKS[_n] = (_at, _at + _w)
    _at += _w
NMASK = _at


def build(nc, out_x, in_x, in_par, in_msk, in_w, in_fo, in_w1, in_w2, in_aw2):
    with ExitStack() as ctx:
        def sb(name, shape, dt=F32):
            return ctx.enter_context(nc.sbuf_tensor(name, shape, dt))

        def sem(name):
            return ctx.enter_context(nc.semaphore(name))

        bank = [ctx.enter_context(nc.psum_tensor(f"bank{i}", [P, S], F32)) for i in range(8)]

        x = sb("x", [P, DB, S])
        hh = sb("hh", [P, DB, S], F16)
        hl = sb("hl", [P, DB, S], F16)
        raw = sb("raw", [P, SLOTS, D])
        whi = sb("whi", [P, SLOTS, D], F16)
        wlo = sb("wlo", [P, SLOTS, D], F16)
        par = sb("par", [P, NPAR])
        msk = sb("msk", [P, NMASK])
        gain = sb("gain", [P, 8 * DB])
        fcw = sb("fcw", [P, 2 * FIN * FC])
        gcw = sb("gcw", [P, 12 * GC])
        hon = sb("hon", [P, 3])
        hf = sb("hf", [P, 2, S])
        rln = sb("rln", [P, S])
        rstd = sb("rstd", [P, S])
        epsc = sb("epsc", [P, 4])
        onec = sb("onec", [P, 1])
        CONSTS = 7
        LATER = 5
        ARENA = 29472
        arena = sb("arena", [P, ARENA])

        def pr(name, i=0, n=1):
            a = PARAM[name][0] + i
            return par[:, a:a + n]

        def mk(name):
            return msk[:, MASKS[name][0]:MASKS[name][1]]

        ident = mk("ident")
        ones = sb("ones", [P, P])[:, :]
        zero = sb("zero", [1, S], F16)

        def view(at, *dims):
            n = 1
            for d in dims:
                n *= d
            assert at + n <= ARENA, (at, n)
            v = arena[:, at:at + n]
            if len(dims) == 1:
                return v
            if len(dims) == 2:
                return v.rearrange("p (a b) -> p a b", b=dims[1])
            return v.rearrange("p (a b c) -> p a b c", b=dims[1], c=dims[2])

        y = view(0, DB, S)
        sq = view(4096, DB, S)
        gh = view(8192, FB * S // 2).bitcast(F16).rearrange("p (f s) -> p f s", s=S)
        gl = view(8192 + FB * S // 2, FB * S // 2).bitcast(F16).rearrange("p (f s) -> p f s", s=S)
        cu = view(19456, 4, S)
        gf = view(21504, S)

        QKVS = view(0, 12, S)
        AK = view(6144, H, NT, P)
        AQ = view(8192, H, NT, P)
        TT = view(10240, H, NT, P)
        UU = view(12288, H, NT, P)
        XX = view(14336, H, NT, P)
        BM = view(16384, H, NT, P)
        KD = view(18432, H, NT, P)
        EE = view(20480, 3, S)
        GAT = view(22016, H, S)
        QBP = view(24064, 4 * S).bitcast(F16).rearrange("p (l h s) -> p l h s", l=2, s=S)
        KSP = view(26112, 2 * S).bitcast(F16).rearrange("p (l b s) -> p l b s", l=2, s=S)
        VTP = view(27136, 2 * S).bitcast(F16).rearrange("p (l b n c) -> p l b n c", l=2, b=2, c=P)
        VBD = view(28160, 2, 4 * DH)
        KCM = view(28672, NCP).bitcast(F16).rearrange("p (l c) -> p l c", l=2)
        SIG = view(28704, NT, 64)
        G = view(28960, S)[0:H]
        ROWT = view(28960, S)
        GZ = view(18944, 3, S)[0:H]
        BLKP = view(6144, 2 * CL * NC).bitcast(F16).rearrange("p (l t m) -> p l t m", l=2, t=2)
        BLK = view(18944, 2, CL, NC)
        HS = view(8192, 2, 2, NCP)
        KCF = view(8448, 2, S)
        VF = view(20992, 2, S)
        W1 = view(10496, 2 * CL // 8, 8 * P)
        W1P = view(9472, 2 * CL // 8 * 8 * P).bitcast(F16).rearrange("p (k l m) -> p k l m", l=2, m=8 * P)
        W2 = view(18688, 2, P)
        SM = view(10496, 2, S)
        PP = view(11520, 3, S)
        PTP = view(13056, 3 * S).bitcast(F16).rearrange("p (l u s) -> p l u s", l=2, s=S)
        ACC = view(14592, NT, S)
        TMP = view(16640, S)
        CSC = view(17152, NT, NH * NCP)
        CPT = view(13056, NT, 2 * P)
        US, WT, OA = AK, XX, TT
        VN, SS, SD = BM[:, 0], BM[:, 1], BM[:, 2]

        small = sb("small", [P, 512])
        GT, BT, GLB, EGT, BEG, EKD, EGL = (small[:, 16 * i:16 * i + 16] for i in range(7))
        NMX = small[:, 112:114]
        LS = small[:, 128:144]
        RC = small[:, 144:152]
        CMX, CLS, CRC = small[:, 160:192], small[:, 192:224], small[:, 224:256]
        NA = small[:, 256:257]
        EBL = small[:, 288:320]
        DEC = small[:, 320:336]

        LQ = view(0, H, S)
        LK = view(2048, H, S)
        VTT = view(4096, NT, D)
        RS = view(8192, DB, S)
        LB = view(12288, H, S)
        SQO = view(12288, DB, S)
        KDT = view(14336, H, NT, P)
        LA = view(16384, H, NT, P)
        KKT = view(18432, 2, 1024)
        EX = view(20736, 3, S)
        QT = view(22272, 2, S)
        OO = view(23296, DB, S)
        VFF = OO
        LST = view(27392, H, 2 * P)
        ALRS = view(28416, S)
        LZ = view(18432, 4, S)
        AW2 = view(28928, S)

        s_par = sem("params_loaded")
        s_x = [sem(f"x_loaded{i}") for i in range(2)]
        s_msk = sem("masks_loaded")
        s_w1 = sem("cmp_weights_loaded")
        s_aw = sem("gla_weights_loaded")
        s_cst = sem("constants_ready")
        w_dma = [sem(f"chunk_loaded{i}") for i in range(SLOTS)]
        w_hi = sem("chunk_high_ready")
        w_lo = sem("chunk_low_ready")
        w_used = sem("chunk_used")
        b_free = [sem(f"bank_read{i}") for i in range(SLOTS)]
        s_sq = sem("square_ready")
        s_sum = sem("sum_of_squares_ready")
        s_ln = sem("log_ready")
        s_rstd = sem("rstd_ready")
        s_yn = sem("y_normed")
        s_xr = [sem("x_updated_odd"), sem("x_updated_even")]
        s_hf = sem("h32_ready")
        s_hh = sem("h_high_ready")
        s_h = sem("h_ready")
        s_cv = sem("conv_started")
        s_c1 = sem("conv_stepped")
        s_silu = sem("gate_silu_ready")
        s_prod = sem("products_ready")
        s_gh = sem("g_high_ready")
        s_g = sem("g_ready")
        s_out = sem("output_stored")
        s_om = sem("mixer_output_ready")
        s_omh = sem("mixer_output_high_ready")
        v_link = sem("vector_step")
        a_link = sem("scalar_step")
        g_link = sem("pool_step")
        (s_qs, s_blk, s_hid, s_hs, s_kv, s_kcm, s_vt, s_vtk, s_rt, s_se, s_sg, s_cs, s_cm, s_ce, s_cp, s_ct, s_cpt,
         s_co, s_ca, s_s, s_m, s_e, s_t, s_pc, s_pv, s_o, s_cb, s_acc, s_at, s_qh, s_vh, s_kch, s_pl, s_wh, s_wl, s_bh16, s_bl16,
         s_clr) = (sem(n) for n in (
             "qkv_ready", "cmp_blocks_ready", "cmp_hidden_summed", "cmp_hidden_ready", "cmp_kv_summed", "cmp_kv_ready",
             "v_transposed", "v_tokens_ready", "rows_transposed", "gate_exp_ready", "gates_ready",
             "cmp_scores", "cmp_scores_masked", "cmp_exp_ready", "cmp_probs_ready", "cmp_probs_transposed",
             "cmp_probs_t_ready", "cmp_out_summed", "cmp_out_ready", "scores_summed", "scores_masked", "probs_ready",
             "probs_transposed", "probs_t_ready", "pv_summed", "attention_summed", "attention_bank_read",
             "attention_ready", "attention_transposed", "nsa_operand_high_ready", "v_tokens_high_ready", "cmp_k_high_ready",
             "probs_t_low_ready", "cmp_w1_high_ready", "cmp_w1_low_ready", "cmp_blocks_high_ready",
             "cmp_blocks_low_ready", "cleared"))
        (s_ga, s_g1, s_gg, s_gtr, s_gt, s_ge, s_gk, s_nq, s_ns, s_nl, s_nr, s_nn, s_gb, s_dd, s_d, s_ex, s_eg, s_e1,
         s_e2, s_qg, s_kk, s_qk, s_kt, s_vr, s_ak, s_aq, s_kd, s_bv) = (sem(n) for n in (
             "decay_exp_ready", "softplus_ready", "decays_cumulated", "decay_columns_summed", "decay_columns_ready",
             "decay_exps_ready", "decay_products_ready", "qk_square_ready", "qk_sum_ready", "qk_log_ready",
             "qk_rstd_ready", "qk_normed", "decay_row_spread", "decay_differences_ready", "decay_row_read",
             "decay_pair_exp_ready", "decay_row_exp_ready", "kk_decay_ready", "qk_decay_ready", "q_decayed",
             "kk_summed", "qk_summed", "k_transposed", "v_heads_transposed", "kk_ready", "qk_t_ready",
             "k_tokens_ready", "v_beta_ready"))
        (s_b, s_tt, s_ut, s_uu, s_xp, s_xx, s_zu, s_zt, s_u, s_w, s_us, s_wt, s_p2, s_vn, s_oo, s_ds, s_ss, s_oa,
         s_hq, s_hsum, s_hln, s_hr, s_on) = (sem(n) for n in (
             "level_blocks_ready", "inverse_ready", "inverse_transposed", "inverse_t_ready", "x_summed", "x_ready",
             "u_update_summed", "t_update_summed", "u_summed", "w_summed", "u_ready", "w_ready", "old_value_summed",
             "new_value_ready", "head_out_summed", "state_update_summed", "state_ready", "head_out_ready",
             "head_square_ready", "head_sum_ready", "head_log_ready", "head_rstd_ready", "head_out_gated"))
        (s_z, s_zl, s_zc, s_lb, s_bl, s_lx, s_le, s_lk, s_lg, s_lap, s_la, s_kp, s_kdt, s_vp, s_lo, s_lds,
         s_lss, s_loo, s_lm, s_og) = (sem(n) for n in (
             "decay_logit_summed", "decay_log_ready", "decay_log_joined", "log_decays_cumulated", "chunk_decays_ready",
             "decay_to_end_ready", "gla_exps_ready", "gla_k_ready", "gla_decayed", "gla_kq_summed", "gla_kq_ready",
             "gla_k_transposed", "gla_k_tokens_ready", "gla_v_transposed", "gla_out_summed",
             "gla_state_summed", "gla_state_ready", "gla_out_ready", "gla_k_mixed_ready", "gla_out_gated"))
        s_vv = [sem(f"gla_v_tokens_ready{i}") for i in range(2)]

        vl, al, gl_ = [0], [0], [0]
        PASSES = ((0, 0), (0, 1), (1, 0))

        def link(eng, ins, signal, at):
            ins.then_inc(signal, 1)
            at[0] += 1
            eng.wait_ge(signal, at[0])

        def tiles(a):
            return a.rearrange("p (n c) -> p n c", c=P)

        def spread(a, n):
            return a.unsqueeze(1).to_broadcast([a.shape[0], n, a.shape[1]])

        def along(a, n):
            return a.unsqueeze(2).to_broadcast([a.shape[0], a.shape[1], n])

        def kb_of(c):
            for a in C_FOUT:
                if a <= c < a + 3 * OUTB:
                    return OUT_SUB[(c - a) % 3]
            return DB

        def load(sp, c, src, it=0, n=0):
            if c >= SLOTS:
                sp.wait_ge(w_lo, it * n + (c - SLOTS + 1))
            sp.dma_start(raw[:, c % SLOTS, 0:kb_of(c) * P], src).then_inc(w_dma[c % SLOTS], 16)

        def split_hi(act, c, it=0, n=0):
            if c >= C_END:
                return
            act.wait_ge(w_dma[c % SLOTS], it * (n // SLOTS * 16) + 16 * (c // SLOTS + 1))
            if c >= SLOTS:
                act.wait_ge(w_used, it * n + (c - SLOTS + 1))
            k = kb_of(c) * P
            act.activation(whi[:, c % SLOTS, 0:k], raw[:, c % SLOTS, 0:k], ACT.Copy, scale=WS).then_inc(w_hi, 1)

        def split_lo(dve, c, it=0, n=0):
            if c >= C_END:
                return
            dve.wait_ge(w_hi, it * n + (c + 1))
            k = kb_of(c) * P
            dve.scalar_tensor_tensor(out=wlo[:, c % SLOTS, 0:k], in0=raw[:, c % SLOTS, 0:k], scalar=WS,
                                     in1=whi[:, c % SLOTS, 0:k], op0=ALU.mult, op1=ALU.subtract).then_inc(w_lo, 1)

        def chunk(pe, c, o, mh, ml, k0=0, first=True, last=True, it=0, n=0):
            pe.wait_ge(w_lo, it * n + (c + 1))
            if first and o >= SLOTS:
                no = n if kb_of(c) == DB and n != 12 else 4
                pe.wait_ge(b_free[o % SLOTS], it * (no // SLOTS) + o // SLOTS)
            s, nk = c % SLOTS, kb_of(c)
            for k in range(nk):
                wh, wl = whi[:, s, k * P:(k + 1) * P], wlo[:, s, k * P:(k + 1) * P]
                pe.matmul(bank[o % SLOTS][:, :], wh, mh[:, k0 + k, :], start=(first and k == 0), stop=False)
                pe.matmul(bank[o % SLOTS][:, :], wh, ml[:, k0 + k, :], start=False, stop=False)
                m = pe.matmul(bank[o % SLOTS][:, :], wl, mh[:, k0 + k, :], start=False, stop=(last and k == nk - 1))
            m.then_inc(w_used, 1)

        def first_two(pe, c, o, ready, value, order=range(DB)):
            pe.wait_ge(w_lo, c + 2)
            for j in range(2):
                if o + j >= SLOTS:
                    pe.wait_ge(b_free[(o + j) % SLOTS], (o + j) // SLOTS)
            for i, k in enumerate(order):
                pe.wait_ge(ready, value + i + 1)
                for j in range(2):
                    out, s = bank[(o + j) % SLOTS][:, :], (c + j) % SLOTS
                    wh, wl = whi[:, s, k * P:(k + 1) * P], wlo[:, s, k * P:(k + 1) * P]
                    pe.matmul(out, wh, hh[:, k, :], start=(i == 0), stop=False)
                    pe.matmul(out, wh, hl[:, k, :], start=False, stop=False)
                    m = pe.matmul(out, wl, hh[:, k, :], start=False, stop=(i == DB - 1))
                    if i == DB - 1:
                        m.then_inc(w_used, 1)

        def project(pe, c, o, count, e):
            first_two(pe, c, o, s_h, DB * (e // 2))
            peel = 2 + (count - 2) % SLOTS
            for i in range(2, peel):
                chunk(pe, c + i, o + i, hh, hl)
            with pe.Fori(0, (count - peel) // SLOTS) as it:
                for j in range(SLOTS):
                    chunk(pe, c + peel + j, o + peel + j, hh, hl, it=it, n=SLOTS)

        def pe_outproj(pe, c, o, e, value, order=range(DB)):
            first_two(pe, c, o, s_om, value, order)
            for d in range(2, DB):
                chunk(pe, c + d, o + d, hh, hl)
                pe_sum_block(pe, e, d - 2, d == 2, False)
            pe_sum_block(pe, e, DB - 2, False, False)
            pe_sum_block(pe, e, DB - 1, False, True)

        def summed(eng, c, it=0, n=0):
            eng.wait_ge(w_used, it * n + (c + 1))

        def was_read(eng, o, it=0, n=0):
            eng.wait_ge(b_free[o % SLOTS], it * (n // SLOTS) + (o // SLOTS + 1))

        def pe_sum_block(pe, e, d, first, last):
            if first and e:
                pe.wait_ge(s_ln, e)
            pe.wait_ge(s_sq, DB * e + d + 1)
            m = pe.matmul(bank[4][:, :], ones, sq[:, d, :], start=first, stop=last)
            if last:
                m.then_inc(s_sum, 1)

        def pe_sum(pe, e):
            for d in range(DB):
                pe_sum_block(pe, e, d, d == 0, d == DB - 1)

        def act_rstd(act, e):
            act.preload_act_table_set("natural_log_exp_and_others")
            act.wait_ge(s_sum, e + 1)
            act.activation(rln[:, :], bank[4][:, :], ACT.Ln, bias=epsc[:, 0:1]).then_inc(s_ln, 1)
            act.wait_ge(s_ln, e + 1)
            act.activation(rstd[:, :], rln[:, :], ACT.Exp, scale=-0.5).then_inc(s_rstd, 1)

        def act_pre(act, e):
            base = DB * (e // 2)
            for d in range(DB):
                if e:
                    x_updated(act, e - 1, d)
                else:
                    act.wait_ge(s_x[2 * d // DB], 16)
                act.activation(sq[:, d, :], x[:, d, :], ACT.Square).then_inc(s_sq, 1)
            act_rstd(act, e)
            for d in range(DB):
                act.wait_ge(s_hf, base + d + 1)
                act.activation(hh[:, d, :], hf[:, d % 2, :], ACT.Copy).then_inc(s_hh, 1)

        def dve_pre(dve, e):
            base = DB * (e // 2)

            def low(d):
                dve.wait_ge(s_hh, base + d + 1)
                dve.tensor_tensor(hl[:, d, :], hf[:, d % 2, :], hh[:, d, :], ALU.subtract).then_inc(s_h, 1)

            dve.wait_ge(s_rstd, e + 1)
            for d in range(DB):
                if d >= 2:
                    dve.wait_ge(s_h, base + d - 1)
                dve.scalar_tensor_tensor(out=hf[:, d % 2, :], in0=x[:, d, :], scalar=gain[:, e * DB + d:e * DB + d + 1],
                                         in1=rstd[:, :], op0=ALU.mult, op1=ALU.mult).then_inc(s_hf, 1)
                if d:
                    low(d - 1)
            low(DB - 1)

        def x_updated(eng, e, d):
            eng.wait_ge(s_xr[1 - d % 2], DB // 2 * (e // 2) + d // 2 + 1)

        def dve_post(dve, e):
            base = DB * (e // 2)
            dve.wait_ge(s_rstd, e + 1)
            for d in range(DB):
                dve.scalar_tensor_tensor(out=y[:, d, :], in0=y[:, d, :], scalar=gain[:, e * DB + d:e * DB + d + 1],
                                         in1=rstd[:, :], op0=ALU.mult, op1=ALU.mult).then_inc(s_yn, 1)
                if d % 2:
                    dve.wait_ge(s_yn, base + d + 1)
                    dve.tensor_tensor(x[:, d, :], x[:, d, :], y[:, d, :], ALU.add).then_inc(s_xr[0], 1)

        def pool_post(pool, e):
            for d in range(0, DB, 2):
                pool.wait_ge(s_yn, DB * (e // 2) + d + 1)
                pool.tensor_tensor(x[:, d, :], x[:, d, :], y[:, d, :], ALU.add).then_inc(s_xr[1], 1)

        def act_output(act, c, o, d, it=0, nc_=0, no=0):
            summed(act, c, it, nc_)
            at = bass.ds(it * no + d, 1)
            src = bank[o % SLOTS][:, :].unsqueeze(1)
            act.activation(sq[:, at, :], src, ACT.Square, scale=1 / WS).then_inc(s_sq, 1)
            act.activation(y[:, at, :], src, ACT.Copy, scale=1 / WS).then_inc(b_free[o % SLOTS], 1)

        def act_outproj(act, c, o):
            with act.Fori(0, DB // SLOTS) as it:
                for j in range(SLOTS):
                    split_hi(act, c + j + 2, it, SLOTS)
                    act_output(act, c + j, o + j, j, it, SLOTS, SLOTS)

        def dve_outproj(dve, c):
            with dve.Fori(0, DB // SLOTS) as it:
                for j in range(SLOTS):
                    split_lo(dve, c + j + 2, it, SLOTS)

        def pe_ffn(pe, L):
            e = 4 * L + 3
            project(pe, C_FIN[L], O_FIN[L], FIN, e - 1)
            pe.wait_ge(s_ln, e)
            pe.matmul(bank[4][:, :], zero[:, 0:P], zero[:, :], start=True, stop=False)

            def sum_block(it, j):
                pe.wait_ge(s_sq, it * SLOTS + (DB * e + j + 1))
                pe.matmul(bank[4][:, :].unsqueeze(1), ones, sq[:, bass.ds(it * SLOTS + j, 1), :], start=False, stop=False)

            with pe.Fori(0, 2) as it:
                for j in range(SLOTS):
                    for u in range(3):
                        if j == 0:
                            pe.wait_ge(s_g, FB * L + min(8 * (u + 1), FB))
                        chunk(pe, C_FOUT[L] + 3 * j + u, O_FOUT[L] + j, gh, gl, 8 * u, u == 0, u == 2, it, 12)
                    if j:
                        sum_block(it, j - 1)
                sum_block(it, SLOTS - 1)
            pe.matmul(bank[4][:, :], zero[:, 0:P], zero[:, :], start=False, stop=True).then_inc(s_sum, 1)

        def act_ffn(act, L):
            act.preload_act_table_set("silu_and_others")
            c0, o0 = C_FIN[L], O_FIN[L]
            with act.Fori(0, FIN // SLOTS) as it:
                for j in range(SLOTS):
                    split_hi(act, c0 + j + 2, it, SLOTS)
                    summed(act, c0 + j, it, SLOTS)
                    if j % 2 == 0:
                        act.wait_ge(s_prod, it * 2 + (FB * L + j // 2 + 1))
                    k = it * SLOTS + (L * FIN + j)
                    act.activation(cu[:, j, :], bank[(o0 + j) % SLOTS][:, :], ACT.Identity,
                                   scale=fcw[:, bass.ds(k + 2 * 2 * FIN, 1)], bias=par[:, bass.ds(k + PARAM["fcb"][0], 1)]
                                   ).then_inc(s_cv, 1)
                    if j % 2 == 0:
                        was_read(act, o0 + j, it, SLOTS)
                        act.activation(cu[:, j, :], cu[:, j, :], ACT.Silu).then_inc(s_silu, 1)
            if L == 0:
                with act.Fori(0, 2) as it:
                    act_ffn_out(act, L, it)
            else:
                for it in range(2):
                    act_ffn_out(act, L, it)

        def act_ffn_out(act, L, it):
            for j in range(12):
                c = C_FOUT[L] + j
                if L == 0:
                    split_hi(act, c + 2, it, 12)
                else:
                    split_hi(act, c + 2 + 12 * it)
                if j % 3 == 2:
                    act_output(act, c, O_FOUT[L] + j // 3, j // 3, it, 12, 4)

        def dve_ffn(dve, L):
            c0, o0 = C_FIN[L], O_FIN[L]
            with dve.Fori(0, FIN // SLOTS) as it:
                for j in range(SLOTS):
                    split_lo(dve, c0 + j + 2, it, SLOTS)
                    k = it * SLOTS + (L * FIN + j)
                    b = bank[(o0 + j) % SLOTS]
                    dve.wait_ge(s_cv, it * SLOTS + (12 + L * FIN + j + 1))
                    dve.scalar_tensor_tensor(out=cu[:, j, 1:S], in0=b[:, 0:S - 1],
                                             scalar=fcw[:, bass.ds(k + 2 * FIN, 1)], in1=cu[:, j, 1:S],
                                             op0=ALU.mult, op1=ALU.add).then_inc(s_c1, 1)
                    dve.wait_ge(s_c1, it * SLOTS + (24 + L * FIN + j + 1))
                    dve.scalar_tensor_tensor(out=cu[:, j, 2:S], in0=b[:, 0:S - 2],
                                             scalar=fcw[:, bass.ds(k, 1)], in1=cu[:, j, 2:S],
                                             op0=ALU.mult, op1=ALU.add).then_inc(b_free[(o0 + j) % SLOTS], 1)
                    if j % 2:
                        p = it * 2 + (FB * L + j // 2 + 1)
                        at = bass.ds(it * 2 + j // 2, 1)
                        g32 = gf.unsqueeze(1)
                        dve.wait_ge(s_silu, p)
                        was_read(dve, o0 + j, it, SLOTS)
                        dve.tensor_tensor(gf, cu[:, j - 1, :], cu[:, j, :], ALU.mult).then_inc(s_prod, 1)
                        dve.wait_ge(s_prod, p + 2)
                        dve.tensor_copy(gh[:, at, :], g32).then_inc(s_gh, 1)
                        dve.wait_ge(s_gh, p)
                        dve.tensor_tensor(gl[:, at, :], g32, gh[:, at, :], ALU.subtract).then_inc(s_g, 1)
            if L == 0:
                with dve.Fori(0, 2) as it:
                    for j in range(12):
                        split_lo(dve, C_FOUT[L] + j + 2, it, 12)
            else:
                for c in range(C_FOUT[L], C_END):
                    split_lo(dve, c + 2)

        def act_hybrid_in(act):
            act.preload_act_table_set("silu_and_others")

            def silu(i):
                was_read(act, O_HIN + QKV + i)
                act.activation(QKVS[:, i, :], QKVS[:, i, :], ACT.Silu).then_inc(s_qs, 1)

            def leave(o, out, func=ACT.Copy, scale=1 / WS):
                act.activation(out, bank[o % SLOTS][:, :], func, scale=scale).then_inc(b_free[o % SLOTS], 1)

            def high(o, out):
                act.activation(out, bank[o % SLOTS][:, :], ACT.Copy, scale=1 / WS).then_inc(s_qh, 1)

            for o in range(HIN):
                split_hi(act, o + 2)
                act_compress(act, o)
                summed(act, o)
                if o == ROWS:
                    leave(o, ROWT)
                elif o < QB:
                    i = o - QKV
                    act.activation(QKVS[:, i, :], bank[o % SLOTS][:, :], ACT.Identity,
                                   scale=gcw[:, i * GC + 3:i * GC + 4]).then_inc(s_cv, 1)
                    if i:
                        silu(i - 1)
                elif o < KC:
                    if o == QB:
                        silu(11)
                    high(o, QBP[:, 0, o - QB, :])
                elif o < KSW:
                    leave(o, KCF[:, o - KC, :])
                elif o < VSW:
                    high(o, KSP[:, 0, o - KSW, :])
                elif o < GA:
                    leave(o, VF[:, o - VSW, :])
                else:
                    leave(o, GAT[:, o - GA, :], ACT.Silu)

        def dve_hybrid_in(dve):
            for o in range(HIN):
                split_lo(dve, o + 2)
                dve_compress(dve, o)
                if QKV <= o < QB:
                    i = o - QKV
                    dve.wait_ge(s_cv, i + 1)
                    for t in (1, 2, 3):
                        m = dve.scalar_tensor_tensor(
                            out=QKVS[:, i, t:S], in0=bank[o % SLOTS][:, 0:S - t], scalar=gcw[:, i * GC + 3 - t:i * GC + 4 - t],
                            in1=QKVS[:, i, t:S], op0=ALU.mult, op1=ALU.add)
                        if t < 3:
                            m.then_inc(s_c1, 1)
                            dve.wait_ge(s_c1, 2 * i + t)
                    m.then_inc(b_free[o % SLOTS], 1)
                elif QB <= o < KC or KSW <= o < VSW:
                    i, pair = (o - QB, QBP) if o < KC else (o - KSW, KSP)
                    dve.wait_ge(s_qh, i + 1 if o < KC else KC - QB + i + 1)
                    dve.scalar_tensor_tensor(out=pair[:, 1, i, :], in0=bank[o % SLOTS][:, :], scalar=1 / WS,
                                             in1=pair[:, 0, i, :], op0=ALU.mult, op1=ALU.subtract
                                             ).then_inc(b_free[o % SLOTS], 1)

        W1_AT, BLK_AT = 9, VC + 1

        def pe_compress_in(pe):
            pe.wait_ge(s_wl, 8)
            pe.wait_ge(s_bl16, 2)
            for t in range(2):
                for g in range(2):
                    r = slice(g * DH, (g + 1) * DH)
                    for q in range(CL):
                        for j, (a, b) in enumerate(PASSES):
                            m = pe.matmul(bank[4 + g][:, t * NCP:t * NCP + NC], W1P[r, (t * CL + q) // 8, a, q % 8 * P:(q % 8 + 1) * P],
                                          BLKP[r, b, t, q * NC:(q + 1) * NC], start=(q == 0 and j == 0),
                                          stop=(q == CL - 1 and j == 2))
            m.then_inc(s_hid, 1)

        def pe_compress_v(pe):
            pe.wait_ge(s_msk, 16)
            for b in range(2):
                was_read(pe, O_HIN + VSW + b)
                for n in range(NT):
                    m = pe.transpose(bank[6 + b][:, n * P:(n + 1) * P], VF[:, b, n * P:(n + 1) * P], ident)
                m.then_inc(s_vt, 1)

        def pe_compress_out(pe):
            pe.wait_ge(s_hs, 4)
            pe.matmul(bank[5][:, 0:2 * NCP], W2[:, 0, :], HS[:, 0, :, :].rearrange("p g c -> p (g c)"), start=True, stop=True)
            for g in range(2):
                m = pe.matmul(bank[5][0:NCP, 64 + g * DH:64 + (g + 1) * DH], HS[:, 1, g, :], W2[:, 1, 0:DH],
                              start=True, stop=True)
            m.then_inc(s_kv, 1)
            for n in range(NT):
                m = pe.transpose(bank[4][:, n * P:(n + 1) * P], ROWT[:, n * P:(n + 1) * P], ident)
            m.then_inc(s_rt, 1)

        def dve_compress(dve, o):
            if o == 0:
                dve.memset(HS[:, :, :, :], 0.0).then_inc(s_clr, 1)
                dve.memset(VBD[:, :, :], 0.0).then_inc(s_clr, 1)
            k = o - W1_AT
            if 0 <= k < 8:
                dve.wait_ge(s_wh, k + 1)
                dve.scalar_tensor_tensor(out=W1P[:, k, 1, :], in0=W1[:, k, :], scalar=WS, in1=W1P[:, k, 0, :],
                                         op0=ALU.mult, op1=ALU.subtract).then_inc(s_wl, 1)
            t = o - BLK_AT
            if 0 <= t < 2:
                pe_ = PARAM["pe"][0]
                was_read(dve, O_HIN + KC + t)
                src = KCF[:, t, :].rearrange("p (c r) -> p r c", r=CS)
                for a in range(2):
                    dve.tensor_tensor(BLK[:, t, a * CS:(a + 1) * CS, :], src[:, :, a:a + NC],
                                      along(par[:, pe_ + t * CL + a * CS:pe_ + t * CL + (a + 1) * CS], NC),
                                      ALU.add).then_inc(s_blk, 1)
            t = o - BLK_AT - 1
            if 0 <= t < 2:
                dve.wait_ge(s_bh16, t + 1)
                dve.tensor_tensor(BLKP[:, 1, t, :], BLK[:, t, :, :].rearrange("p q c -> p (q c)"), BLKP[:, 0, t, :],
                                  ALU.subtract).then_inc(s_bl16, 1)
            if o == GA + 1:
                for b in range(2):
                    dve.wait_ge(s_vh, b + 1)
                    dve.tensor_tensor(VTP[:, 1, b, :, :], tiles(bank[6 + b][:, :]), VTP[:, 0, b, :, :],
                                      ALU.subtract).then_inc(s_vtk, 1)
            if o == GA + 3:
                dve.wait_ge(s_kch, 2)
                for g in range(2):
                    r = slice(g * DH, (g + 1) * DH)
                    dve.tensor_tensor(KCM[r, 1, :], bank[5][r, g * NCP:(g + 1) * NCP], KCM[r, 0, :],
                                      ALU.subtract).then_inc(s_kcm, 1)
                dve.wait_ge(s_clr, 2)
                for i in range(4):
                    dve.tensor_copy(VBD[i * NCP:(i + 1) * NCP, :, i * DH:(i + 1) * DH],
                                    bank[5][0:NCP, 64:64 + 2 * DH].rearrange("p (g d) -> p g d", g=2)).then_inc(s_kcm, 1)

        def act_compress(act, o):
            k = o - W1_AT
            if k == 0:
                act.wait_ge(s_w1, 16 * 6)
            if 0 <= k < 8:
                if k:
                    act.wait_ge(s_wl, k)
                act.activation(W1P[:, k, 0, :], W1[:, k, :], ACT.Copy, scale=WS).then_inc(s_wh, 1)
            t = o - BLK_AT - 1
            if 0 <= t < 2:
                act.wait_ge(s_blk, 2 * t + 2)
                act.activation(BLKP[:, 0, t, :], BLK[:, t, :, :].rearrange("p q c -> p (q c)"), ACT.Copy).then_inc(s_bh16, 1)
            if o == GA:
                act.wait_ge(s_hid, 1)
                act.wait_ge(s_clr, 1)
                for t in range(2):
                    for g in range(2):
                        act.activation(HS[:, t, g, 0:NC], bank[4 + g][:, t * NCP:t * NCP + NC], ACT.Silu, scale=1 / WS,
                                       bias=pr("b1", t)).then_inc(s_hs, 1)
            if o == GA + 1:
                for b in range(2):
                    act.wait_ge(s_vt, b + 1)
                    act.activation(VTP[:, 0, b, :, :], tiles(bank[6 + b][:, :]), ACT.Copy).then_inc(s_vh, 1)
            if o == GA + 2:
                act.wait_ge(s_kv, 1)
                for g in range(2):
                    r = slice(g * DH, (g + 1) * DH)
                    act.activation(KCM[r, 0, :], bank[5][r, g * NCP:(g + 1) * NCP], ACT.Copy).then_inc(s_kch, 1)

        def act_gates(act):
            act.preload_act_table_set("natural_log_exp_and_others")
            act.wait_ge(s_rt, 1)
            act.activation(SIG[:, :, 0:56], tiles(bank[4][:, :])[:, :, 32:88], ACT.Exp, scale=-1.0).then_inc(s_se, 1)
            link(act, act.activation(GZ[:, 0, :], ROWT[0:H, :], ACT.Identity, bias=pr("dtb")[0:H]), a_link, al)
            link(act, act.activation(GZ[:, 1, :], GZ[:, 0, :], ACT.Abs), a_link, al)
            link(act, act.activation(GZ[:, 1, :], GZ[:, 1, :], ACT.Exp, scale=-1.0), a_link, al)
            act.activation(GZ[:, 1, :], GZ[:, 1, :], ACT.Ln, bias=onec[0:H, 0:1]).then_inc(s_ga, 1)
            act.activation(NA[0:H, :], pr("alog")[0:H], ACT.Exp).then_inc(s_ga, 1)

        def dve_gates(dve):
            dve.wait_ge(s_se, 1)
            link(dve, dve.tensor_scalar(SIG[:, :, 0:56], SIG[:, :, 0:56], 1.0, None, ALU.add), v_link, vl)
            dve.reciprocal(SIG[:, :, 0:56], SIG[:, :, 0:56]).then_inc(s_sg, 1)

        def dve_decays(dve):
            dve.wait_ge(s_ga, 2)
            link(dve, dve.scalar_tensor_tensor(out=GZ[:, 2, :], in0=GZ[:, 0, :], scalar=0.0, in1=GZ[:, 1, :],
                                               op0=ALU.max, op1=ALU.add), v_link, vl)
            link(dve, dve.tensor_scalar(GZ[:, 2, :], GZ[:, 2, :], NA[0:H, :], -1.0, ALU.mult, ALU.mult), v_link, vl)
            for n in range(NT):
                t = slice(n * P, (n + 1) * P)
                dve.tensor_tensor_scan(G[:, t], ones[0:H, :], GZ[:, 2, t], 0.0, ALU.mult, ALU.add).then_inc(s_gg, 1)

        def pe_cmp(pe):
            pe.wait_ge(s_kcm, 6)
            for o in range(HIN - SLOTS, HIN):
                was_read(pe, o)
            for g in range(2):
                r = slice(g * DH, (g + 1) * DH)
                for n in range(NT):
                    for h in range(4):
                        a = (n * 4 + h) * NCP
                        for j, (a_, b_) in enumerate(PASSES):
                            m = pe.matmul(bank[2 + g][:, a:a + NCP], QBP[r, a_, h, n * P:(n + 1) * P], KCM[r, b_, :],
                                          start=(j == 0), stop=(j == 2))
                m.then_inc(s_cs, 1)
            pe.wait_ge(s_cp, 1)
            for n in range(NT):
                for g in range(2):
                    m = pe.transpose(bank[2 + n // 2][:, (n % 2 * 2 + g) * P:(n % 2 * 2 + g + 1) * P],
                                     CSC[:, n, g * P:(g + 1) * P], ident)
                if n % 2:
                    m.then_inc(s_ct, 1)
            for n in range(NT):
                pe.wait_ge(s_cpt, n // 2 + 1)
                if n >= 2:
                    pe.wait_ge(s_ca, n - 1)
                for g in range(2):
                    m = pe.matmul(bank[6 + n % 2][:, g * 4 * DH:(g + 1) * 4 * DH], CPT[:, n, g * P:(g + 1) * P],
                                  VBD[:, g, :], start=True, stop=True)
                m.then_inc(s_co, 1)

        def heads(a):
            return a.rearrange("p n (h c) -> p n h c", c=NCP)

        def dve_cmp(dve):
            rows = CSC.rearrange("p n (h c) -> p (n h) c", c=NCP)
            cadd, c01 = mk("cadd").rearrange("p (n c) -> p n c", c=NCP), mk("c01").rearrange("p (n c) -> p n c", c=NCP)
            for a in range(2):
                dve.wait_ge(s_cs, a + 1)
                link(dve, dve.tensor_tensor(heads(CSC)[:, :, 4 * a:4 * a + 4, :],
                                            bank[2 + a][:, :].rearrange("p (n h c) -> p n h c", h=4, c=NCP),
                                            cadd.unsqueeze(2).to_broadcast([P, NT, 4, NCP]), ALU.add), v_link, vl)
            link(dve, dve.tensor_reduce(CMX, rows, AX_X, ALU.max), v_link, vl)
            dve.tensor_tensor(rows, rows, along(CMX, NCP), ALU.subtract).then_inc(s_cm, 1)
            dve_gates(dve)
            dve.wait_ge(s_ce, 1)
            link(dve, dve.tensor_reduce(CLS, rows, AX_X, ALU.add), v_link, vl)
            link(dve, dve.reciprocal(CRC, CLS), v_link, vl)
            dve.wait_ge(s_sg, 1)
            link(dve, dve.tensor_tensor(CRC.rearrange("p (n h) -> p n h", h=NH), CRC.rearrange("p (n h) -> p n h", h=NH),
                                        SIG[:, :, 32:40], ALU.mult), v_link, vl)
            link(dve, dve.tensor_tensor(rows, rows, along(CRC, NCP), ALU.mult), v_link, vl)
            dve.tensor_tensor(heads(CSC), heads(CSC), c01.unsqueeze(2).to_broadcast([P, NT, NH, NCP]),
                              ALU.mult).then_inc(s_cp, 1)
            dve_decays(dve)
            for a in range(2):
                dve.wait_ge(s_ct, a + 1)
                dve.tensor_copy(CPT[:, 2 * a:2 * a + 2, :], bank[2 + a][:, :].rearrange("p (n c) -> p n c", n=2)
                                ).then_inc(s_cpt, 1)
            for n in range(NT):
                dve.wait_ge(s_co, n + 1)
                dve.tensor_copy(ACC[:, n, :], bank[6 + n % 2][:, :]).then_inc(s_ca, 1)

        UNITS = NT * 2 * NH

        TB = (2, 6, 7)
        def unit(u):
            return u // (2 * NH), u // NH % 2, u % NH, (u // (2 * NH) + 1) * P

        def pe_attention(pe):
            pe.wait_ge(s_vtk, 2)
            for u in range(UNITS + 4):
                if u < UNITS:
                    i, b, h, keys = unit(u)
                    r = slice(h // 4 * DH, h // 4 * DH + DH)
                    if u >= 2:
                        pe.wait_ge(s_m, u - 1)
                    for j, (a_, b_) in enumerate(PASSES):
                        m = pe.matmul(bank[4 + u % 2][:, 0:keys], QBP[r, a_, h % 4, i * P:(i + 1) * P], KSP[r, b_, b, 0:keys],
                                      start=(j == 0), stop=(j == 2))
                    m.then_inc(s_s, 1)
                if 2 <= u < UNITS + 2:
                    w = u - 2
                    i = unit(w)[0]
                    pe.wait_ge(s_e, w + 1)
                    if w >= 3:
                        pe.wait_ge(s_pl, w - 2)
                    else:
                        pe.wait_ge(s_ca, NT)
                    for k in range(i + 1):
                        m = pe.transpose(bank[TB[w % 3]][:, k * P:(k + 1) * P], PP[:, w % 3, k * P:(k + 1) * P], ident)
                    m.then_inc(s_t, 1)
                if u >= 4:
                    w = u - 4
                    i, b, h, keys = unit(w)
                    v = w // NH
                    pe.wait_ge(s_pl, w + 1)
                    if h == 0 and v >= 2:
                        pe.wait_ge(s_cb, v - 1)
                    for k in range(i + 1):
                        for j, (a_, b_) in enumerate(PASSES):
                            m = pe.matmul(bank[v % 2][:, h * DH:(h + 1) * DH], PTP[:, a_, w % 3, k * P:(k + 1) * P],
                                          VTP[:, b_, b, k, h // 4 * DH:h // 4 * DH + DH], start=(k == 0 and j == 0),
                                          stop=(k == i and j == 2))
                    m.then_inc(s_pv, 1)
                    if w % (2 * NH) == 6 and i:
                        pe_attention_out(pe, i - 1)
            pe_attention_out(pe, NT - 1)

        def pe_attention_out(pe, i):
            pe.wait_ge(s_acc, i + 1)
            if i:
                pe.wait_ge(s_om, i)
            for k in range(4):
                m = pe.transpose(bank[3][:, k * P:(k + 1) * P], ACC[:, i, k * P:(k + 1) * P], ident)
            m.then_inc(s_at, 1)

        def act_attention(act):
            act.wait_ge(s_cm, 1)
            act.activation(CSC[:, :, :], CSC[:, :, :], ACT.Exp, scale=DH ** -0.5).then_inc(s_ce, 1)

            def high(i):
                act.wait_ge(s_at, i + 1)
                act.activation(hh[:, 4:8, i * P:(i + 1) * P], tiles(bank[3][:, :]), ACT.Copy).then_inc(s_omh, 1)

            for u in range(UNITS + 2):
                if u >= 2:
                    w = u - 2
                    keys = unit(w)[3]
                    act.wait_ge(s_t, w + 1)
                    if w >= 3:
                        act.wait_ge(s_pv, w - 2)
                    act.activation(PTP[:, 0, w % 3, 0:keys], bank[TB[w % 3]][:, 0:keys], ACT.Copy).then_inc(s_pc, 1)
                if u >= UNITS:
                    continue
                i, b, h, keys = unit(u)
                v = u // NH
                act.wait_ge(s_m, u + 1)
                if u >= 3:
                    act.wait_ge(s_t, u - 2)
                if h == 0 and v >= 2:
                    act.wait_ge(s_cb, v - 1)
                act.activation(PP[:, u % 3, 0:keys], SM[:, u % 2, 0:keys], ACT.Exp, scale=-1.0,
                               bias=NMX[:, u % 2:u % 2 + 1], accum_out=LS[:, v % 2 * NH + h:v % 2 * NH + h + 1]
                               ).then_inc(s_e, 1)
                if u % (2 * NH) == 12 and i:
                    high(i - 1)
            high(NT - 1)

        def dve_attention(dve):
            def low(i):
                dve.wait_ge(s_omh, i + 1)
                t = slice(i * P, (i + 1) * P)
                dve.tensor_tensor(hl[:, 4:8, t], tiles(bank[3][:, :]), hh[:, 4:8, t], ALU.subtract).then_inc(s_om, 1)

            def combine(v):
                i, b = v // 2, v % 2
                dve.wait_ge(s_pv, NH * (v + 1))
                link(dve, dve.reciprocal(RC, LS[:, b * NH:(b + 1) * NH]), v_link, vl)
                link(dve, dve.tensor_tensor(RC, RC, SIG[:, i, 40 + NH * b:48 + NH * b], ALU.mult), v_link, vl)
                dve.tensor_tensor(TMP.rearrange("p (h d) -> p h d", d=DH), bank[v % 2][:, :].rearrange("p (h d) -> p h d", d=DH),
                                  along(RC, DH), ALU.mult).then_inc(s_cb, 1)
                dve.wait_ge(s_cb, v + 1)
                m = dve.tensor_tensor(ACC[:, i, :], ACC[:, i, :], TMP, ALU.add)
                if b:
                    m.then_inc(s_acc, 1)
                else:
                    link(dve, m, v_link, vl)

            for u in range(UNITS + 3):
                if u < UNITS:
                    i, b, h, keys = unit(u)
                    dve.wait_ge(s_s, u + 1)
                    if u >= 2:
                        dve.wait_ge(s_e, u - 1)
                    dve.tensor_tensor_reduce(out=SM[:, u % 2, 0:keys], in0=bank[4 + u % 2][:, 0:keys],
                                             in1=mk("neg")[:, S - keys:S], scale=-DH ** -0.5, scalar=3e38, op0=ALU.add,
                                             op1=ALU.min, accum_out=NMX[:, u % 2:u % 2 + 1]).then_inc(s_m, 1)
                if u >= 3:
                    w = u - 3
                    keys = unit(w)[3]
                    dve.wait_ge(s_pc, w + 1)
                    dve.tensor_tensor(PTP[:, 1, w % 3, 0:keys], bank[TB[w % 3]][:, 0:keys], PTP[:, 0, w % 3, 0:keys],
                                      ALU.subtract).then_inc(s_pl, 1)
                if u % NH == 4 and u > NH:
                    combine(u // NH - 1)
                if u % (2 * NH) == 14 and u > 2 * NH:
                    low(u // (2 * NH) - 1)
            combine(2 * NT - 1)
            low(NT - 1)

        def pe_gdn_prep(pe):
            for n in range(NT):
                pe.wait_ge(s_gg, n + 1)
                pe.transpose(bank[6][:, n * H:(n + 1) * H], G[:, n * P:(n + 1) * P], ident[0:H, 0:H])
            for h in range(H):
                m = pe.matmul(bank[6][:, 16 + h * NT:16 + (h + 1) * NT], mk("sel")[0:H, h * P:(h + 1) * P],
                              G[:, P - 1:S:P], start=True, stop=True)
            m.then_inc(s_gtr, 1)
            for i in range(8):
                pe.wait_ge(s_nq, i + 1)
                if i >= 2:
                    pe.wait_ge(s_nl, i - 1)
                pe.matmul(bank[i % 2][:, :], ones, EE[:, i % 2, :], start=True, stop=True).then_inc(s_ns, 1)
            for h in range(H):
                if h:
                    pe.wait_ge(s_eg, h)
                pe.matmul(bank[4][:, :], mk("sel")[0:H, h * P:(h + 1) * P], G[:, :], start=True, stop=True).then_inc(s_gb, 1)
                pe.wait_ge(s_nn, 5 + h)
                if h:
                    pe.wait_ge(s_ak, h)
                else:
                    pe.wait_ge(s_gt, 2)
                q, k, v = (tiles(QKVS[:, a + h, :]) for a in (0, 4, 8))
                for n in range(NT):
                    m = pe.matmul(bank[5][:, n * P:(n + 1) * P], k[:, n, :], k[:, n, :], start=True, stop=True)
                m.then_inc(s_kk, 1)
                if h:
                    pe.wait_ge(s_aq, h)
                for n in range(NT):
                    m = pe.matmul(bank[6][:, n * P:(n + 1) * P], k[:, n, :], q[:, n, :], start=True, stop=True)
                m.then_inc(s_qk, 1)
                if h:
                    pe.wait_ge(s_kd, h)
                for n in range(NT):
                    m = pe.transpose(bank[7][:, n * P:(n + 1) * P], k[:, n, :], ident)
                m.then_inc(s_kt, 1)
                if h:
                    pe.wait_ge(s_bv, h)
                else:
                    pe.wait_ge(s_nl, 8)
                for n in range(NT):
                    m = pe.transpose(bank[0][:, n * P:(n + 1) * P], v[:, n, :], ident)
                m.then_inc(s_vr, 1)

        def act_gdn_prep(act):
            act.wait_ge(s_gt, 2)
            act.activation(EGT, GT, ACT.Exp).then_inc(s_ge, 1)
            act.activation(EGL, GLB, ACT.Exp).then_inc(s_ge, 1)
            act.wait_ge(s_gk, 1)
            act.activation(EKD, EKD, ACT.Exp).then_inc(s_ge, 1)

            def rst(i):
                act.wait_ge(s_ns, i + 1)
                if i >= 2:
                    act.wait_ge(s_nn, i - 1)
                act.activation(hf[:, i % 2, :], bank[i % 2][:, :], ACT.Ln, bias=epsc[:, 1:2]).then_inc(s_nl, 1)
                act.wait_ge(s_nl, i + 1)
                act.activation(hf[:, i % 2, :], hf[:, i % 2, :], ACT.Exp, scale=-0.5).then_inc(s_nr, 1)

            for i in range(8):
                act.wait_ge(s_qs, i + 1)
                if i >= 2:
                    act.wait_ge(s_ns, i - 1)
                act.activation(EE[:, i % 2, :], QKVS[:, i, :], ACT.Square).then_inc(s_nq, 1)
                if i:
                    rst(i - 1)
            rst(7)
            for h in range(H):
                act.wait_ge(s_dd, 2 * (h + 1))
                act.activation(EE[:, 0, :], EE[:, 0, :], ACT.Exp, scale=-1.0).then_inc(s_ex, 1)
                act.activation(EE[:, 1, :], EE[:, 1, :], ACT.Exp).then_inc(s_ex, 1)
                if h:
                    act.wait_ge(s_qg, h)
                act.activation(EE[:, 2, :], bank[4][:, :], ACT.Exp).then_inc(s_eg, 1)

        def pool_gdn(pool):
            for h in range(H):
                pool.wait_ge(s_ex, 2 * h + 1)
                link(pool, pool.tensor_tensor(tiles(EE[:, 0, :]), tiles(EE[:, 0, :]), spread(mk("strict"), NT), ALU.mult),
                     g_link, gl_)
                pool.tensor_tensor(tiles(EE[:, 0, :]), tiles(EE[:, 0, :]), along(BT[:, h * NT:(h + 1) * NT], P),
                                   ALU.mult).then_inc(s_e1, 1)
                pool.wait_ge(s_ex, 2 * h + 2)
                pool.tensor_tensor(tiles(EE[:, 1, :]), tiles(EE[:, 1, :]), spread(mk("incl"), NT),
                                   ALU.mult).then_inc(s_e2, 1)
                pool.wait_ge(s_eg, h + 1)
                pool.wait_ge(s_qk, h + 1)
                pool.tensor_tensor(QKVS[:, h, :], QKVS[:, h, :], EE[:, 2, :], ALU.mult).then_inc(s_qg, 1)
            for lv in range(7):
                for h in range(H):
                    if lv == 0:
                        pool.wait_ge(s_ak, h + 1)
                    elif lv == 1:
                        pool.wait_ge(s_tt, h + 1)
                    else:
                        pool.wait_ge(s_xp, (lv - 2) * H + h + 1)
                    m = mk("lev")[:, lv * P:(lv + 1) * P]
                    pool.tensor_tensor(BM[:, h, :, :], AK[:, h, :, :], spread(m, NT), ALU.mult).then_inc(s_b, 1)

        def dve_gdn_prep(dve):
            dve.wait_ge(s_gtr, 1)
            dve.wait_ge(s_sg, 1)
            dve.tensor_copy(GT.rearrange("p (h n) -> p n h", n=NT), bank[6][:, 0:16].rearrange("p (n h) -> p n h", n=NT)
                            ).then_inc(s_gt, 1)
            dve.tensor_copy(GLB, bank[6][:, 16:32]).then_inc(s_gt, 1)
            link(dve, dve.tensor_copy(BT.rearrange("p (h n) -> p n h", n=NT), SIG[:, :, 0:H]), v_link, vl)
            dve.wait_ge(s_gt, 2)
            dve.tensor_tensor(EKD, GLB, GT, ALU.subtract).then_inc(s_gk, 1)
            dve.wait_ge(s_ge, 1)
            dve.tensor_tensor(BEG, BT, EGT, ALU.mult).then_inc(s_gk, 1)
            for i in range(8):
                dve.wait_ge(s_nr, i + 1)
                if i < 4:
                    dve.scalar_tensor_tensor(out=QKVS[:, i, :], in0=QKVS[:, i, :], scalar=P ** -0.5, in1=hf[:, i % 2, :],
                                             op0=ALU.mult, op1=ALU.mult).then_inc(s_nn, 1)
                else:
                    dve.tensor_tensor(QKVS[:, i, :], QKVS[:, i, :], hf[:, i % 2, :], ALU.mult).then_inc(s_nn, 1)
            dve.wait_ge(s_ge, 3)
            dve.wait_ge(s_gk, 2)
            for h in range(H):
                c = slice(h * NT, (h + 1) * NT)
                dve.wait_ge(s_gb, h + 1)
                if h:
                    dve.wait_ge(s_aq, h)
                dve.tensor_tensor(tiles(EE[:, 0, :]), tiles(bank[4][:, :]), along(GT[:, c], P), ALU.subtract).then_inc(s_d, 1)
                dve.wait_ge(s_d, h + 1)
                dve.tensor_scalar(EE[:, 1, :], EE[:, 0, :], 0.0, None, ALU.min).then_inc(s_dd, 1)
                dve.tensor_scalar(EE[:, 0, :], EE[:, 0, :], 0.0, None, ALU.max).then_inc(s_dd, 1)
                dve.wait_ge(s_kt, h + 1)
                dve.tensor_tensor(KD[:, h, :, :], tiles(bank[7][:, :]), along(EKD[:, c], P), ALU.mult)
                dve.tensor_tensor(tiles(QKVS[:, 4 + h, :]), tiles(bank[7][:, :]), along(BEG[:, c], P),
                                  ALU.mult).then_inc(s_kd, 1)
                dve.wait_ge(s_vr, h + 1)
                dve.tensor_tensor(tiles(QKVS[:, 8 + h, :]), tiles(bank[0][:, :]), along(BT[:, c], P),
                                  ALU.mult).then_inc(s_bv, 1)
                dve.wait_ge(s_e1, h + 1)
                dve.tensor_tensor(AK[:, h, :, :], tiles(bank[5][:, :]), tiles(EE[:, 0, :]), ALU.mult).then_inc(s_ak, 1)
                dve.wait_ge(s_e2, h + 1)
                dve.tensor_tensor(AQ[:, h, :, :], tiles(bank[6][:, :]), tiles(EE[:, 1, :]), ALU.mult).then_inc(s_aq, 1)

        def pe_inverse(pe):
            for h in range(H):
                pe.wait_ge(s_tt, h + 1)
                if h == 0:
                    pe.wait_ge(s_bv, H)
                for n in range(NT):
                    m = pe.transpose(bank[h][:, n * P:(n + 1) * P], TT[:, h, n, :], ident)
                m.then_inc(s_ut, 1)
            for lv in range(1, 7):
                for h in range(H):
                    pe.wait_ge(s_uu, (lv - 1) * H + h + 1)
                    pe.wait_ge(s_b, lv * H + h + 1)
                    pe.wait_ge(s_tt, (lv - 1) * H + h + 1)
                    for n in range(NT):
                        m = pe.matmul(bank[h][:, n * P:(n + 1) * P], BM[:, h, n, :], UU[:, h, n, :], start=True, stop=True)
                    m.then_inc(s_xp, 1)
                for h in range(H):
                    pe.wait_ge(s_xx, (lv - 1) * H + h + 1)
                    if lv == 1:
                        pe.wait_ge(s_aq, H)
                    for n in range(NT):
                        m = pe.matmul(bank[4 + h][:, n * P:(n + 1) * P], TT[:, h, n, :], XX[:, h, n, :], start=True, stop=True)
                    m.then_inc(s_zu, 1)
                for h in range(H):
                    if lv == 6:
                        break
                    for n in range(NT):
                        m = pe.matmul(bank[h][:, n * P:(n + 1) * P], XX[:, h, n, :], TT[:, h, n, :], start=True, stop=True)
                    m.then_inc(s_zt, 1)

        def dve_inverse(dve):
            for h in range(H):
                dve.wait_ge(s_b, h + 1)
                dve.tensor_tensor(TT[:, h, :, :], spread(ident, NT), BM[:, h, :, :], ALU.subtract).then_inc(s_tt, 1)
            for h in range(H):
                dve.wait_ge(s_ut, h + 1)
                dve.tensor_copy(UU[:, h, :, :], tiles(bank[h][:, :])).then_inc(s_uu, 1)
            for lv in range(1, 7):
                for h in range(H):
                    dve.wait_ge(s_zu, (lv - 1) * H + h + 1)
                    dve.tensor_tensor(UU[:, h, :, :], UU[:, h, :, :], tiles(bank[4 + h][:, :]), ALU.subtract).then_inc(s_uu, 1)
                for h in range(H):
                    if lv == 6:
                        break
                    dve.wait_ge(s_zt, (lv - 1) * H + h + 1)
                    dve.tensor_tensor(TT[:, h, :, :], TT[:, h, :, :], tiles(bank[h][:, :]), ALU.subtract).then_inc(s_tt, 1)

        def act_inverse(act):
            for i in range(6 * H):
                act.wait_ge(s_xp, i + 1)
                act.activation(XX[:, i % H, :, :], tiles(bank[i % H][:, :]), ACT.Copy).then_inc(s_xx, 1)

        def pe_gdn_scan(pe):
            for h in range(H):
                pe.wait_ge(s_uu, 6 * H + h + 1)
                for n in range(NT):
                    m = pe.matmul(bank[h][:, n * P:(n + 1) * P], UU[:, h, n, :], QKVS[:, 8 + h, n * P:(n + 1) * P],
                                  start=True, stop=True)
                m.then_inc(s_u, 1)
                for n in range(NT):
                    m = pe.matmul(bank[4 + h][:, n * P:(n + 1) * P], QKVS[:, 4 + h, n * P:(n + 1) * P], UU[:, h, n, :],
                                  start=True, stop=True)
                m.then_inc(s_w, 1)
            for n in range(NT):
                if n:
                    pe.wait_ge(s_ss, n)
                    for h in range(H):
                        m = pe.matmul(bank[0][:, h * P:(h + 1) * P], WT[:, h, n, :], SS[:, h, :],
                                      start=True, stop=True)
                    m.then_inc(s_p2, 1)
                pe.wait_ge(s_vn, n + 1)
                if n == 0:
                    pe.wait_ge(s_wt, H)
                if n < NT - 1:
                    for h in range(H):
                        m = pe.matmul(bank[1][:, h * P:(h + 1) * P], KD[:, h, n, :], VN[:, h, :], start=True, stop=True)
                    m.then_inc(s_ds, 1)
                for h in range(H):
                    o = bank[4 + n][:, h * P:(h + 1) * P]
                    if n:
                        pe.matmul(o, SS[:, h, :], QKVS[:, h, n * P:(n + 1) * P], start=True, stop=False)
                    m = pe.matmul(o, VN[:, h, :], AQ[:, h, n, :], start=(n == 0), stop=True)
                m.then_inc(s_oo, 1)
            for h in range(H):
                pe.wait_ge(s_hq, h + 1)
                pe.matmul(bank[4 + h][:, :], ones, EE[:, h % 2, :], start=True, stop=True).then_inc(s_hsum, 1)

        def act_gdn_scan(act):
            for h in range(H):
                act.wait_ge(s_u, h + 1)
                act.activation(US[:, h, :, :], tiles(bank[h][:, :]), ACT.Copy).then_inc(s_us, 1)
                act.wait_ge(s_w, h + 1)
                act.activation(WT[:, h, :, :], tiles(bank[4 + h][:, :]), ACT.Copy).then_inc(s_wt, 1)
            for n in range(NT):
                act.wait_ge(s_oo, n + 1)
                act.activation(OA[:, :, n, :], tiles(bank[4 + n][:, :]), ACT.Copy).then_inc(s_oa, 1)
            act.wait_ge(s_oa, NT)

            def rst(h):
                act.wait_ge(s_hsum, h + 1)
                if h >= 2:
                    act.wait_ge(s_on, h - 1)
                act.activation(hf[:, h % 2, :], bank[4 + h][:, :], ACT.Ln, bias=epsc[:, 2:3]).then_inc(s_hln, 1)
                act.wait_ge(s_hln, h + 1)
                act.activation(hf[:, h % 2, :], hf[:, h % 2, :], ACT.Exp, scale=-0.5).then_inc(s_hr, 1)

            for h in range(H):
                if h >= 2:
                    act.wait_ge(s_hsum, h - 1)
                act.activation(tiles(EE[:, h % 2, :]), OA[:, h, :, :], ACT.Square).then_inc(s_hq, 1)
                if h:
                    rst(h - 1)
            rst(H - 1)
            for h in range(H):
                act.wait_ge(s_on, h + 1)
                act.activation(tiles(hh[:, h, :]), OA[:, h, :, :], ACT.Copy).then_inc(s_omh, 1)

        def dve_gdn_scan(dve):
            dve.wait_ge(s_us, H)
            dve.wait_ge(s_wt, H)
            for n in range(NT):
                if n == 0:
                    dve.tensor_copy(VN, US[:, :, 0, :]).then_inc(s_vn, 1)
                else:
                    link(dve, dve.tensor_tensor(SD, SS, along(EGL[:, n:4 * H:NT], P), ALU.mult), v_link, vl)
                    dve.wait_ge(s_p2, n)
                    dve.tensor_tensor(VN, US[:, :, n, :], tiles(bank[0][:, :]), ALU.subtract).then_inc(s_vn, 1)
                if n < NT - 1:
                    dve.wait_ge(s_ds, n + 1)
                    if n == 0:
                        dve.tensor_copy(SS, tiles(bank[1][:, :])).then_inc(s_ss, 1)
                    else:
                        dve.wait_ge(s_oo, n + 1)
                        dve.tensor_tensor(SS, SD, tiles(bank[1][:, :]), ALU.add).then_inc(s_ss, 1)
                    dve.wait_ge(s_ss, n + 1)
            for h in range(H):
                dve.wait_ge(s_hr, h + 1)
                link(dve, dve.scalar_tensor_tensor(out=OA[:, h, :, :], in0=OA[:, h, :, :], scalar=hon[:, 0:1],
                                                   in1=tiles(hf[:, h % 2, :]), op0=ALU.mult, op1=ALU.mult), v_link, vl)
                dve.tensor_tensor(OA[:, h, :, :], OA[:, h, :, :], tiles(GAT[:, h, :]), ALU.mult).then_inc(s_on, 1)
            for h in range(H):
                dve.wait_ge(s_omh, NT + h + 1)
                dve.tensor_tensor(tiles(hl[:, h, :]), OA[:, h, :, :], tiles(hh[:, h, :]), ALU.subtract).then_inc(s_om, 1)

        HB = DH
        AT_Z, AT_B, AT_K, AT_KQ, AT_V, AT_S = 2, 6, GV, GV + 2, GR, GR + 2

        def pe_gla(pe):
            first_two(pe, C_GIN, O_GIN, s_h, 2 * DB)
            for i in range(2, GIN + 1):
                pe_gla_step(pe, i)
                if i < GIN:
                    chunk(pe, C_GIN + i, O_GIN + i, hh, hl)
            pe.wait_ge(s_loo, 2 * NT)
            pe.wait_ge(s_lss, NT - 1)
            for h in range(H):
                for a in range(2):
                    pe.wait_ge(s_hq, H + 2 * h + a + 1)
                    m = pe.matmul(bank[4 + h][:, :], ones, SQO[:, 2 * h + a, :], start=(a == 0), stop=(a == 1))
                m.then_inc(s_hsum, 1)

        def pe_gla_step(pe, i):
            k = i - AT_Z
            if k in (0, 1):
                was_read(pe, O_GIN + ALR)
                pe.wait_ge(s_aw, 16)
                for h in (2 * k, 2 * k + 1):
                    pe.matmul(bank[4 + h][:, :], AW2[0:16, h * P:(h + 1) * P], ALRS[0:16, :], start=True, stop=True
                              ).then_inc(s_z, 1)
            h = i - AT_KQ - 1
            if 0 <= h < H:
                kk = KKT[:, h % 2, :]
                qt = QT[:, h % 2, :].rearrange("p (n a r) -> p n a r", a=2, r=HB)
                pe.wait_ge(s_lm, h + 1)
                if h >= 2:
                    pe.wait_ge(s_la, h - 1)
                for n in range(NT):
                    pe.matmul(bank[4 + h % 2][:, n * P + HB:(n + 1) * P], kk[:, n * P:(n + 1) * P], qt[:, n, 1, :],
                              start=True, stop=True)
                    m = pe.matmul(bank[4 + h % 2][:, n * P:n * P + HB], kk[:, S + n * P:S + (n + 1) * P], qt[:, n, 0, :],
                                  start=True, stop=True)
                m.then_inc(s_lap, 1)
                pe.wait_ge(s_lg, h + 1)
                if h >= 2:
                    pe.wait_ge(s_kdt, h - 1)
                for n in range(NT):
                    m = pe.transpose(bank[6 + h % 2][:, n * P:(n + 1) * P], LK[:, h, n * P:(n + 1) * P], ident)
                m.then_inc(s_kp, 1)
            k = i - AT_V - 1
            if k in (0, 1):
                if k == 0:
                    pe.wait_ge(s_la, H)
                    pe.wait_ge(s_kdt, H)
                    for o in range(4):
                        was_read(pe, O_GIN + GR - 1 - o)
                for j in range(4 * k, 4 * k + 4):
                    n, a = j // 2, j % 2
                    if k:
                        pe.wait_ge(s_vv[a], j // 2 - 1)
                    for b in range(4):
                        m = pe.transpose(bank[4 + j % 4][:, b * P:(b + 1) * P], VFF[:, 4 * a + b, n * P:(n + 1) * P], ident)
                    m.then_inc(s_vp, 1)
            n = i - AT_S - 1
            if 0 <= n < NT:
                if n == 0:
                    for a in range(2):
                        pe.wait_ge(s_vv[a], NT)
                else:
                    pe.wait_ge(s_lss, n)
                    pe.wait_ge(s_loo, 2 * n)
                if n < NT - 1:
                    for h in range(H):
                        m = pe.matmul(bank[4 + h // 2][:, h % 2 * 2 * P:(h % 2 + 1) * 2 * P], KDT[:, h, n, :],
                                      VTT[:, n, h * 2 * P:(h + 1) * 2 * P], start=True, stop=True)
                    m.then_inc(s_lds, 1)
                for i_ in range(DB):
                    h = i_ // 2
                    o = bank[6 + i_ // 4][:, i_ % 4 * P:(i_ % 4 + 1) * P]
                    if n:
                        pe.matmul(o, LST[:, h, i_ % 2 * P:(i_ % 2 + 1) * P], LQ[:, h, n * P:(n + 1) * P], start=True, stop=False)
                    m = pe.matmul(o, VTT[:, n, i_ * P:(i_ + 1) * P], LA[:, h, n, :], start=(n == 0), stop=True)
                m.then_inc(s_lo, 1)

        def act_gla(act):
            for i in range(GIN):
                o = O_GIN + i
                split_hi(act, C_GIN + i + 2)
                if i == GR:
                    act.preload_act_table_set("silu_and_others")
                act_gla_step(act, i)
                summed(act, C_GIN + i)
                src = bank[o % SLOTS][:, :]
                if i == ALR:
                    m = act.activation(ALRS, src, ACT.Copy, scale=1 / WS)
                elif i < GK:
                    m = act.activation(LQ[:, i - GQ, :], src, ACT.Copy, scale=P ** -0.5 / WS)
                elif i < GV:
                    m = act.activation(LK[:, i - GK, :], src, ACT.Copy, scale=1 / WS)
                elif i < GR:
                    m = act.activation(VFF[:, i - GV, :], src, ACT.Copy, scale=1 / WS)
                else:
                    m = act.activation(RS[:, i - GR, :], src, ACT.Silu, scale=1 / WS)
                m.then_inc(b_free[o % SLOTS], 1)
            act.preload_act_table_set("natural_log_exp_and_others")
            for h in range(H):
                act.wait_ge(s_hsum, H + h + 1)
                if h >= 2:
                    act.wait_ge(s_on, H + 2 * (h - 1))
                act.activation(hf[:, h % 2, :], bank[4 + h][:, :], ACT.Ln, bias=epsc[:, 3:4]).then_inc(s_hln, 1)
                act.wait_ge(s_hln, H + h + 1)
                act.activation(hf[:, h % 2, :], hf[:, h % 2, :], ACT.Exp, scale=-0.5).then_inc(s_hr, 1)
                for a in range(2):
                    i = 2 * h + a
                    act.wait_ge(s_on, H + i + 1)
                    act.activation(hh[:, i, :], OO[:, i, :], ACT.Copy).then_inc(s_omh, 1)

        def act_gla_step(act, i):
            h = i - AT_Z
            if 0 <= h < H:
                z, t = LZ[:, h % 2, :], LZ[:, 2 + h % 2, :]
                act.wait_ge(s_z, h + 1)
                if h >= 2:
                    act.wait_ge(s_lb, h - 1)
                link(act, act.activation(z, bank[4 + h][:, :], ACT.Identity, bias=pr("lab", h)), a_link, al)
                link(act, act.activation(t, z, ACT.Abs), a_link, al)
                link(act, act.activation(t, t, ACT.Exp, scale=-1.0), a_link, al)
                act.activation(t, t, ACT.Ln, bias=onec[:, 0:1]).then_inc(s_zl, 1)
            if i == AT_B:
                act.wait_ge(s_lb, H)
                act.activation(EBL.rearrange("p (h c) -> p h c", h=H), LB[:, :, HB - 1:S:HB], ACT.Exp, scale=1 / 16
                               ).then_inc(s_bl, 1)
            h = i - AT_K
            if 0 <= h < H:
                act.wait_ge(s_lx, h + 1)
                act.activation(EX[:, 0, :], EX[:, 0, :], ACT.Exp, scale=1 / 16).then_inc(s_le, 1)
                act.activation(EX[:, 1, :], LB[:, h, :], ACT.Exp, scale=1 / 16).then_inc(s_le, 1)
                act.activation(EX[:, 2, :], LB[:, h, :], ACT.Exp, scale=-1 / 16).then_inc(s_le, 1)
            h = i - AT_KQ - 1
            if 0 <= h < H:
                act.wait_ge(s_kp, h + 1)
                act.activation(KDT[:, h, :, :], tiles(bank[6 + h % 2][:, :]), ACT.Copy).then_inc(s_kdt, 1)
            k = i - AT_V - 1
            if k in (0, 1):
                for n in (2 * k, 2 * k + 1):
                    act.wait_ge(s_vp, 2 * n + 1)
                    act.activation(VTT[:, n, 0:S], bank[4 + 2 * n % 4][:, :], ACT.Copy).then_inc(s_vv[0], 1)
            n = i - AT_S - 1
            if 0 <= n < NT:
                act.wait_ge(s_lo, n + 1)
                for a in range(2):
                    act.activation(OO[:, 4 * a:4 * a + 4, n * P:(n + 1) * P], tiles(bank[6 + a][:, :]),
                                   ACT.Copy).then_inc(s_loo, 1)
            if n == NT - 1:
                act.wait_ge(s_loo, 2 * NT)
                for b in range(DB):
                    act.activation(SQO[:, b, :], OO[:, b, :], ACT.Square).then_inc(s_hq, 1)

        def pool_gla(pool):
            for h in range(H):
                qt = QT[:, h % 2, :].rearrange("p (n a r) -> p n a r", a=2, r=HB)
                mixed, kt = (KKT[:, h % 2, a:a + S].rearrange("p (n a r) -> p n a r", a=2, r=HB) for a in (0, S))
                q, k = (a[:, h, :].rearrange("p (n a r) -> p n a r", a=2, r=HB) for a in (LQ, LK))
                e = EBL[:, 8 * h:8 * h + 8].rearrange("p (n a) -> p n a", a=2)
                pool.wait_ge(s_bl, 1)
                pool.wait_ge(s_lk, h + 1)
                pool.tensor_copy(mixed[:, :, 0, :], k[:, :, 0, :])
                pool.tensor_copy(mixed[:, :, 1, :], kt[:, :, 1, :]).then_inc(s_lm, 1)
                pool.tensor_copy(q[:, :, 0, :], qt[:, :, 0, :])
                pool.tensor_tensor(q[:, :, 1, :], qt[:, :, 1, :], along(e[:, :, 0], HB), ALU.mult)
                pool.tensor_tensor(k[:, :, 0, :], k[:, :, 0, :], along(e[:, :, 1], HB), ALU.mult).then_inc(s_lg, 1)

        def dve_gla(dve):
            for i in range(GIN):
                split_lo(dve, C_GIN + i + 2)
                dve_gla_step(dve, i)
            was_read(dve, O_GIN + GIN - 1)
            for i in range(DB):
                dve.wait_ge(s_hq, H + i + 1)
                dve.scalar_tensor_tensor(out=OO[:, i, :], in0=OO[:, i, :], scalar=hon[:, 1 + i % 2:2 + i % 2],
                                         in1=RS[:, i, :], op0=ALU.mult, op1=ALU.mult).then_inc(s_og, 1)
            for i in range(DB + 1):
                if i < DB:
                    dve.wait_ge(s_hr, H + i // 2 + 1)
                    dve.wait_ge(s_og, i + 1)
                    dve.tensor_tensor(OO[:, i, :], OO[:, i, :], hf[:, i // 2 % 2, :], ALU.mult).then_inc(s_on, 1)
                if i:
                    j = i - 1
                    dve.wait_ge(s_omh, DB + j + 1)
                    dve.tensor_tensor(hl[:, j, :], OO[:, j, :], hh[:, j, :], ALU.subtract).then_inc(s_om, 1)

        def dve_gla_step(dve, i):
            h = i - AT_Z
            if 0 <= h < H:
                z, t = LZ[:, h % 2, :], LZ[:, 2 + h % 2, :]
                dve.wait_ge(s_zl, h + 1)
                dve.scalar_tensor_tensor(out=z, in0=z, scalar=0.0, in1=t, op0=ALU.min, op1=ALU.subtract).then_inc(s_zc, 1)
                dve.wait_ge(s_zc, h + 1)
                dve.tensor_tensor_scan(LB[:, h, :], mk("seg"), z, 0.0, ALU.mult, ALU.add).then_inc(s_lb, 1)
            if i == AT_B:
                dve.wait_ge(s_bl, 1)
                dve.wait_ge(s_lb, H)
                dve.tensor_tensor(DEC, EBL[:, 0:32:2], EBL[:, 1:32:2], ALU.mult).then_inc(s_bl, 1)
            h = i - AT_K
            if 0 <= h < H:
                b = LB[:, h, :].rearrange("p (c r) -> p c r", r=HB)
                if h:
                    dve.wait_ge(s_lk, h)
                dve.tensor_tensor(EX[:, 0, :].rearrange("p (c r) -> p c r", r=HB), along(LB[:, h, HB - 1:S:HB], HB), b,
                                  ALU.subtract).then_inc(s_lx, 1)
                dve.wait_ge(s_le, 3 * (h + 1))
                if h >= 2:
                    dve.wait_ge(s_lg, h - 1)
                    dve.wait_ge(s_lap, h - 1)
                dve.tensor_tensor(QT[:, h % 2, :], LQ[:, h, :], EX[:, 1, :], ALU.mult)
                dve.tensor_tensor(KKT[:, h % 2, S:2 * S], LK[:, h, :], EX[:, 2, :], ALU.mult)
                dve.tensor_tensor(LK[:, h, :], LK[:, h, :], EX[:, 0, :], ALU.mult).then_inc(s_lk, 1)
            h = i - AT_KQ - 1
            if 0 <= h < H:
                dve.wait_ge(s_lap, h + 1)
                dve.tensor_tensor(LA[:, h, :, :], tiles(bank[4 + h % 2][:, :]), spread(mk("incl"), NT), ALU.mult
                                  ).then_inc(s_la, 1)
            k = i - AT_V - 1
            if k in (0, 1):
                for n in (2 * k, 2 * k + 1):
                    dve.wait_ge(s_vp, 2 * n + 2)
                    dve.tensor_copy(VTT[:, n, S:2 * S], bank[5 + 2 * n % 4][:, :]).then_inc(s_vv[1], 1)
            n = i - AT_S - 1
            if 0 <= n < NT - 1:
                if n:
                    dve.wait_ge(s_bl, 2)
                    dve.wait_ge(s_lo, n + 1)
                    dve.wait_ge(s_lss, n)
                    link(dve, dve.tensor_tensor(LST, LST, along(DEC[:, n:4 * H:NT], 2 * P), ALU.mult), v_link, vl)
                dve.wait_ge(s_lds, n + 1)
                for a in range(2):
                    src = bank[4 + a][:, :].rearrange("p (h d) -> p h d", h=2)
                    dst = LST[:, 2 * a:2 * a + 2, :]
                    if n == 0:
                        m = dve.tensor_copy(dst, src)
                    else:
                        m = dve.tensor_tensor(dst, dst, src, ALU.add)
                m.then_inc(s_lss, 1)

        block = ctx.enter_context(nc.Block())

        @block.sync
        def _(sp):
            for a in range(2):
                half = slice(a * DB // 2, (a + 1) * DB // 2)
                sp.dma_start(x[:, half, :], in_x[:, half, :]).then_inc(s_x[a], 16)
            sp.dma_start(par[:, :], in_par).then_inc(s_par, 16)

            def flow(c, w, count, peel=0):
                for i in range(peel):
                    load(sp, c + i, in_w[w + i])
                with sp.Fori(0, (count - peel) // SLOTS) as it:
                    for j in range(SLOTS):
                        src = in_w[bass.ds(it * SLOTS + (w + peel + j), 1)].rearrange("a p n -> (a p) n")
                        load(sp, c + peel + j, src, it, SLOTS)

            def flow_out(L):
                with sp.Fori(0, 2) as it:
                    for j in range(12):
                        a = j % 3
                        src = in_fo[bass.ds(it * 4 + (DB * L + j // 3), 1), :, a * D:a * D + OUT_SUB[a] * P]
                        load(sp, C_FOUT[L] + j, src.rearrange("a p n -> (a p) n"), it, 12)

            for i in range(SLOTS):
                load(sp, i, in_w[i])
            sp.dma_start(msk[:, :], in_msk).then_inc(s_msk, 16)
            for t in range(2):
                for g in range(2):
                    sp.dma_start(W1[g * DH:(g + 1) * DH, 4 * t:4 * t + 4, :], in_w1[t]).then_inc(s_w1, 16)
                sp.dma_start(W2[:, t, :], in_w2[t]).then_inc(s_w1, 16)
            for i in range(SLOTS, 7):
                load(sp, i, in_w[i])
            flow(C_HIN + 7, W_HIN + 7, HIN - 7)
            flow(C_HOUT, W_HOUT, OUTB)
            flow(C_F0, W_F0, FIN)
            flow_out(0)
            sp.wait_ge(s_g, FB)
            sp.dma_start(AW2[0:16, :], in_aw2).then_inc(s_aw, 16)
            flow(C_GIN, W_GIN, GIN, 1)
            flow(C_GOUT, W_GOUT, OUTB)
            flow(C_F1, W_F1, FIN)
            flow_out(1)
            for d in range(DB):
                x_updated(sp, 7, d)
                sp.dma_start(out_x[:, d, :], x[:, d, :]).then_inc(s_out, 16)
            sp.wait_ge(s_out, 16 * DB)

        @block.tensor
        def _(pe):
            pe.wait_ge(s_cst, CONSTS)
            pe_sum(pe, 0)
            project(pe, C_HIN, O_HIN, GA, 0)
            pe_compress_in(pe)
            chunk(pe, GA, GA, hh, hl)
            pe_compress_v(pe)
            chunk(pe, GA + 1, GA + 1, hh, hl)
            pe_compress_out(pe)
            chunk(pe, GA + 2, GA + 2, hh, hl)
            chunk(pe, GA + 3, GA + 3, hh, hl)
            pe_cmp(pe)
            pe_attention(pe)
            pe_gdn_prep(pe)
            pe_inverse(pe)
            pe_gdn_scan(pe)
            pe.wait_ge(s_om, NT)
            pe_outproj(pe, C_HOUT, O_HOUT, 1, 0, (4, 5, 6, 7, 0, 1, 2, 3))
            pe_sum(pe, 2)
            pe_ffn(pe, 0)
            pe_sum(pe, 4)
            pe_gla(pe)
            pe_outproj(pe, C_GOUT, O_GOUT, 5, DB)
            pe_sum(pe, 6)
            pe_ffn(pe, 1)

        @block.scalar
        def _(act):
            act.wait_ge(s_cst, CONSTS)
            split_hi(act, 0)
            split_hi(act, 1)
            act_pre(act, 0)
            act_hybrid_in(act)
            act_gates(act)
            act_attention(act)
            act_gdn_prep(act)
            act_inverse(act)
            act_gdn_scan(act)
            act_outproj(act, C_HOUT, O_HOUT)
            act_rstd(act, 1)
            act_pre(act, 2)
            act_ffn(act, 0)
            act_rstd(act, 3)
            act_pre(act, 4)
            act_gla(act)
            act_outproj(act, C_GOUT, O_GOUT)
            act_rstd(act, 5)
            act_pre(act, 6)
            act_ffn(act, 1)
            act_rstd(act, 7)

        @block.gpsimd
        def _(pool):
            pool_gdn(pool)
            pool_post(pool, 1)
            pool_post(pool, 3)
            pool_gla(pool)
            pool_post(pool, 5)
            pool_post(pool, 7)

        @block.vector
        def _(dve):
            dve.memset(ones, 1.0).then_inc(s_cst, 1)
            dve.memset(zero[:, :], 0.0).then_inc(s_cst, 1)
            dve.memset(epsc[:, 0:1], D * EPS).then_inc(s_cst, 1)
            dve.memset(epsc[:, 1:2], EPS).then_inc(s_cst, 1)
            dve.memset(epsc[:, 2:3], P * EPS).then_inc(s_cst, 1)
            dve.memset(epsc[:, 3:4], 2 * P * EPS).then_inc(s_cst, 1)
            dve.memset(onec[:, :], 1.0).then_inc(s_cst, 1)
            dve.wait_ge(s_par, 16)
            dve.tensor_scalar(gain[:, :], pr("gain", 0, 8 * DB), D ** 0.5, None, ALU.mult).then_inc(s_cst, 1)
            dve.tensor_scalar(fcw[:, :], pr("fcw", 0, 2 * FIN * FC), 1 / WS, None, ALU.mult).then_inc(s_cst, 1)
            dve.tensor_scalar(gcw[:, :], pr("gcw", 0, 12 * GC), 1 / WS, None, ALU.mult).then_inc(s_cst, 1)
            dve.tensor_scalar(hon[:, 0:1], pr("gon"), P ** 0.5, None, ALU.mult).then_inc(s_cst, 1)
            dve.tensor_scalar(hon[:, 1:3], pr("lon", 0, 2), (2 * P) ** 0.5, None, ALU.mult).then_inc(s_cst, 1)
            dve.memset(cu[:, 0, 0:1], 0.0).then_inc(s_prod, 1)
            dve.memset(cu[:, 0, 1:2], 0.0).then_inc(s_prod, 1)
            split_lo(dve, 0)
            split_lo(dve, 1)
            dve.wait_ge(s_cst, CONSTS + LATER)
            for a in range(2):
                dve.wait_ge(s_x[a], 16)
            dve_pre(dve, 0)
            dve_hybrid_in(dve)
            dve_cmp(dve)
            dve_attention(dve)
            dve_gdn_prep(dve)
            dve_inverse(dve)
            dve_gdn_scan(dve)
            dve_outproj(dve, C_HOUT)
            dve_post(dve, 1)
            dve_pre(dve, 2)
            dve_ffn(dve, 0)
            dve_post(dve, 3)
            dve_pre(dve, 4)
            dve_gla(dve)
            dve_outproj(dve, C_GOUT)
            dve_post(dve, 5)
            dve_pre(dve, 6)
            dve_ffn(dve, 1)
            dve_post(dve, 7)


def host_layout(i):
    import numpy as np

    i = {k: np.asarray(v) for k, v in i.items()}

    def cols(w):
        k, n = w.shape
        return w.reshape(k // P, P, n // P, P).transpose(2, 1, 0, 3).reshape(n // P, P, k)

    def rows(a):
        return a.reshape(-1, P).T

    w = i["hyb_w_in"][0]
    at = np.cumsum([0, 3 * H * P, H, H, H * P, NH * DH, 6 * 2 * DH, 3 * NH])
    qkv, beta, dec, gate, qb, kv, gb = (w[:, at[j]:at[j + 1]] for j in range(7))
    small = np.zeros((D, P), w.dtype)
    small[:, 0:H], small[:, 32:32 + H], small[:, 64:64 + 3 * NH] = dec, beta, gb
    qb = qb.reshape(D, 2, 4, DH).transpose(0, 2, 1, 3).reshape(D, NH * DH)
    kv = kv.reshape(D, 6, 2 * DH)[:, [0, 1, 2, 4, 3, 5]].reshape(D, 12 * DH)
    hin = np.concatenate([small, qkv, qb, kv, gate], 1)
    g = i["gla_w_in"][0]
    alr = np.zeros((D, P), g.dtype)
    alr[:, 0:16] = g[:, 3 * D:]
    gin = np.concatenate([alr, g[:, 0:3 * D]], 1)

    def pairs(a):
        return a.reshape(a.shape[:-1] + (2, FB, P)).swapaxes(-3, -2).reshape(a.shape)

    fin = pairs(i["ffn_w_in"])
    in_w = np.concatenate([cols(hin), cols(i["hyb_w_out"][0]), cols(fin[0]), cols(gin), cols(i["gla_w_out"][0]), cols(fin[1])])
    in_fo = np.concatenate([cols(i["ffn_w_out"][0]), cols(i["ffn_w_out"][1])])
    par = np.zeros((P, NPAR), np.float32)

    def put(name, a):
        a = a.reshape(a.shape[0], -1)
        par[0:a.shape[0], PARAM[name][0]:PARAM[name][0] + a.shape[1]] = a

    put("gain", rows(i["norm_gains"]))
    put("fcw", rows(pairs(i["ffn_conv_w"]).transpose(1, 0, 2)))
    put("fcb", rows(pairs(i["ffn_conv_b"])))
    put("gcw", i["gdn_conv_w"][0].reshape(GC, 12, P).transpose(2, 1, 0))
    put("alog", i["gdn_A_log"][0][:, None])
    put("dtb", i["gdn_dt_bias"][0][:, None])
    put("gon", rows(i["gdn_o_norm"]))
    put("b1", rows(i["nsa_cmp_b1"]))
    put("pe", np.concatenate([i["nsa_cmp_pe"][0].transpose(2, 0, 1)] * 2))
    put("lon", rows(i["gla_o_norm"]))
    put("lab", rows(i["gla_a_b"]))
    w2 = i["nsa_cmp_w2"][0]
    return {
        "in_x": i["x"][0].T.reshape(DB, P, S).transpose(1, 0, 2),
        "in_par": par, "in_msk": masks(), "in_w": in_w, "in_fo": in_fo,
        "in_w1": i["nsa_cmp_w1"][0].reshape(2, CL, DH, P).transpose(0, 2, 1, 3).reshape(2, DH, 4, 8 * P),
        "in_w2": np.concatenate([w2, w2], 2),
        "in_aw2": i["gla_a_w2"][0],
    }


def masks():
    import numpy as np

    m = np.zeros((P, NMASK), np.float32)

    def put(name, a):
        m[0:a.shape[0], MASKS[name][0]:MASKS[name][1]] = a

    r = np.arange(P)
    put("ident", np.eye(P))
    put("strict", r[:, None] > r[None, :])
    put("incl", r[:, None] <= r[None, :])
    put("lev", np.concatenate([(r[:, None] >> l + 1 == r[None, :] >> l + 1) & (r[:, None] >> l & 1 == 1)
                               & (r[None, :] >> l & 1 == 0) for l in range(7)], 1))
    neg = np.zeros((P, S))
    neg[:, S - P:] = np.where(r[None, :] > r[:, None], NEG, 0.0)
    put("neg", neg)
    put("seg", np.tile(np.arange(S) % DH != 0, (P, 1)))
    t = r[:, None, None] + P * np.arange(NT)[None, :, None]
    c = np.arange(NCP)[None, None, :]
    ok = ((c * CS + CL - 1 <= t) & (c < NC)).reshape(P, -1)
    put("cadd", np.where(ok, 0.0, NEG))
    put("c01", ok)
    put("sel", np.kron(np.eye(H), np.ones((1, P))))
    return m


def kernel(**inputs):
    import numpy as np
    import concourse.bacc as bacc
    from concourse.bass_utils import run_bass_kernel_spmd

    nc = bacc.Bacc("TRN2", target_bir_lowering=False, num_devices=1)
    arrays = {k: np.ascontiguousarray(a) for k, a in host_layout(inputs).items()}
    aps = {k: nc.dram_tensor(k, a.shape, mybir.dt.from_np(a.dtype), kind="ExternalInput").ap() for k, a in arrays.items()}
    out = nc.dram_tensor("out_x", (P, DB, S), F32, kind="ExternalOutput").ap()
    build(nc, out, **aps)
    r = run_bass_kernel_spmd(nc, [arrays], core_ids=[0])
    o = np.asarray(r.results[0]["out_x"])
    return o.transpose(2, 1, 0).reshape(1, S, D)
```

```python
from contextlib import ExitStack

import concourse.bass as bass
from concourse import mybir

F32 = mybir.dt.float32
F16 = mybir.dt.float16
ALU = mybir.AluOpType
ACT = mybir.ActivationFunctionType
AX_X = mybir.AxisListType.X

P = 128
D = 1024
S = 512
DB = D // P
NT = S // P
EPS = 1e-6
NEG = -1e30
WS = 16.0
SLOTS = 4
LEAD = 3

H = 4
GC = 4
NH = 8
DH = 64
NC = 31
NCP = 32
CL, CS = 32, 16

DFF = 2816
FB = DFF // P
FC = 3
OUT_SUB = (8, 8, 6)

HIN, OUTB, FIN, GIN = 27, DB, 2 * FB, 25
C_HIN, O_HIN = 0, 0
C_HOUT, O_HOUT = C_HIN + HIN, O_HIN + HIN
C_F0, O_F0 = C_HOUT + OUTB, O_HOUT + OUTB
C_FO0, O_FO0 = C_F0 + FIN, O_F0 + FIN
C_GIN, O_GIN = C_FO0 + 3 * OUTB, O_FO0 + OUTB
C_GOUT, O_GOUT = C_GIN + GIN, O_GIN + GIN
C_F1, O_F1 = C_GOUT + OUTB, O_GOUT + OUTB
C_FO1, O_FO1 = C_F1 + FIN, O_F1 + FIN
C_END = C_FO1 + 3 * OUTB
C_FIN, O_FIN = (C_F0, C_F1), (O_F0, O_F1)
C_FOUT, O_FOUT = (C_FO0, C_FO1), (O_FO0, O_FO1)

W_HIN, W_HOUT, W_F0 = 0, HIN, HIN + OUTB
W_GIN = W_F0 + FIN
W_GOUT = W_GIN + GIN
W_F1 = W_GOUT + OUTB
W_FIN = (W_F0, W_F1)

ROWS, QKV, KC, VC, GA, QB, KSW, VSW = 0, 1, 13, 14, 15, 19, 23, 25
ALR, GQ, GK, GV, GR = 0, 1, 5, 9, 17

PARAM = {}
_at = 0
for _n, _w in (("gain", 8 * DB), ("fcw", 2 * FIN * FC), ("fcb", 2 * FIN), ("gcw", 12 * GC), ("alog", 1), ("dtb", 1),
               ("gon", 1), ("b1", 2), ("pe", 2 * CL), ("lon", 2), ("lab", 4)):
    PARAM[_n] = (_at, _at + _w)
    _at += _w
NPAR = _at

MASKS = {}
_at = 0
for _n, _w in (("ident", P), ("strict", P), ("incl", P), ("lev", 7 * P), ("neg", S), ("seg", S),
               ("cadd", NT * NCP), ("c01", NT * NCP), ("sel", H * P)):
    MASKS[_n] = (_at, _at + _w)
    _at += _w
NMASK = _at


def build(nc, out_x, in_x, in_par, in_msk, in_w, in_fo, in_w1, in_w2, in_aw2):
    with ExitStack() as ctx:
        def sb(name, shape, dt=F32):
            return ctx.enter_context(nc.sbuf_tensor(name, shape, dt))

        def sem(name):
            return ctx.enter_context(nc.semaphore(name))

        bank = [ctx.enter_context(nc.psum_tensor(f"bank{i}", [P, S], F32)) for i in range(8)]

        x = sb("x", [P, DB, S])
        hh = sb("hh", [P, DB, S], F16)
        hl = sb("hl", [P, DB, S], F16)
        raw = sb("raw", [P, SLOTS, D])
        whi = sb("whi", [P, SLOTS, D], F16)
        wlo = sb("wlo", [P, SLOTS, D], F16)
        par = sb("par", [P, NPAR])
        msk = sb("msk", [P, NMASK])
        gain = sb("gain", [P, 8 * DB])
        fcw = sb("fcw", [P, 2 * FIN * FC])
        gcw = sb("gcw", [P, 12 * GC])
        hon = sb("hon", [P, 3])
        hf = sb("hf", [P, 2, S])
        rln = sb("rln", [P, S])
        rstd = sb("rstd", [P, S])
        epsc = sb("epsc", [P, 4])
        onec = sb("onec", [P, 1])
        CONSTS = 6
        LATER = 5
        XP = 4
        ARENA = 29472
        arena = sb("arena", [P, ARENA])

        def pr(name, i=0, n=1):
            a = PARAM[name][0] + i
            return par[:, a:a + n]

        def mk(name):
            return msk[:, MASKS[name][0]:MASKS[name][1]]

        ident = mk("ident")
        ones = sb("ones", [P, P])[:, :]

        def view(at, *dims):
            n = 1
            for d in dims:
                n *= d
            assert at + n <= ARENA, (at, n)
            v = arena[:, at:at + n]
            if len(dims) == 1:
                return v
            if len(dims) == 2:
                return v.rearrange("p (a b) -> p a b", b=dims[1])
            return v.rearrange("p (a b c) -> p a b c", b=dims[1], c=dims[2])

        y = view(0, DB, S)
        sq = view(4096, DB, S)
        sqa = view(22016, S)
        gh = view(8192, FB * S // 2).bitcast(F16).rearrange("p (f s) -> p f s", s=S)
        gl = view(8192 + FB * S // 2, FB * S // 2).bitcast(F16).rearrange("p (f s) -> p f s", s=S)
        cu = view(19456, 4, S)
        gf = view(21504, S)

        QKVS = view(0, 12, S)
        AK = view(6144, H, NT, P)
        AQ = view(8192, H, NT, P)
        TT = view(10240, H, NT, P)
        UU = view(12288, H, NT, P)
        XX = view(14336, H, NT, P)
        BM = view(16384, H, NT, P)
        GB = view(18432, H, S)
        EE = view(20480, 2, S)
        GAT = view(22016, H, S)
        QBP = view(24064, 4 * S).bitcast(F16).rearrange("p (l h s) -> p l h s", l=2, s=S)
        KSP = view(26112, 2 * S).bitcast(F16).rearrange("p (l b s) -> p l b s", l=2, s=S)
        VTP = view(27136, 2 * S).bitcast(F16).rearrange("p (l b n c) -> p l b n c", l=2, b=2, c=P)
        KD = view(24064, H, NT, P)
        VBD = view(28160, 2, 4 * DH)
        KCM = view(28672, NCP).bitcast(F16).rearrange("p (l c) -> p l c", l=2)
        SIG = view(28704, NT, 64)
        G = view(28960, S)[0:H]
        ROWT = view(28960, S)
        SQT = view(6144, 2, S)
        GZ = view(7168, 2, S)[0:H]
        BLKP = view(6144, 2 * CL * NC).bitcast(F16).rearrange("p (l t m) -> p l t m", l=2, t=2)
        BLK = view(18944, 2, CL, NC)
        HS = view(8192, 2, 2, NCP)
        KCF = view(8448, 2, S)
        VF = view(20992, 2, S)
        W1 = view(10496, 2 * CL // 8, 8 * P)
        W1P = view(9472, 2 * CL // 8 * 8 * P).bitcast(F16).rearrange("p (k l m) -> p k l m", l=2, m=8 * P)
        W2 = view(18688, 2, P)
        SM = view(10496, 2, S)
        PP = view(11520, 3, S)
        PTP = view(13056, 3 * S).bitcast(F16).rearrange("p (l u s) -> p l u s", l=2, s=S)
        ACC = view(14592, NT, S)
        TMP = view(16640, S)
        CSC = view(17152, NT, NH * NCP)
        CPT = view(13056, NT, 2 * P)
        US, WT, OA = AK, XX, TT
        VN, SS, SD = BM[:, 0], BM[:, 1], BM[:, 2]

        small = sb("small", [P, 512])
        GT, BT, GLB, EGT, BEG, EKD, EGL = (small[:, 16 * i:16 * i + 16] for i in range(7))
        NMX = small[:, 112:114]
        LS = small[:, 128:144]
        RC = small[:, 144:152]
        CMX, CLS, CRC = small[:, 160:192], small[:, 192:224], small[:, 224:256]
        NA = small[:, 256:257]
        EBL = small[:, 288:320]
        DEC = small[:, 320:336]

        LQ = view(0, H, S)
        LK = view(2048, H, S)
        VTT = view(4096, NT, D)
        RS = view(8192, DB, S)
        LB = view(12288, H, S)
        SQO = view(12288, DB, S)
        KDT = view(14336, H, NT, P)
        LA = view(16384, H, NT, P)
        KKT = view(18432, 2, 1024)
        EX = view(20736, 3, S)
        QT = view(22272, 2, S)
        OO = view(23296, DB, S)
        VFF = OO
        LST = view(27392, H, 2 * P)
        ALRS = view(28416, S)
        LZ = view(18432, 4, S)
        AW2 = view(28928, S)

        s_par = sem("params_loaded")
        s_x = [sem(f"x_loaded{i}") for i in range(XP)]
        s_msk = sem("masks_loaded")
        s_w1 = sem("cmp_weights_loaded")
        s_aw = sem("gla_weights_loaded")
        s_cst = sem("constants_ready")
        w_dma = [sem(f"chunk_loaded{i}") for i in range(SLOTS)]
        w_hi = sem("chunk_high_ready")
        w_lo = sem("chunk_low_ready")
        w_used = sem("chunk_used")
        b_free = [sem(f"bank_read{i}") for i in range(SLOTS)]
        s_sq = sem("square_ready")
        s_sa = sem("squares_accumulated")
        s_sum = sem("sum_of_squares_ready")
        s_ln = sem("log_ready")
        s_rstd = sem("rstd_ready")
        s_yn = sem("y_normed")
        s_xr = [sem("x_updated_odd"), sem("x_updated_even")]
        s_hf = sem("h32_ready")
        s_hh = sem("h_high_ready")
        s_h = sem("h_ready")
        s_cv = sem("conv_started")
        s_c1 = sem("conv_stepped")
        s_silu = sem("gate_silu_ready")
        s_prod = sem("products_ready")
        s_gh = sem("g_high_ready")
        s_g = sem("g_ready")
        s_out = sem("output_stored")
        s_om = sem("mixer_output_ready")
        s_omh = sem("mixer_output_high_ready")
        v_link = sem("vector_step")
        a_link = sem("scalar_step")
        g_link = sem("pool_step")
        (s_qs, s_blk, s_hid, s_hs, s_kv, s_kcm, s_vt, s_vtk, s_rt, s_se, s_sg, s_cs, s_cm, s_ce, s_cp, s_ct, s_cpt,
         s_co, s_ca, s_s, s_m, s_e, s_t, s_pc, s_pv, s_cb, s_acc, s_at, s_qh, s_vh, s_kch, s_pl, s_wh, s_wl, s_bh16, s_bl16,
         s_clr, s_mk, s_gbr) = (sem(n) for n in (
             "qkv_ready", "cmp_blocks_ready", "cmp_hidden_summed", "cmp_hidden_ready", "cmp_kv_summed", "cmp_kv_ready",
             "v_transposed", "v_tokens_ready", "rows_transposed", "gate_exp_ready", "gates_ready",
             "cmp_scores", "cmp_scores_masked", "cmp_exp_ready", "cmp_probs_ready", "cmp_probs_transposed",
             "cmp_probs_t_ready", "cmp_out_summed", "cmp_out_ready", "scores_summed", "scores_masked", "probs_ready",
             "probs_transposed", "probs_t_ready", "pv_summed", "attention_bank_read",
             "attention_ready", "attention_transposed", "nsa_operand_high_ready", "v_tokens_high_ready", "cmp_k_high_ready",
             "probs_t_low_ready", "cmp_w1_high_ready", "cmp_w1_low_ready", "cmp_blocks_high_ready",
             "cmp_blocks_low_ready", "cleared",
             "cmp_scores_read", "decay_row_ready"))
        (s_ga, s_gg, s_gtr, s_gt, s_ge, s_gk, s_nq, s_ns, s_nl, s_nr, s_nn, s_gb, s_dd, s_d, s_ex, s_eg, s_e1,
         s_e2, s_qg, s_kk, s_qk, s_kt, s_vr, s_ak, s_aq, s_kd, s_bv) = (sem(n) for n in (
             "decay_exp_ready", "decays_cumulated", "decay_columns_summed", "decay_columns_ready",
             "decay_exps_ready", "decay_products_ready", "qk_square_ready", "qk_sum_ready", "qk_log_ready",
             "qk_rstd_ready", "qk_normed", "decay_row_spread", "decay_differences_ready", "decay_row_read",
             "decay_pair_exp_ready", "decay_row_exp_ready", "kk_decay_ready", "qk_decay_ready", "q_decayed",
             "kk_summed", "qk_summed", "k_transposed", "v_heads_transposed", "kk_ready", "qk_t_ready",
             "k_tokens_ready", "v_beta_ready"))
        (s_b, s_tt, s_ut, s_uu, s_xp, s_xx, s_zu, s_zt, s_u, s_w, s_us, s_wt, s_p2, s_vn, s_oo, s_ds, s_ss, s_oa,
         s_hq, s_hsum, s_hln, s_hr, s_on) = (sem(n) for n in (
             "level_blocks_ready", "inverse_ready", "inverse_transposed", "inverse_t_ready", "x_summed", "x_ready",
             "u_update_summed", "t_update_summed", "u_summed", "w_summed", "u_ready", "w_ready", "old_value_summed",
             "new_value_ready", "head_out_summed", "state_update_summed", "state_ready", "head_out_ready",
             "head_square_ready", "head_sum_ready", "head_log_ready", "head_rstd_ready", "head_out_gated"))
        (s_z, s_zl, s_zc, s_lb, s_bl, s_lx, s_le, s_lk, s_lg, s_lap, s_la, s_kp, s_kdt, s_vp, s_lo, s_lds,
         s_lss, s_loo, s_lm, s_og) = (sem(n) for n in (
             "decay_logit_summed", "decay_log_ready", "decay_log_joined", "log_decays_cumulated", "chunk_decays_ready",
             "decay_to_end_ready", "gla_exps_ready", "gla_k_ready", "gla_decayed", "gla_kq_summed", "gla_kq_ready",
             "gla_k_transposed", "gla_k_tokens_ready", "gla_v_transposed", "gla_out_summed",
             "gla_state_summed", "gla_state_ready", "gla_out_ready", "gla_k_mixed_ready", "gla_out_gated"))
        s_vv = [sem(f"gla_v_tokens_ready{i}") for i in range(2)]

        vl, al, gl_ = [0], [0], [0]
        PASSES = ((0, 0), (0, 1), (1, 0))

        def link(eng, ins, signal, at):
            ins.then_inc(signal, 1)
            at[0] += 1
            eng.wait_ge(signal, at[0])

        def tiles(a):
            return a.rearrange("p (n c) -> p n c", c=P)

        def spread(a, n):
            return a.unsqueeze(1).to_broadcast([a.shape[0], n, a.shape[1]])

        def along(a, n):
            return a.unsqueeze(2).to_broadcast([a.shape[0], a.shape[1], n])

        def kb_of(c):
            for a in C_FOUT:
                if a <= c < a + 3 * OUTB:
                    return OUT_SUB[(c - a) % 3]
            return DB

        def load(sp, c, src, it=0, n=0):
            if c >= SLOTS:
                sp.wait_ge(w_lo, it * n + (c - SLOTS + 1))
            sp.dma_start(raw[:, c % SLOTS, 0:kb_of(c) * P], src).then_inc(w_dma[c % SLOTS], 16)

        def split_hi(act, c, it=0, n=0):
            if c >= C_END:
                return
            act.wait_ge(w_dma[c % SLOTS], it * (n // SLOTS * 16) + 16 * (c // SLOTS + 1))
            if c >= SLOTS:
                act.wait_ge(w_used, it * n + (c - SLOTS + 1))
            act.activation(whi[:, c % SLOTS, :], raw[:, c % SLOTS, :], ACT.Copy, scale=WS).then_inc(w_hi, 1)

        def split_lo(dve, c, it=0, n=0):
            if c >= C_END:
                return
            dve.wait_ge(w_hi, it * n + (c + 1))
            dve.scalar_tensor_tensor(out=wlo[:, c % SLOTS, :], in0=raw[:, c % SLOTS, :], scalar=WS,
                                     in1=whi[:, c % SLOTS, :], op0=ALU.mult, op1=ALU.subtract).then_inc(w_lo, 1)

        def chunk(pe, c, o, mh, ml, k0=0, first=True, last=True, it=0, n=0):
            pe.wait_ge(w_lo, it * n + (c + 1))
            if first and o >= SLOTS:
                no = n if kb_of(c) == DB and n != 12 else 4
                pe.wait_ge(b_free[o % SLOTS], it * (no // SLOTS) + o // SLOTS)
            s, nk = c % SLOTS, kb_of(c)
            for k in range(nk):
                wh, wl = whi[:, s, k * P:(k + 1) * P], wlo[:, s, k * P:(k + 1) * P]
                pe.matmul(bank[o % SLOTS][:, :], wh, mh[:, k0 + k, :], start=(first and k == 0), stop=False)
                pe.matmul(bank[o % SLOTS][:, :], wh, ml[:, k0 + k, :], start=False, stop=False)
                m = pe.matmul(bank[o % SLOTS][:, :], wl, mh[:, k0 + k, :], start=False, stop=(last and k == nk - 1))
            m.then_inc(w_used, 1)

        def two_start(pe, c, o):
            pe.wait_ge(w_lo, c + 2)
            for j in range(2):
                if o + j >= SLOTS:
                    pe.wait_ge(b_free[(o + j) % SLOTS], (o + j) // SLOTS)

        def two_block(pe, c, o, k, first, last, t=slice(0, S), done=True):
            for j in range(2):
                out, s = bank[(o + j) % SLOTS][:, t], (c + j) % SLOTS
                wh, wl = whi[:, s, k * P:(k + 1) * P], wlo[:, s, k * P:(k + 1) * P]
                pe.matmul(out, wh, hh[:, k, t], start=first, stop=False)
                pe.matmul(out, wh, hl[:, k, t], start=False, stop=False)
                m = pe.matmul(out, wl, hh[:, k, t], start=False, stop=last)
                if last and done:
                    m.then_inc(w_used, 1)

        def first_two(pe, c, o, e):
            two_start(pe, c, o)
            for a in range(2):
                for k in range(DB):
                    pe.wait_ge(s_h, 2 * DB * (e // 2) + DB * a + k + 1)
                    two_block(pe, c, o, k, k == 0, k == DB - 1, half(a), a == 1)

        def project(pe, c, o, count, e):
            first_two(pe, c, o, e)
            peel = 2 + (count - 2) % SLOTS
            for i in range(2, peel):
                chunk(pe, c + i, o + i, hh, hl)
            with pe.Fori(0, (count - peel) // SLOTS) as it:
                for j in range(SLOTS):
                    chunk(pe, c + peel + j, o + peel + j, hh, hl, it=it, n=SLOTS)

        def pe_outproj(pe, c, o, e):
            for d in range(2, DB):
                chunk(pe, c + d, o + d, hh, hl)
            pe_sum_all(pe, e)

        def summed(eng, c, it=0, n=0):
            eng.wait_ge(w_used, it * n + (c + 1))

        def was_read(eng, o, it=0, n=0):
            eng.wait_ge(b_free[o % SLOTS], it * (n // SLOTS) + (o // SLOTS + 1))

        HALF = S // 2

        def half(a):
            return slice(a * HALF, (a + 1) * HALF)

        def squares(e):
            return DB * e + DB * (max(e - 1, 0) // 2)

        def accumulated(e):
            return (DB + 1) * ((e + 1) // 2 + 1)

        def pe_sum_all(pe, e):
            if e:
                pe.wait_ge(s_ln, 2 * e)
            pe.wait_ge(s_sa, accumulated(e))
            for a in range(2):
                pe.matmul(bank[4 + a][:, 0:HALF], ones, sqa[:, half(a)], start=True, stop=True).then_inc(s_sum, 1)

        def dve_sum_start(dve, e):
            dve.memset(sqa, 0.0).then_inc(s_sa, 1)

        def dve_sum_block(dve, e, d, it=0, n=0):
            at = bass.ds(it * n + d, 1) if n else slice(d, d + 1)
            dve.wait_ge(s_sq, it * n + (squares(e) + d + 1))
            dve.wait_ge(s_sa, it * n + (accumulated(e) - DB + d))
            out = sqa.unsqueeze(1)
            dve.tensor_tensor(out, out, sq[:, at, :], ALU.add).then_inc(s_sa, 1)

        def pe_sum(pe, e):
            for a in range(2):
                pe.wait_ge(s_ln, 2 * (e - 1) + a + 1)
                for d in range(DB):
                    pe.wait_ge(s_sq, squares(e) + DB * a + d + 1)
                    m = pe.matmul(bank[4 + a][:, 0:HALF], ones, sq[:, d, half(a)], start=(d == 0), stop=(d == DB - 1))
                m.then_inc(s_sum, 1)

        def act_rstd(act, e, a):
            act.wait_ge(s_sum, 2 * e + a + 1)
            act.activation(rln[:, half(a)], bank[4 + a][:, 0:HALF], ACT.Ln, bias=epsc[:, 0:1]).then_inc(s_ln, 1)
            act.wait_ge(s_ln, 2 * e + a + 1)
            act.activation(rstd[:, half(a)], rln[:, half(a)], ACT.Exp, scale=-0.5).then_inc(s_rstd, 1)

        def act_post(act, e):
            act.preload_act_table_set("natural_log_exp_and_others")
            act_rstd(act, e, 0)
            act_rstd(act, e, 1)

        def act_pre(act, e):
            if e == 0:
                act.preload_act_table_set("natural_log_exp_and_others")
                for d in range(DB):
                    act.wait_ge(s_x[XP * d // DB], 16)
                    act.activation(sq[:, d, :], x[:, d, :], ACT.Square).then_inc(s_sq, 1)
                for c in range(LEAD):
                    split_hi(act, c)
                act_rstd(act, e, 0)
            else:
                for a in range(2):
                    for d in range(DB):
                        x_updated(act, e - 1, d, a)
                        act.activation(sq[:, d, half(a)], x[:, d, half(a)], ACT.Square).then_inc(s_sq, 1)
                        if a == 1 and d == 2:
                            act_rstd(act, e, 0)
            act_rstd(act, e, 1)
            base = 2 * DB * (e // 2)
            for a in range(2):
                for d in range(DB):
                    act.wait_ge(s_hf, base + DB * a + d + 1)
                    act.activation(hh[:, d, half(a)], hf[:, d % 2, half(a)], ACT.Copy).then_inc(s_hh, 1)

        def dve_pre(dve, e):
            base = 2 * DB * (e // 2)

            def low(a, d):
                dve.wait_ge(s_hh, base + DB * a + d + 1)
                dve.tensor_tensor(hl[:, d, half(a)], hf[:, d % 2, half(a)], hh[:, d, half(a)], ALU.subtract).then_inc(s_h, 1)

            for a in range(2):
                dve.wait_ge(s_rstd, 2 * e + a + 1)
                for d in range(DB):
                    if d >= 2:
                        dve.wait_ge(s_h, base + DB * a + d - 1)
                    dve.scalar_tensor_tensor(out=hf[:, d % 2, half(a)], in0=x[:, d, half(a)],
                                             scalar=gain[:, e * DB + d:e * DB + d + 1], in1=rstd[:, half(a)],
                                             op0=ALU.mult, op1=ALU.mult).then_inc(s_hf, 1)
                    if d:
                        low(a, d - 1)
                low(a, DB - 1)

        def x_updated(eng, e, d, a):
            eng.wait_ge(s_xr[1 - d % 2], DB * (e // 2) + DB // 2 * a + d // 2 + 1)

        def dve_post(dve, e):
            base = 2 * DB * (e // 2)
            for a in range(2):
                dve.wait_ge(s_rstd, 2 * e + a + 1)
                for d in range(DB):
                    dve.scalar_tensor_tensor(out=y[:, d, half(a)], in0=y[:, d, half(a)],
                                             scalar=gain[:, e * DB + d:e * DB + d + 1], in1=rstd[:, half(a)],
                                             op0=ALU.mult, op1=ALU.mult).then_inc(s_yn, 1)
                    if d % 2:
                        dve.wait_ge(s_yn, base + DB * a + d + 1)
                        dve.tensor_tensor(x[:, d, half(a)], x[:, d, half(a)], y[:, d, half(a)], ALU.add).then_inc(s_xr[0], 1)

        def pool_post(pool, e):
            for a in range(2):
                for d in range(0, DB, 2):
                    pool.wait_ge(s_yn, 2 * DB * (e // 2) + DB * a + d + 1)
                    pool.tensor_tensor(x[:, d, half(a)], x[:, d, half(a)], y[:, d, half(a)], ALU.add).then_inc(s_xr[1], 1)

        def act_output(act, c, o, d, it=0, nc_=0, no=0):
            summed(act, c, it, nc_)
            at = bass.ds(it * no + d, 1)
            src = bank[o % SLOTS][:, :].unsqueeze(1)
            act.activation(sq[:, at, :], src, ACT.Square, scale=1 / WS).then_inc(s_sq, 1)
            act.activation(y[:, at, :], src, ACT.Copy, scale=1 / WS).then_inc(b_free[o % SLOTS], 1)

        def act_outproj(act, c, o):
            with act.Fori(0, DB // SLOTS) as it:
                for j in range(SLOTS):
                    split_hi(act, c + j + LEAD, it, SLOTS)
                    act_output(act, c + j, o + j, j, it, SLOTS, SLOTS)

        def dve_outproj(dve, c, e):
            dve.wait_ge(s_om, DB * (e // 4 + 1))
            dve_sum_start(dve, e)
            with dve.Fori(0, DB // SLOTS) as it:
                for j in range(SLOTS):
                    split_lo(dve, c + j + LEAD, it, SLOTS)
                    dve_sum_block(dve, e, j, it, SLOTS)

        def pe_ffn(pe, L):
            e = 4 * L + 3
            project(pe, C_FIN[L], O_FIN[L], FIN, e - 1)
            with pe.Fori(0, 2) as it:
                for j in range(SLOTS):
                    for u in range(3):
                        if j == 0:
                            pe.wait_ge(s_g, FB * L + min(8 * (u + 1), FB))
                        chunk(pe, C_FOUT[L] + 3 * j + u, O_FOUT[L] + j, gh, gl, 8 * u, u == 0, u == 2, it, 12)
            pe_sum_all(pe, e)

        def act_ffn(act, L):
            act.preload_act_table_set("silu_and_others")
            c0, o0 = C_FIN[L], O_FIN[L]
            with act.Fori(0, FIN // SLOTS) as it:
                for j in range(SLOTS):
                    split_hi(act, c0 + j + LEAD, it, SLOTS)
                    summed(act, c0 + j, it, SLOTS)
                    if j % 2 == 0:
                        act.wait_ge(s_prod, it * 2 + (FB * L + j // 2 + 1))
                    k = it * SLOTS + (L * FIN + j)
                    act.activation(cu[:, j, :], bank[(o0 + j) % SLOTS][:, :], ACT.Identity,
                                   scale=fcw[:, bass.ds(k + 2 * 2 * FIN, 1)], bias=par[:, bass.ds(k + PARAM["fcb"][0], 1)]
                                   ).then_inc(s_cv, 1)
                    if j % 2 == 0:
                        was_read(act, o0 + j, it, SLOTS)
                        act.activation(cu[:, j, :], cu[:, j, :], ACT.Silu).then_inc(s_silu, 1)
            if L == 0:
                with act.Fori(0, 2) as it:
                    act_ffn_out(act, L, it)
            else:
                for it in range(2):
                    act_ffn_out(act, L, it)

        def act_ffn_out(act, L, it):
            for j in range(12):
                c = C_FOUT[L] + j
                if L == 0:
                    split_hi(act, c + LEAD, it, 12)
                else:
                    split_hi(act, c + LEAD + 12 * it)
                if j % 3 == 2:
                    act_output(act, c, O_FOUT[L] + j // 3, j // 3, it, 12, 4)

        def dve_ffn(dve, L):
            c0, o0 = C_FIN[L], O_FIN[L]
            with dve.Fori(0, FIN // SLOTS) as it:
                for j in range(SLOTS):
                    split_lo(dve, c0 + j + LEAD, it, SLOTS)
                    k = it * SLOTS + (L * FIN + j)
                    b = bank[(o0 + j) % SLOTS]
                    dve.wait_ge(s_cv, it * SLOTS + (12 + L * FIN + j + 1))
                    dve.scalar_tensor_tensor(out=cu[:, j, 1:S], in0=b[:, 0:S - 1],
                                             scalar=fcw[:, bass.ds(k + 2 * FIN, 1)], in1=cu[:, j, 1:S],
                                             op0=ALU.mult, op1=ALU.add).then_inc(s_c1, 1)
                    dve.wait_ge(s_c1, it * SLOTS + (24 + L * FIN + j + 1))
                    dve.scalar_tensor_tensor(out=cu[:, j, 2:S], in0=b[:, 0:S - 2],
                                             scalar=fcw[:, bass.ds(k, 1)], in1=cu[:, j, 2:S],
                                             op0=ALU.mult, op1=ALU.add).then_inc(b_free[(o0 + j) % SLOTS], 1)
                    if j % 2:
                        p = it * 2 + (FB * L + j // 2 + 1)
                        at = bass.ds(it * 2 + j // 2, 1)
                        g32 = gf.unsqueeze(1)
                        dve.wait_ge(s_silu, p)
                        was_read(dve, o0 + j, it, SLOTS)
                        dve.tensor_tensor(gf, cu[:, j - 1, :], cu[:, j, :], ALU.mult).then_inc(s_prod, 1)
                        dve.wait_ge(s_prod, p + 2)
                        dve.tensor_copy(gh[:, at, :], g32).then_inc(s_gh, 1)
                        dve.wait_ge(s_gh, p)
                        dve.tensor_tensor(gl[:, at, :], g32, gh[:, at, :], ALU.subtract).then_inc(s_g, 1)
            e = 4 * L + 3
            dve_sum_start(dve, e)
            if L == 0:
                with dve.Fori(0, 2) as it:
                    for j in range(12):
                        split_lo(dve, C_FOUT[L] + j + LEAD, it, 12)
                        if j % 3 == 2:
                            dve_sum_block(dve, e, j // 3, it, SLOTS)
            else:
                for j in range(3 * DB):
                    split_lo(dve, C_FOUT[L] + j + LEAD)
                    if j % 3 == 2:
                        dve_sum_block(dve, e, j // 3)

        def act_hybrid_in(act):
            act.preload_act_table_set("silu_and_others")

            def silu(i):
                was_read(act, O_HIN + QKV + i)
                act.activation(QKVS[:, i, :], QKVS[:, i, :], ACT.Silu).then_inc(s_qs, 1)

            def leave(o, out, func=ACT.Copy, scale=1 / WS):
                act.activation(out, bank[o % SLOTS][:, :], func, scale=scale).then_inc(b_free[o % SLOTS], 1)

            def high(o, out):
                act.activation(out, bank[o % SLOTS][:, :], ACT.Copy, scale=1 / WS).then_inc(s_qh, 1)

            for o in range(HIN):
                split_hi(act, o + LEAD)
                act_compress(act, o)
                act_early(act, o)
                summed(act, o)
                if o == ROWS:
                    leave(o, ROWT)
                elif o < KC:
                    i = o - QKV
                    act.activation(QKVS[:, i, :], bank[o % SLOTS][:, :], ACT.Identity,
                                   scale=gcw[:, i * GC + 3:i * GC + 4]).then_inc(s_cv, 1)
                    if i:
                        silu(i - 1)
                elif o < GA:
                    if o == KC:
                        silu(11)
                    leave(o, KCF[:, o - KC, :])
                elif o < QB:
                    leave(o, GAT[:, o - GA, :], ACT.Silu)
                elif o < KSW:
                    high(o, QBP[:, 0, o - QB, :])
                elif o < VSW:
                    high(o, KSP[:, 0, o - KSW, :])
                else:
                    leave(o, VF[:, o - VSW, :])
            for b in range(2):
                act.wait_ge(s_vt, b + 1)
                act.activation(VTP[:, 0, b, :, :], tiles(bank[6 + b][:, :]), ACT.Copy).then_inc(s_vh, 1)
            for h in range(H):
                act.wait_ge(s_gb, h + 1)
                act.activation(GB[:, h, :], bank[h % 2][:, :], ACT.Copy).then_inc(s_gbr, 1)

        def dve_hybrid_in(dve):
            for o in range(HIN):
                split_lo(dve, o + LEAD)
                dve_early(dve, o)
                dve_compress(dve, o)
                if QKV <= o < KC:
                    i = o - QKV
                    dve.wait_ge(s_cv, i + 1)
                    for t in (1, 2, 3):
                        m = dve.scalar_tensor_tensor(
                            out=QKVS[:, i, t:S], in0=bank[o % SLOTS][:, 0:S - t], scalar=gcw[:, i * GC + 3 - t:i * GC + 4 - t],
                            in1=QKVS[:, i, t:S], op0=ALU.mult, op1=ALU.add)
                        if t < 3:
                            m.then_inc(s_c1, 1)
                            dve.wait_ge(s_c1, 2 * i + t)
                    m.then_inc(b_free[o % SLOTS], 1)
                elif QB <= o < VSW:
                    i, pair = (o - QB, QBP) if o < KSW else (o - KSW, KSP)
                    dve.wait_ge(s_qh, o - QB + 1)
                    dve.scalar_tensor_tensor(out=pair[:, 1, i, :], in0=bank[o % SLOTS][:, :], scalar=1 / WS,
                                             in1=pair[:, 0, i, :], op0=ALU.mult, op1=ALU.subtract
                                             ).then_inc(b_free[o % SLOTS], 1)
                if S_AT <= o < S_AT + 2:
                    dve_cmp_mask(dve, o - S_AT)
                if o == QB:
                    was_read(dve, O_HIN + QB - 1)
                    dve.tensor_scalar(GAT, GAT, hon[:, 0:1], None, ALU.mult).then_inc(s_gg, 1)
            dve_cmp_probs(dve)

        W1_AT, BLK_AT = 5, VC + 1
        H_AT = GA + 3
        N_AT = QB - 1
        G_AT = QB
        S_AT = VSW - 1

        def pe_early(pe, o):
            if o == G_AT:
                pe.wait_ge(s_msk, 16)
                was_read(pe, O_HIN + ROWS)
                pe.wait_ge(s_hs, 4)
                for n in range(NT):
                    m = pe.transpose(bank[4][:, n * P:(n + 1) * P], ROWT[:, n * P:(n + 1) * P], ident)
                m.then_inc(s_rt, 1)
            i = o - N_AT - 1
            if 0 <= i < 8:
                pe.wait_ge(s_nq, i + 1)
                if i >= 2:
                    pe.wait_ge(s_nl, i - 1)
                pe.matmul(bank[6 + i % 2][:, :], ones, SQT[:, i % 2, :], start=True, stop=True).then_inc(s_ns, 1)
            if o == G_AT + 5:
                pe.wait_ge(s_kcm, 6)
                for n in range(NT):
                    pe.wait_ge(s_gg, n + 2)
                    pe.transpose(bank[5][:, n * H:(n + 1) * H], G[:, n * P:(n + 1) * P], ident[0:H, 0:H])
                for h in range(H):
                    m = pe.matmul(bank[5][:, 16 + h * NT:16 + (h + 1) * NT], mk("sel")[0:H, h * P:(h + 1) * P],
                                  G[:, P - 1:S:P], start=True, stop=True)
                m.then_inc(s_gtr, 1)

        def act_early(act, o):
            i = o - N_AT
            if 0 <= i < 8:
                act.wait_ge(s_qs, i + 1)
                if i >= 2:
                    act.wait_ge(s_ns, i - 1)
                act.activation(SQT[:, i % 2, :], QKVS[:, i, :], ACT.Square).then_inc(s_nq, 1)
            i = o - N_AT - 1
            if i == 0:
                act.preload_act_table_set("natural_log_exp_and_others")
            if 0 <= i < 8:
                act.wait_ge(s_ns, i + 1)
                if i >= 2:
                    act.wait_ge(s_nn, i - 1)
                act.activation(hf[:, i % 2, :], bank[6 + i % 2][:, :], ACT.Ln, bias=epsc[:, 1:2]).then_inc(s_nl, 1)
                act.wait_ge(s_nl, i + 1)
                act.activation(hf[:, i % 2, :], hf[:, i % 2, :], ACT.Exp, scale=-0.5).then_inc(s_nr, 1)
            if o == G_AT + 2:
                act.wait_ge(s_rt, 1)
                act.activation(SIG[:, :, 0:56], tiles(bank[4][:, :])[:, :, 32:88], ACT.Exp, scale=-1.0).then_inc(s_se, 1)
                act.activation(NA[0:H, :], pr("alog")[0:H], ACT.Exp).then_inc(s_ga, 1)
            if o == G_AT + 3:
                link(act, act.activation(GZ[:, 0, :], ROWT[0:H, :], ACT.Identity, bias=pr("dtb")[0:H]), a_link, al)
                link(act, act.activation(GZ[:, 1, :], GZ[:, 0, :], ACT.Abs), a_link, al)
                link(act, act.activation(GZ[:, 1, :], GZ[:, 1, :], ACT.Exp, scale=-1.0), a_link, al)
                act.activation(GZ[:, 1, :], GZ[:, 1, :], ACT.Ln, bias=onec[0:H, 0:1]).then_inc(s_ga, 1)
            if o == G_AT + 6:
                act.wait_ge(s_gt, 2)
                act.activation(EGT, GT, ACT.Exp).then_inc(s_ge, 1)
                act.activation(EGL, GLB, ACT.Exp).then_inc(s_ge, 1)
                act.wait_ge(s_gk, 1)
                act.activation(EKD, EKD, ACT.Exp).then_inc(s_ge, 1)
            if o == HIN - 1:
                act.wait_ge(s_cm, 1)
                act.activation(CSC[:, :, :], CSC[:, :, :], ACT.Exp, scale=DH ** -0.5).then_inc(s_ce, 1)

        def dve_early(dve, o):
            i = o - N_AT - 1
            if 0 <= i < 8:
                dve.wait_ge(s_nr, i + 1)
                if i < 4:
                    dve.scalar_tensor_tensor(out=QKVS[:, i, :], in0=QKVS[:, i, :], scalar=P ** -0.5, in1=hf[:, i % 2, :],
                                             op0=ALU.mult, op1=ALU.mult).then_inc(s_nn, 1)
                else:
                    dve.tensor_tensor(QKVS[:, i, :], QKVS[:, i, :], hf[:, i % 2, :], ALU.mult).then_inc(s_nn, 1)
            if o == G_AT + 2:
                dve.wait_ge(s_se, 1)
                link(dve, dve.tensor_scalar(SIG[:, :, 0:56], SIG[:, :, 0:56], 1.0, None, ALU.add), v_link, vl)
                dve.reciprocal(SIG[:, :, 0:56], SIG[:, :, 0:56]).then_inc(s_sg, 1)
            if o == G_AT + 4:
                dve.wait_ge(s_ga, 2)
                link(dve, dve.scalar_tensor_tensor(out=GZ[:, 1, :], in0=GZ[:, 0, :], scalar=0.0, in1=GZ[:, 1, :],
                                                   op0=ALU.max, op1=ALU.add), v_link, vl)
                link(dve, dve.tensor_scalar(GZ[:, 1, :], GZ[:, 1, :], NA[0:H, :], -1.0, ALU.mult, ALU.mult), v_link, vl)
                for n in range(NT):
                    t = slice(n * P, (n + 1) * P)
                    dve.tensor_tensor_scan(G[:, t], ones[0:H, :], GZ[:, 1, t], 0.0, ALU.mult, ALU.add).then_inc(s_gg, 1)
            if o == G_AT + 5:
                dve.wait_ge(s_gtr, 1)
                dve.wait_ge(s_sg, 1)
                dve.tensor_copy(GT.rearrange("p (h n) -> p n h", n=NT), bank[5][:, 0:16].rearrange("p (n h) -> p n h", n=NT)
                                ).then_inc(s_gt, 1)
                dve.tensor_copy(GLB, bank[5][:, 16:32]).then_inc(s_gt, 1)
                link(dve, dve.tensor_copy(BT.rearrange("p (h n) -> p n h", n=NT), SIG[:, :, 0:H]), v_link, vl)
                dve.wait_ge(s_gt, 2)
                dve.tensor_tensor(EKD, GLB, GT, ALU.subtract).then_inc(s_gk, 1)
            if o == G_AT + 7:
                dve.wait_ge(s_ge, 1)
                dve.tensor_tensor(BEG, BT, EGT, ALU.mult).then_inc(s_gk, 1)

        def pe_compress_in(pe):
            pe.wait_ge(s_wl, 8)
            pe.wait_ge(s_bl16, 2)
            for t in range(2):
                for q in range(CL):
                    for j, (a, b) in enumerate(PASSES):
                        for g in range(2):
                            r = slice(g * DH, (g + 1) * DH)
                            m = pe.matmul(bank[4 + g][:, t * NCP:t * NCP + NC], W1P[r, (t * CL + q) // 8, a, q % 8 * P:(q % 8 + 1) * P],
                                          BLKP[r, b, t, q * NC:(q + 1) * NC], start=(q == 0 and j == 0),
                                          stop=(q == CL - 1 and j == 2))
            m.then_inc(s_hid, 1)

        def pe_compress_v(pe):
            pe.wait_ge(s_nl, 8)
            for b in range(2):
                was_read(pe, O_HIN + VSW + b)
                for n in range(NT):
                    m = pe.transpose(bank[6 + b][:, n * P:(n + 1) * P], VF[:, b, n * P:(n + 1) * P], ident)
                m.then_inc(s_vt, 1)

        def pe_compress_out(pe):
            pe.wait_ge(s_hs, 4)
            pe.matmul(bank[5][:, 0:2 * NCP], W2[:, 0, :], HS[:, 0, :, :].rearrange("p g c -> p (g c)"), start=True, stop=True)
            for g in range(2):
                m = pe.matmul(bank[5][0:NCP, 64 + g * DH:64 + (g + 1) * DH], HS[:, 1, g, :], W2[:, 1, 0:DH],
                              start=True, stop=True)
            m.then_inc(s_kv, 1)

        def dve_compress(dve, o):
            if o == 0:
                dve.memset(HS[:, :, :, :], 0.0).then_inc(s_clr, 1)
                dve.memset(VBD[:, :, :], 0.0).then_inc(s_clr, 1)
            k = o - W1_AT
            if 0 <= k < 8:
                dve.wait_ge(s_wh, k + 1)
                dve.scalar_tensor_tensor(out=W1P[:, k, 1, :], in0=W1[:, k, :], scalar=WS, in1=W1P[:, k, 0, :],
                                         op0=ALU.mult, op1=ALU.subtract).then_inc(s_wl, 1)
            t = o - BLK_AT
            if 0 <= t < 2:
                pe_ = PARAM["pe"][0]
                was_read(dve, O_HIN + KC + t)
                src = KCF[:, t, :].rearrange("p (c r) -> p r c", r=CS)
                for a in range(2):
                    dve.tensor_tensor(BLK[:, t, a * CS:(a + 1) * CS, :], src[:, :, a:a + NC],
                                      along(par[:, pe_ + t * CL + a * CS:pe_ + t * CL + (a + 1) * CS], NC),
                                      ALU.add).then_inc(s_blk, 1)
            t = o - BLK_AT - 1
            if 0 <= t < 2:
                dve.wait_ge(s_bh16, t + 1)
                dve.tensor_tensor(BLKP[:, 1, t, :], BLK[:, t, :, :].rearrange("p q c -> p (q c)"), BLKP[:, 0, t, :],
                                  ALU.subtract).then_inc(s_bl16, 1)
            if o == H_AT + 3:
                dve.wait_ge(s_kch, 2)
                for g in range(2):
                    r = slice(g * DH, (g + 1) * DH)
                    dve.tensor_tensor(KCM[r, 1, :], bank[5][r, g * NCP:(g + 1) * NCP], KCM[r, 0, :],
                                      ALU.subtract).then_inc(s_kcm, 1)
                dve.wait_ge(s_clr, 2)
                for i in range(4):
                    dve.tensor_copy(VBD[i * NCP:(i + 1) * NCP, :, i * DH:(i + 1) * DH],
                                    bank[5][0:NCP, 64:64 + 2 * DH].rearrange("p (g d) -> p g d", g=2)).then_inc(s_kcm, 1)

        def act_compress(act, o):
            k = o - W1_AT
            if k == 0:
                act.wait_ge(s_w1, 16 * 6)
            if 0 <= k < 8:
                if k:
                    act.wait_ge(s_wl, k)
                act.activation(W1P[:, k, 0, :], W1[:, k, :], ACT.Copy, scale=WS).then_inc(s_wh, 1)
            t = o - BLK_AT - 1
            if 0 <= t < 2:
                act.wait_ge(s_blk, 2 * t + 2)
                act.activation(BLKP[:, 0, t, :], BLK[:, t, :, :].rearrange("p q c -> p (q c)"), ACT.Copy).then_inc(s_bh16, 1)
            if o == H_AT:
                act.wait_ge(s_hid, 1)
                act.wait_ge(s_clr, 1)
                for t in range(2):
                    for g in range(2):
                        act.activation(HS[:, t, g, 0:NC], bank[4 + g][:, t * NCP:t * NCP + NC], ACT.Silu, scale=1 / WS,
                                       bias=pr("b1", t)).then_inc(s_hs, 1)
            if o == H_AT + 2:
                act.wait_ge(s_kv, 1)
                for g in range(2):
                    r = slice(g * DH, (g + 1) * DH)
                    act.activation(KCM[r, 0, :], bank[5][r, g * NCP:(g + 1) * NCP], ACT.Copy).then_inc(s_kch, 1)

        def pe_cmp_scores(pe, g):
            if g:
                pe.wait_ge(s_mk, 1)
            else:
                pe.wait_ge(s_se, 1)
                pe.wait_ge(s_kcm, 6)
                for o in range(QB, KSW):
                    was_read(pe, O_HIN + o)
            r = slice(g * DH, (g + 1) * DH)
            for n in range(NT):
                for h in range(4):
                    a = (n * 4 + h) * NCP
                    for j, (a_, b_) in enumerate(PASSES):
                        m = pe.matmul(bank[4][:, a:a + NCP], QBP[r, a_, h, n * P:(n + 1) * P], KCM[r, b_, :],
                                      start=(j == 0), stop=(j == 2))
            m.then_inc(s_cs, 1)

        def pe_cmp(pe):
            pe.wait_ge(s_gt, 2)
            pe.wait_ge(s_cp, 1)
            for n in range(NT):
                for g in range(2):
                    m = pe.transpose(bank[4 + n // 2][:, (n % 2 * 2 + g) * P:(n % 2 * 2 + g + 1) * P],
                                     CSC[:, n, g * P:(g + 1) * P], ident)
                if n % 2:
                    m.then_inc(s_ct, 1)
            pe_compress_v(pe)
            for o in range(HIN - SLOTS, HIN):
                was_read(pe, O_HIN + o)

            def spread_row(h):
                if h >= 2:
                    pe.wait_ge(s_gbr, h - 1)
                pe.matmul(bank[h % 2][:, :], mk("sel")[0:H, h * P:(h + 1) * P], G[:, :], start=True, stop=True).then_inc(s_gb, 1)

            spread_row(0)
            spread_row(1)
            for n in range(NT):
                pe.wait_ge(s_cpt, n // 2 + 1)
                if n >= 2:
                    pe.wait_ge(s_ca, n - 1)
                for g in range(2):
                    m = pe.matmul(bank[2 + n % 2][:, g * 4 * DH:(g + 1) * 4 * DH], CPT[:, n, g * P:(g + 1) * P],
                                  VBD[:, g, :], start=True, stop=True)
                m.then_inc(s_co, 1)
            spread_row(2)
            spread_row(3)

        def heads(a):
            return a.rearrange("p n (h c) -> p n h c", c=NCP)

        CROWS = CSC.rearrange("p n (h c) -> p (n h) c", c=NCP)

        def dve_cmp_mask(dve, g):
            cadd = mk("cadd").rearrange("p (n c) -> p n c", c=NCP)
            dve.wait_ge(s_cs, g + 1)
            dve.tensor_tensor(heads(CSC)[:, :, 4 * g:4 * g + 4, :], bank[4][:, :].rearrange("p (n h c) -> p n h c", h=4, c=NCP),
                              cadd.unsqueeze(2).to_broadcast([P, NT, 4, NCP]), ALU.add).then_inc(s_mk, 1)
            if g:
                dve.wait_ge(s_mk, 2)
                link(dve, dve.tensor_reduce(CMX, CROWS, AX_X, ALU.max), v_link, vl)
                dve.tensor_tensor(CROWS, CROWS, along(CMX, NCP), ALU.subtract).then_inc(s_cm, 1)

        def dve_cmp_probs(dve):
            c01 = mk("c01").rearrange("p (n c) -> p n c", c=NCP)
            dve.wait_ge(s_ce, 1)
            link(dve, dve.tensor_reduce(CLS, CROWS, AX_X, ALU.add), v_link, vl)
            link(dve, dve.reciprocal(CRC, CLS), v_link, vl)
            dve.wait_ge(s_sg, 1)
            link(dve, dve.tensor_tensor(CRC.rearrange("p (n h) -> p n h", h=NH), CRC.rearrange("p (n h) -> p n h", h=NH),
                                        SIG[:, :, 32:40], ALU.mult), v_link, vl)
            link(dve, dve.tensor_tensor(CROWS, CROWS, along(CRC, NCP), ALU.mult), v_link, vl)
            dve.tensor_tensor(heads(CSC), heads(CSC), c01.unsqueeze(2).to_broadcast([P, NT, NH, NCP]),
                              ALU.mult).then_inc(s_cp, 1)

        def dve_cmp(dve):
            for a in range(2):
                dve.wait_ge(s_ct, a + 1)
                dve.tensor_copy(CPT[:, 2 * a:2 * a + 2, :], bank[4 + a][:, :].rearrange("p (n c) -> p n c", n=2)
                                ).then_inc(s_cpt, 1)
            for b in range(2):
                dve.wait_ge(s_vh, b + 1)
                dve.tensor_tensor(VTP[:, 1, b, :, :], tiles(bank[6 + b][:, :]), VTP[:, 0, b, :, :],
                                  ALU.subtract).then_inc(s_vtk, 1)
            for n in range(NT):
                dve.wait_ge(s_co, n + 1)
                dve.tensor_copy(ACC[:, n, :], bank[2 + n % 2][:, :]).then_inc(s_ca, 1)

        UNITS = NT * 2 * NH

        TB = (2, 6, 7)
        DECAYS_AT = (8, 16, 24, 32)

        def unit(u):
            return u // (2 * NH), u // NH % 2, u % NH, (u // (2 * NH) + 1) * P

        def pe_attention(pe):
            pe.wait_ge(s_vtk, 2)
            for u in range(UNITS + 4):
                if u < UNITS:
                    i, b, h, keys = unit(u)
                    r = slice(h // 4 * DH, h // 4 * DH + DH)
                    if u >= 2:
                        pe.wait_ge(s_m, u - 1)
                    for j, (a_, b_) in enumerate(PASSES):
                        m = pe.matmul(bank[4 + u % 2][:, 0:keys], QBP[r, a_, h % 4, i * P:(i + 1) * P], KSP[r, b_, b, 0:keys],
                                      start=(j == 0), stop=(j == 2))
                    m.then_inc(s_s, 1)
                if 2 <= u < UNITS + 2:
                    w = u - 2
                    i = unit(w)[0]
                    pe.wait_ge(s_e, w + 1)
                    if w >= 3:
                        pe.wait_ge(s_pl, w - 2)
                    else:
                        pe.wait_ge(s_ca, NT)
                    for k in range(i + 1):
                        m = pe.transpose(bank[TB[w % 3]][:, k * P:(k + 1) * P], PP[:, w % 3, k * P:(k + 1) * P], ident)
                    m.then_inc(s_t, 1)
                if u >= 4:
                    w = u - 4
                    i, b, h, keys = unit(w)
                    v = w // NH
                    pe.wait_ge(s_pl, w + 1)
                    if w == 0:
                        pe.wait_ge(s_gbr, H)
                    if h == 0 and v >= 2:
                        pe.wait_ge(s_cb, v - 1)
                    for k in range(i + 1):
                        for j, (a_, b_) in enumerate(PASSES):
                            m = pe.matmul(bank[v % 2][:, h * DH:(h + 1) * DH], PTP[:, a_, w % 3, k * P:(k + 1) * P],
                                          VTP[:, b_, b, k, h // 4 * DH:h // 4 * DH + DH], start=(k == 0 and j == 0),
                                          stop=(k == i and j == 2))
                    m.then_inc(s_pv, 1)
                    if w % (2 * NH) == 6 and i:
                        pe_attention_out(pe, i - 1)

        def pe_attention_out(pe, i):
            pe.wait_ge(s_acc, 2 * (i + 1))
            if i:
                pe.wait_ge(s_om, i)
            for k in range(4):
                m = pe.transpose(bank[3][:, k * P:(k + 1) * P], ACC[:, i, k * P:(k + 1) * P], ident)
            m.then_inc(s_at, 1)

        def act_attention(act):
            def high(i):
                act.wait_ge(s_at, i + 1)
                act.activation(hh[:, 4:8, i * P:(i + 1) * P], tiles(bank[3][:, :]), ACT.Copy).then_inc(s_omh, 1)

            for u in range(UNITS + 2):
                if u in DECAYS_AT:
                    a = DECAYS_AT.index(u)
                    act.wait_ge(s_dd, 2 * (a + 1))
                    act.activation(AK[:, a, :, :], AK[:, a, :, :], ACT.Exp, scale=-1.0).then_inc(s_ex, 1)
                    act.activation(AQ[:, a, :, :], AQ[:, a, :, :], ACT.Exp).then_inc(s_ex, 1)
                    act.wait_ge(s_d, a + 1)
                    act.activation(GB[:, a, :], GB[:, a, :], ACT.Exp).then_inc(s_eg, 1)
                if u >= 2:
                    w = u - 2
                    keys = unit(w)[3]
                    act.wait_ge(s_t, w + 1)
                    if w >= 3:
                        act.wait_ge(s_pv, w - 2)
                    act.activation(PTP[:, 0, w % 3, 0:keys], bank[TB[w % 3]][:, 0:keys], ACT.Copy).then_inc(s_pc, 1)
                if u >= UNITS:
                    continue
                i, b, h, keys = unit(u)
                v = u // NH
                act.wait_ge(s_m, u + 1)
                if u >= 3:
                    act.wait_ge(s_t, u - 2)
                if h == 0 and v >= 2:
                    act.wait_ge(s_cb, v - 1)
                act.activation(PP[:, u % 3, 0:keys], SM[:, u % 2, 0:keys], ACT.Exp, scale=-1.0,
                               bias=NMX[:, u % 2:u % 2 + 1], accum_out=LS[:, v % 2 * NH + h:v % 2 * NH + h + 1]
                               ).then_inc(s_e, 1)
                if u % (2 * NH) == 12 and i:
                    high(i - 1)
            high(NT - 1)

        def dve_attention(dve):
            def low(i):
                dve.wait_ge(s_omh, i + 1)
                t = slice(i * P, (i + 1) * P)
                dve.tensor_tensor(hl[:, 4:8, t], tiles(bank[3][:, :]), hh[:, 4:8, t], ALU.subtract).then_inc(s_om, 1)

            def combine(v):
                i, b = v // 2, v % 2
                dve.wait_ge(s_pv, NH * (v + 1))
                link(dve, dve.reciprocal(RC, LS[:, b * NH:(b + 1) * NH]), v_link, vl)
                link(dve, dve.tensor_tensor(RC, RC, SIG[:, i, 40 + NH * b:48 + NH * b], ALU.mult), v_link, vl)
                if v:
                    dve.wait_ge(s_acc, v)
                dve.tensor_tensor(TMP.rearrange("p (h d) -> p h d", d=DH), bank[v % 2][:, :].rearrange("p (h d) -> p h d", d=DH),
                                  along(RC, DH), ALU.mult).then_inc(s_cb, 1)

            for u in range(UNITS + 3):
                if u < UNITS:
                    i, b, h, keys = unit(u)
                    dve.wait_ge(s_s, u + 1)
                    if u >= 2:
                        dve.wait_ge(s_e, u - 1)
                    dve.tensor_tensor_reduce(out=SM[:, u % 2, 0:keys], in0=bank[4 + u % 2][:, 0:keys],
                                             in1=mk("neg")[:, S - keys:S], scale=-DH ** -0.5, scalar=3e38, op0=ALU.add,
                                             op1=ALU.min, accum_out=NMX[:, u % 2:u % 2 + 1]).then_inc(s_m, 1)
                if u >= 3:
                    w = u - 3
                    keys = unit(w)[3]
                    dve.wait_ge(s_pc, w + 1)
                    dve.tensor_tensor(PTP[:, 1, w % 3, 0:keys], bank[TB[w % 3]][:, 0:keys], PTP[:, 0, w % 3, 0:keys],
                                      ALU.subtract).then_inc(s_pl, 1)
                if u % NH == 4 and u > NH:
                    combine(u // NH - 1)
                if u % (2 * NH) == 14 and u > 2 * NH:
                    low(u // (2 * NH) - 1)
            combine(2 * NT - 1)
            low(NT - 1)

        PREP_BANKS = ((5, 7, 6, 0), (4, 2, 3, 1))

        def pe_gdn_prep(pe):
            for h in range(H):
                b = PREP_BANKS[h % 2]
                if h >= 2:
                    pe.wait_ge(s_ak, h - 1)
                q, k, v = (tiles(QKVS[:, a + h, :]) for a in (0, 4, 8))
                for n in range(NT):
                    m = pe.matmul(bank[b[0]][:, n * P:(n + 1) * P], k[:, n, :], k[:, n, :], start=True, stop=True)
                m.then_inc(s_kk, 1)
                if h >= 2:
                    pe.wait_ge(s_kd, h - 1)
                for n in range(NT):
                    m = pe.transpose(bank[b[1]][:, n * P:(n + 1) * P], k[:, n, :], ident)
                m.then_inc(s_kt, 1)
                if h == 0:
                    pe_attention_out(pe, NT - 1)
                if h == 1:
                    pe.wait_ge(s_om, NT)
                if h >= 2:
                    pe.wait_ge(s_aq, h - 1)
                for n in range(NT):
                    m = pe.matmul(bank[b[2]][:, n * P:(n + 1) * P], k[:, n, :], q[:, n, :], start=True, stop=True)
                m.then_inc(s_qk, 1)
                if h >= 2:
                    pe.wait_ge(s_bv, h - 1)
                for n in range(NT):
                    m = pe.transpose(bank[b[3]][:, n * P:(n + 1) * P], v[:, n, :], ident)
                m.then_inc(s_vr, 1)

        def act_gdn_prep(act):
            act.wait_ge(s_ge, 3)
            act.wait_ge(s_gk, 2)
            for h in range(H):
                src = bank[PREP_BANKS[h % 2][1]]
                act.wait_ge(s_kt, h + 1)
                for n in range(NT):
                    t = slice(n * P, (n + 1) * P)
                    act.activation(KD[:, h, n, :], src[:, t], ACT.Identity, scale=EKD[:, h * NT + n:h * NT + n + 1])
                act.wait_ge(s_qk, h + 1)
                for n in range(NT):
                    t = slice(n * P, (n + 1) * P)
                    m = act.activation(QKVS[:, 4 + h, t], src[:, t], ACT.Identity, scale=BEG[:, h * NT + n:h * NT + n + 1])
                m.then_inc(s_kd, 1)

        def pool_gdn(pool):
            def blocks(lv, h):
                if lv == 0:
                    pool.wait_ge(s_ak, h + 1)
                m = mk("lev")[:, lv * P:(lv + 1) * P]
                pool.tensor_tensor(BM[:, h, :, :], AK[:, h, :, :], spread(m, NT), ALU.mult).then_inc(s_b, 1)

            def differences(h):
                pool.wait_ge(s_gbr, h + 1)
                pool.tensor_tensor(AK[:, h, :, :], tiles(GB[:, h, :]), along(GT[:, h * NT:(h + 1) * NT], P), ALU.subtract
                                   ).then_inc(s_d, 1)
                pool.wait_ge(s_d, h + 1)
                pool.tensor_scalar(AQ[:, h, :, :], AK[:, h, :, :], 0.0, None, ALU.min).then_inc(s_dd, 1)
                pool.wait_ge(s_dd, 2 * h + 1)
                pool.tensor_scalar(AK[:, h, :, :], AK[:, h, :, :], 0.0, None, ALU.max).then_inc(s_dd, 1)

            def attention_add(v):
                pool.wait_ge(s_cb, v + 1)
                if v:
                    pool.wait_ge(s_acc, v)
                else:
                    pool.wait_ge(s_ca, NT)
                pool.tensor_tensor(ACC[:, v // 2, :], ACC[:, v // 2, :], TMP, ALU.add).then_inc(s_acc, 1)

            pool.wait_ge(s_gt, 2)
            differences(0)
            for h in range(H):
                if h < H - 1:
                    differences(h + 1)
                pool.wait_ge(s_ex, 2 * h + 1)
                link(pool, pool.tensor_tensor(AK[:, h, :, :], AK[:, h, :, :], spread(mk("strict"), NT), ALU.mult), g_link, gl_)
                pool.tensor_tensor(AK[:, h, :, :], AK[:, h, :, :], along(BT[:, h * NT:(h + 1) * NT], P), ALU.mult
                                   ).then_inc(s_e1, 1)
                pool.wait_ge(s_ex, 2 * h + 2)
                pool.tensor_tensor(AQ[:, h, :, :], AQ[:, h, :, :], spread(mk("incl"), NT), ALU.mult).then_inc(s_e2, 1)
                attention_add(h)
            for v in range(H, 2 * NT):
                attention_add(v)
            for h in range(H):
                pool.wait_ge(s_eg, h + 1)
                pool.wait_ge(s_qk, h + 1)
                pool.tensor_tensor(QKVS[:, h, :], QKVS[:, h, :], GB[:, h, :], ALU.mult).then_inc(s_qg, 1)
                if h:
                    blocks(0, h - 1)
            blocks(0, H - 1)
            for lv in range(1, 7):
                for h in range(H):
                    if lv == 1:
                        pool.wait_ge(s_tt, h + 1)
                    else:
                        pool.wait_ge(s_xp, (lv - 2) * H + h + 1)
                    blocks(lv, h)

        def dve_gdn_prep(dve):
            for h in range(H):
                c = slice(h * NT, (h + 1) * NT)
                b = PREP_BANKS[h % 2]
                dve.wait_ge(s_kk, h + 1)
                dve.wait_ge(s_e1, h + 1)
                dve.tensor_tensor(AK[:, h, :, :], tiles(bank[b[0]][:, :]), AK[:, h, :, :], ALU.mult).then_inc(s_ak, 1)
                dve.wait_ge(s_qk, h + 1)
                dve.wait_ge(s_e2, h + 1)
                dve.tensor_tensor(AQ[:, h, :, :], tiles(bank[b[2]][:, :]), AQ[:, h, :, :], ALU.mult).then_inc(s_aq, 1)
                dve.wait_ge(s_vr, h + 1)
                dve.tensor_tensor(tiles(QKVS[:, 8 + h, :]), tiles(bank[b[3]][:, :]), along(BT[:, c], P),
                                  ALU.mult).then_inc(s_bv, 1)
                if h:
                    dve_inverse_start(dve, h - 1)
            dve_inverse_start(dve, H - 1)

        def dve_inverse_start(dve, h):
            dve.wait_ge(s_b, h + 1)
            dve.tensor_tensor(TT[:, h, :, :], spread(ident, NT), BM[:, h, :, :], ALU.subtract).then_inc(s_tt, 1)

        def pe_inverse(pe):
            for h in range(H):
                pe.wait_ge(s_tt, h + 1)
                if h == 0:
                    pe.wait_ge(s_bv, H)
                    pe.wait_ge(s_kd, H)
                    pe.wait_ge(s_aq, H)
                for n in range(NT):
                    m = pe.transpose(bank[h][:, n * P:(n + 1) * P], TT[:, h, n, :], ident)
                m.then_inc(s_ut, 1)
            for lv in range(1, 7):
                for h in range(H):
                    pe.wait_ge(s_uu, (lv - 1) * H + h + 1)
                    pe.wait_ge(s_b, lv * H + h + 1)
                    if lv >= 3:
                        pe.wait_ge(s_tt, (lv - 2) * H + h + 1)
                    for n in range(NT):
                        m = pe.matmul(bank[h][:, n * P:(n + 1) * P], BM[:, h, n, :], UU[:, h, n, :], start=True, stop=True)
                    m.then_inc(s_xp, 1)
                for h in range(H):
                    pe.wait_ge(s_xx, (lv - 1) * H + h + 1)
                    if lv == 1:
                        break
                    for n in range(NT):
                        m = pe.transpose(bank[h][:, n * P:(n + 1) * P], UU[:, h, n, :], ident)
                    m.then_inc(s_zt, 1)
                for h in range(H):
                    pe.wait_ge(s_xx, (lv - 1) * H + h + 1)
                    pe.wait_ge(s_tt, (lv - 1) * H + h + 1 if lv > 1 else H)
                    if lv == 1:
                        pe.wait_ge(s_aq, H)
                    for n in range(NT):
                        m = pe.matmul(bank[4 + h][:, n * P:(n + 1) * P], TT[:, h, n, :], XX[:, h, n, :], start=True, stop=True)
                    m.then_inc(s_zu, 1)

        def dve_inverse(dve):
            for h in range(H):
                dve.wait_ge(s_ut, h + 1)
                dve.tensor_copy(UU[:, h, :, :], tiles(bank[h][:, :])).then_inc(s_uu, 1)
            for lv in range(1, 7):
                for h in range(H):
                    if lv == 1:
                        break
                    dve.wait_ge(s_zt, (lv - 2) * H + h + 1)
                    dve.tensor_copy(TT[:, h, :, :], tiles(bank[h][:, :])).then_inc(s_tt, 1)
                for h in range(H):
                    dve.wait_ge(s_zu, (lv - 1) * H + h + 1)
                    dve.tensor_tensor(UU[:, h, :, :], UU[:, h, :, :], tiles(bank[4 + h][:, :]), ALU.subtract).then_inc(s_uu, 1)

        def act_inverse(act):
            for i in range(6 * H):
                act.wait_ge(s_xp, i + 1)
                act.activation(XX[:, i % H, :, :], tiles(bank[i % H][:, :]), ACT.Copy).then_inc(s_xx, 1)

        SUM_BANK = (4, 5, 6, 1)

        def pe_gdn_scan(pe):
            def head_sum(n):
                pe.wait_ge(s_hq, n + 1)
                if n < NT - 1:
                    pe.wait_ge(s_oa, n + 1)
                pe.matmul(bank[SUM_BANK[n]][:, :], ones, EE[:, n % 2, :], start=True, stop=True).then_inc(s_hsum, 1)

            for h in range(H):
                pe.wait_ge(s_uu, 6 * H + h + 1)
                for n in range(NT):
                    m = pe.matmul(bank[h][:, n * P:(n + 1) * P], UU[:, h, n, :], QKVS[:, 8 + h, n * P:(n + 1) * P],
                                  start=True, stop=True)
                m.then_inc(s_u, 1)
                for n in range(NT):
                    m = pe.matmul(bank[4 + h][:, n * P:(n + 1) * P], QKVS[:, 4 + h, n * P:(n + 1) * P], UU[:, h, n, :],
                                  start=True, stop=True)
                m.then_inc(s_w, 1)
            pe.wait_ge(s_om, NT)
            pe.wait_ge(s_us, H)
            two_start(pe, C_HOUT, O_HOUT)
            for n in range(NT):
                if n:
                    pe.wait_ge(s_ss, n)
                    for h in range(H):
                        m = pe.matmul(bank[2][:, h * P:(h + 1) * P], WT[:, h, n, :], SS[:, h, :],
                                      start=True, stop=True)
                    m.then_inc(s_p2, 1)
                two_block(pe, C_HOUT, O_HOUT, DB // 2 + n, n == 0, False)
                pe.wait_ge(s_vn, n + 1)
                if n == 0:
                    pe.wait_ge(s_wt, H)
                if n < NT - 1:
                    for h in range(H):
                        m = pe.matmul(bank[1][:, h * P:(h + 1) * P], KD[:, h, n, :], VN[:, h, :], start=True, stop=True)
                    m.then_inc(s_ds, 1)
                for h in range(H):
                    o = bank[4 + n][:, h * P:(h + 1) * P]
                    if n:
                        pe.matmul(o, SS[:, h, :], QKVS[:, h, n * P:(n + 1) * P], start=True, stop=False)
                    m = pe.matmul(o, VN[:, h, :], AQ[:, h, n, :], start=(n == 0), stop=True)
                m.then_inc(s_oo, 1)
                if n:
                    head_sum(n - 1)
            head_sum(NT - 1)

        def act_gdn_scan(act):
            for h in range(H):
                act.wait_ge(s_u, h + 1)
                act.activation(US[:, h, :, :], tiles(bank[h][:, :]), ACT.Copy).then_inc(s_us, 1)
                act.wait_ge(s_w, h + 1)
                act.activation(WT[:, h, :, :], tiles(bank[4 + h][:, :]), ACT.Copy).then_inc(s_wt, 1)
            for n in range(NT + 2):
                if n < NT:
                    act.wait_ge(s_oo, n + 1)
                    if n >= 2:
                        act.wait_ge(s_hsum, n - 1)
                    act.activation(EE[:, n % 2, :], bank[4 + n][:, :], ACT.Square).then_inc(s_hq, 1)
                if 1 <= n <= NT:
                    t = n - 1
                    act.wait_ge(s_hsum, t + 1)
                    if t >= 2:
                        act.wait_ge(s_on, t - 1)
                    act.activation(hf[:, t % 2, :], bank[SUM_BANK[t]][:, :], ACT.Ln, bias=epsc[:, 2:3]).then_inc(s_hln, 1)
                    act.wait_ge(s_hln, t + 1)
                    act.activation(hf[:, t % 2, :], hf[:, t % 2, :], ACT.Exp, scale=-0.5).then_inc(s_hr, 1)
                if n >= 2:
                    t = n - 2
                    act.wait_ge(s_on, t + 1)
                    act.activation(hh[:, 0:H, t * P:(t + 1) * P], OA[:, :, t, :], ACT.Copy).then_inc(s_omh, 1)

        def dve_gdn_scan(dve):
            dve.wait_ge(s_us, H)
            dve.wait_ge(s_wt, H)

            def gate(n):
                dve.wait_ge(s_hq, n + 1)
                dve.tensor_tensor(OA[:, :, n, :], tiles(bank[4 + n][:, :]), GAT[:, :, n * P:(n + 1) * P], ALU.mult
                                  ).then_inc(s_oa, 1)

            def norm(n):
                dve.wait_ge(s_hr, n + 1)
                dve.wait_ge(s_oa, n + 1)
                dve.tensor_tensor(OA[:, :, n, :], OA[:, :, n, :], tiles(hf[:, n % 2, :]), ALU.mult).then_inc(s_on, 1)

            def low(n):
                dve.wait_ge(s_omh, NT + n + 1)
                dve.tensor_tensor(hl[:, 0:H, n * P:(n + 1) * P], OA[:, :, n, :], hh[:, 0:H, n * P:(n + 1) * P],
                                  ALU.subtract).then_inc(s_om, 1)

            for n in range(NT):
                if n == 0:
                    dve.tensor_copy(VN, US[:, :, 0, :]).then_inc(s_vn, 1)
                else:
                    link(dve, dve.tensor_tensor(SD, SS, along(EGL[:, n:4 * H:NT], P), ALU.mult), v_link, vl)
                    dve.wait_ge(s_p2, n)
                    dve.tensor_tensor(VN, US[:, :, n, :], tiles(bank[2][:, :]), ALU.subtract).then_inc(s_vn, 1)
                    gate(n - 1)
                if n < NT - 1:
                    dve.wait_ge(s_ds, n + 1)
                    if n == 0:
                        dve.tensor_copy(SS, tiles(bank[1][:, :])).then_inc(s_ss, 1)
                    else:
                        dve.wait_ge(s_oo, n + 1)
                        dve.tensor_tensor(SS, SD, tiles(bank[1][:, :]), ALU.add).then_inc(s_ss, 1)
                    dve.wait_ge(s_ss, n + 1)
                if n >= 2:
                    norm(n - 2)
            gate(NT - 1)
            low(0)
            low(1)
            for n in range(2, NT):
                norm(n)
            for n in range(2, NT):
                low(n)

        HB = DH
        AT_Z, AT_B, AT_K, AT_KQ, AT_V, AT_S = 2, 6, GV, GV + 2, GR, GR + 2

        def pe_gla(pe):
            first_two(pe, C_GIN, O_GIN, 4)
            for i in range(2, GIN):
                pe_gla_step(pe, i)
                if i == GIN - 1:
                    pe.wait_ge(s_loo, 2 * NT)
                    pe.wait_ge(s_lss, NT - 1)
                    for h in range(H):
                        for a in range(2):
                            pe.wait_ge(s_hq, H + 2 * h + a + 1)
                            m = pe.matmul(bank[4 + h][:, :], ones, SQO[:, 2 * h + a, :], start=(a == 0), stop=(a == 1))
                        m.then_inc(s_hsum, 1)
                chunk(pe, C_GIN + i, O_GIN + i, hh, hl)

        def pe_gla_step(pe, i):
            k = i - AT_Z
            if k in (0, 1):
                was_read(pe, O_GIN + ALR)
                pe.wait_ge(s_aw, 16)
                for h in (2 * k, 2 * k + 1):
                    pe.matmul(bank[4 + h][:, :], AW2[0:16, h * P:(h + 1) * P], ALRS[0:16, :], start=True, stop=True
                              ).then_inc(s_z, 1)
            h = i - AT_KQ - 1
            if 0 <= h < H:
                kk = KKT[:, h % 2, :]
                qt = QT[:, h % 2, :].rearrange("p (n a r) -> p n a r", a=2, r=HB)
                pe.wait_ge(s_lm, h + 1)
                if h >= 2:
                    pe.wait_ge(s_la, h - 1)
                for n in range(NT):
                    pe.matmul(bank[4 + h % 2][:, n * P + HB:(n + 1) * P], kk[:, n * P:(n + 1) * P], qt[:, n, 1, :],
                              start=True, stop=True)
                    m = pe.matmul(bank[4 + h % 2][:, n * P:n * P + HB], kk[:, S + n * P:S + (n + 1) * P], qt[:, n, 0, :],
                                  start=True, stop=True)
                m.then_inc(s_lap, 1)
                pe.wait_ge(s_lg, h + 1)
                if h >= 2:
                    pe.wait_ge(s_kdt, h - 1)
                for n in range(NT):
                    m = pe.transpose(bank[6 + h % 2][:, n * P:(n + 1) * P], LK[:, h, n * P:(n + 1) * P], ident)
                m.then_inc(s_kp, 1)
            k = i - AT_V - 1
            if k in (0, 1):
                if k == 0:
                    pe.wait_ge(s_la, H)
                    pe.wait_ge(s_kdt, H)
                    for o in range(4):
                        was_read(pe, O_GIN + GR - 1 - o)
                for j in range(4 * k, 4 * k + 4):
                    n, a = j // 2, j % 2
                    if k:
                        pe.wait_ge(s_vv[a], j // 2 - 1)
                    for b in range(4):
                        m = pe.transpose(bank[4 + j % 4][:, b * P:(b + 1) * P], VFF[:, 4 * a + b, n * P:(n + 1) * P], ident)
                    m.then_inc(s_vp, 1)
            n = i - AT_S - 1
            if 0 <= n < NT:
                if n == 0:
                    for a in range(2):
                        pe.wait_ge(s_vv[a], NT)
                else:
                    pe.wait_ge(s_lss, n)
                    pe.wait_ge(s_loo, 2 * n)
                if n < NT - 1:
                    for h in range(H):
                        m = pe.matmul(bank[4 + h // 2][:, h % 2 * 2 * P:(h % 2 + 1) * 2 * P], KDT[:, h, n, :],
                                      VTT[:, n, h * 2 * P:(h + 1) * 2 * P], start=True, stop=True)
                    m.then_inc(s_lds, 1)
                for i_ in range(DB):
                    h = i_ // 2
                    o = bank[6 + i_ // 4][:, i_ % 4 * P:(i_ % 4 + 1) * P]
                    if n:
                        pe.matmul(o, LST[:, h, i_ % 2 * P:(i_ % 2 + 1) * P], LQ[:, h, n * P:(n + 1) * P], start=True, stop=False)
                    m = pe.matmul(o, VTT[:, n, i_ * P:(i_ + 1) * P], LA[:, h, n, :], start=(n == 0), stop=True)
                m.then_inc(s_lo, 1)

        def act_gla(act):
            for i in range(GIN):
                o = O_GIN + i
                split_hi(act, C_GIN + i + LEAD)
                if i == GR:
                    act.preload_act_table_set("silu_and_others")
                act_gla_step(act, i)
                if i == GIN - 1:
                    act_gla_norm(act)
                    act.preload_act_table_set("silu_and_others")
                summed(act, C_GIN + i)
                if i == GIN - 1:
                    act_gla_high(act, 0)
                    act_gla_high(act, 1)
                src = bank[o % SLOTS][:, :]
                if i == ALR:
                    m = act.activation(ALRS, src, ACT.Copy, scale=1 / WS)
                elif i < GK:
                    m = act.activation(LQ[:, i - GQ, :], src, ACT.Copy, scale=P ** -0.5 / WS)
                elif i < GV:
                    m = act.activation(LK[:, i - GK, :], src, ACT.Copy, scale=1 / WS)
                elif i < GR:
                    m = act.activation(VFF[:, i - GV, :], src, ACT.Copy, scale=1 / WS)
                else:
                    m = act.activation(RS[:, i - GR, :], src, ACT.Silu, scale=1 / WS)
                m.then_inc(b_free[o % SLOTS], 1)
            for i in range(2, DB):
                act_gla_high(act, i)

        def act_gla_high(act, i):
            act.wait_ge(s_on, H + i + 1)
            act.activation(hh[:, i, :], OO[:, i, :], ACT.Copy).then_inc(s_omh, 1)

        def act_gla_norm(act):
            act.preload_act_table_set("natural_log_exp_and_others")
            for h in range(H):
                act.wait_ge(s_hsum, H + h + 1)
                if h >= 2:
                    act.wait_ge(s_on, H + 2 * (h - 1))
                act.activation(hf[:, h % 2, :], bank[4 + h][:, :], ACT.Ln, bias=epsc[:, 3:4]).then_inc(s_hln, 1)
                act.wait_ge(s_hln, H + h + 1)
                act.activation(hf[:, h % 2, :], hf[:, h % 2, :], ACT.Exp, scale=-0.5).then_inc(s_hr, 1)

        def act_gla_step(act, i):
            h = i - AT_Z
            if 0 <= h < H:
                z, t = LZ[:, h % 2, :], LZ[:, 2 + h % 2, :]
                act.wait_ge(s_z, h + 1)
                if h >= 2:
                    act.wait_ge(s_lb, h - 1)
                link(act, act.activation(z, bank[4 + h][:, :], ACT.Identity, bias=pr("lab", h)), a_link, al)
                link(act, act.activation(t, z, ACT.Abs), a_link, al)
                link(act, act.activation(t, t, ACT.Exp, scale=-1.0), a_link, al)
                act.activation(t, t, ACT.Ln, bias=onec[:, 0:1]).then_inc(s_zl, 1)
            if i == AT_B:
                act.wait_ge(s_lb, H)
                act.activation(EBL.rearrange("p (h c) -> p h c", h=H), LB[:, :, HB - 1:S:HB], ACT.Exp, scale=1 / 16
                               ).then_inc(s_bl, 1)
            h = i - AT_K
            if 0 <= h < H:
                act.wait_ge(s_lx, h + 1)
                act.activation(EX[:, 0, :], EX[:, 0, :], ACT.Exp, scale=1 / 16).then_inc(s_le, 1)
                act.activation(EX[:, 1, :], LB[:, h, :], ACT.Exp, scale=1 / 16).then_inc(s_le, 1)
                act.activation(EX[:, 2, :], LB[:, h, :], ACT.Exp, scale=-1 / 16).then_inc(s_le, 1)
            h = i - AT_KQ - 1
            if 0 <= h < H:
                act.wait_ge(s_kp, h + 1)
                act.activation(KDT[:, h, :, :], tiles(bank[6 + h % 2][:, :]), ACT.Copy).then_inc(s_kdt, 1)
            k = i - AT_V - 1
            if k in (0, 1):
                for n in (2 * k, 2 * k + 1):
                    act.wait_ge(s_vp, 2 * n + 1)
                    act.activation(VTT[:, n, 0:S], bank[4 + 2 * n % 4][:, :], ACT.Copy).then_inc(s_vv[0], 1)
            n = i - AT_S - 1
            if 0 <= n < NT:
                act.wait_ge(s_lo, n + 1)
                for a in range(2):
                    act.activation(OO[:, 4 * a:4 * a + 4, n * P:(n + 1) * P], tiles(bank[6 + a][:, :]),
                                   ACT.Copy).then_inc(s_loo, 1)
            if n == NT - 1:
                act.wait_ge(s_loo, 2 * NT)
                for b in range(DB):
                    act.activation(SQO[:, b, :], OO[:, b, :], ACT.Square).then_inc(s_hq, 1)

        def pool_gla(pool):
            for h in range(H):
                qt = QT[:, h % 2, :].rearrange("p (n a r) -> p n a r", a=2, r=HB)
                mixed, kt = (KKT[:, h % 2, a:a + S].rearrange("p (n a r) -> p n a r", a=2, r=HB) for a in (0, S))
                q, k = (a[:, h, :].rearrange("p (n a r) -> p n a r", a=2, r=HB) for a in (LQ, LK))
                e = EBL[:, 8 * h:8 * h + 8].rearrange("p (n a) -> p n a", a=2)
                pool.wait_ge(s_bl, 1)
                pool.wait_ge(s_lk, h + 1)
                pool.tensor_copy(mixed[:, :, 0, :], k[:, :, 0, :])
                pool.tensor_copy(mixed[:, :, 1, :], kt[:, :, 1, :]).then_inc(s_lm, 1)
                pool.tensor_copy(q[:, :, 0, :], qt[:, :, 0, :])
                pool.tensor_tensor(q[:, :, 1, :], qt[:, :, 1, :], along(e[:, :, 0], HB), ALU.mult)
                pool.tensor_tensor(k[:, :, 0, :], k[:, :, 0, :], along(e[:, :, 1], HB), ALU.mult).then_inc(s_lg, 1)

        def dve_gla(dve):
            for i in range(GIN):
                split_lo(dve, C_GIN + i + LEAD)
                dve_gla_step(dve, i)
            def gate(i):
                dve.wait_ge(s_hq, H + i + 1)
                dve.scalar_tensor_tensor(out=OO[:, i, :], in0=OO[:, i, :], scalar=hon[:, 1 + i % 2:2 + i % 2],
                                         in1=RS[:, i, :], op0=ALU.mult, op1=ALU.mult).then_inc(s_og, 1)

            def norm(i):
                dve.wait_ge(s_hr, H + i // 2 + 1)
                dve.wait_ge(s_og, i + 1)
                dve.tensor_tensor(OO[:, i, :], OO[:, i, :], hf[:, i // 2 % 2, :], ALU.mult).then_inc(s_on, 1)

            def low(i):
                dve.wait_ge(s_omh, DB + i + 1)
                dve.tensor_tensor(hl[:, i, :], OO[:, i, :], hh[:, i, :], ALU.subtract).then_inc(s_om, 1)

            was_read(dve, O_GIN + GIN - 2)
            for i in range(DB - 1):
                gate(i)
            for i in range(DB - 1):
                norm(i)
            low(0)
            low(1)
            was_read(dve, O_GIN + GIN - 1)
            gate(DB - 1)
            norm(DB - 1)
            for i in range(2, DB):
                low(i)

        def dve_gla_step(dve, i):
            h = i - AT_Z
            if 0 <= h < H:
                z, t = LZ[:, h % 2, :], LZ[:, 2 + h % 2, :]
                dve.wait_ge(s_zl, h + 1)
                dve.scalar_tensor_tensor(out=z, in0=z, scalar=0.0, in1=t, op0=ALU.min, op1=ALU.subtract).then_inc(s_zc, 1)
                dve.wait_ge(s_zc, h + 1)
                dve.tensor_tensor_scan(LB[:, h, :], mk("seg"), z, 0.0, ALU.mult, ALU.add).then_inc(s_lb, 1)
            if i == AT_B:
                dve.wait_ge(s_bl, 1)
                dve.wait_ge(s_lb, H)
                dve.tensor_tensor(DEC, EBL[:, 0:32:2], EBL[:, 1:32:2], ALU.mult).then_inc(s_bl, 1)
            h = i - AT_K
            if 0 <= h < H:
                b = LB[:, h, :].rearrange("p (c r) -> p c r", r=HB)
                if h:
                    dve.wait_ge(s_lk, h)
                dve.tensor_tensor(EX[:, 0, :].rearrange("p (c r) -> p c r", r=HB), along(LB[:, h, HB - 1:S:HB], HB), b,
                                  ALU.subtract).then_inc(s_lx, 1)
                dve.wait_ge(s_le, 3 * (h + 1))
                if h >= 2:
                    dve.wait_ge(s_lg, h - 1)
                    dve.wait_ge(s_lap, h - 1)
                dve.tensor_tensor(QT[:, h % 2, :], LQ[:, h, :], EX[:, 1, :], ALU.mult)
                dve.tensor_tensor(KKT[:, h % 2, S:2 * S], LK[:, h, :], EX[:, 2, :], ALU.mult)
                dve.tensor_tensor(LK[:, h, :], LK[:, h, :], EX[:, 0, :], ALU.mult).then_inc(s_lk, 1)
            h = i - AT_KQ - 1
            if 0 <= h < H:
                dve.wait_ge(s_lap, h + 1)
                dve.tensor_tensor(LA[:, h, :, :], tiles(bank[4 + h % 2][:, :]), spread(mk("incl"), NT), ALU.mult
                                  ).then_inc(s_la, 1)
            k = i - AT_V - 1
            if k in (0, 1):
                for n in (2 * k, 2 * k + 1):
                    dve.wait_ge(s_vp, 2 * n + 2)
                    dve.tensor_copy(VTT[:, n, S:2 * S], bank[5 + 2 * n % 4][:, :]).then_inc(s_vv[1], 1)
            n = i - AT_S - 1
            if 0 <= n < NT - 1:
                if n:
                    dve.wait_ge(s_bl, 2)
                    dve.wait_ge(s_lo, n + 1)
                    dve.wait_ge(s_lss, n)
                    link(dve, dve.tensor_tensor(LST, LST, along(DEC[:, n:4 * H:NT], 2 * P), ALU.mult), v_link, vl)
                dve.wait_ge(s_lds, n + 1)
                for a in range(2):
                    src = bank[4 + a][:, :].rearrange("p (h d) -> p h d", h=2)
                    dst = LST[:, 2 * a:2 * a + 2, :]
                    if n == 0:
                        m = dve.tensor_copy(dst, src)
                    else:
                        m = dve.tensor_tensor(dst, dst, src, ALU.add)
                m.then_inc(s_lss, 1)

        block = ctx.enter_context(nc.Block())

        @block.sync
        def _(sp):
            for a in range(XP):
                part = slice(a * DB // XP, (a + 1) * DB // XP)
                sp.dma_start(x[:, part, :], in_x[:, part, :]).then_inc(s_x[a], 16)
            sp.dma_start(par[:, :], in_par).then_inc(s_par, 16)

            def flow(c, w, count, peel=0):
                for i in range(peel):
                    load(sp, c + i, in_w[w + i])
                with sp.Fori(0, (count - peel) // SLOTS) as it:
                    for j in range(SLOTS):
                        src = in_w[bass.ds(it * SLOTS + (w + peel + j), 1)].rearrange("a p n -> (a p) n")
                        load(sp, c + peel + j, src, it, SLOTS)

            def flow_out(L):
                with sp.Fori(0, 2) as it:
                    for j in range(12):
                        a = j % 3
                        src = in_fo[bass.ds(it * 4 + (DB * L + j // 3), 1), :, a * D:a * D + OUT_SUB[a] * P]
                        load(sp, C_FOUT[L] + j, src.rearrange("a p n -> (a p) n"), it, 12)

            for i in range(SLOTS):
                load(sp, i, in_w[i])
            sp.dma_start(msk[:, :], in_msk).then_inc(s_msk, 16)
            for t in range(2):
                for g in range(2):
                    sp.dma_start(W1[g * DH:(g + 1) * DH, 4 * t:4 * t + 4, :], in_w1[t]).then_inc(s_w1, 16)
                sp.dma_start(W2[:, t, :], in_w2[t]).then_inc(s_w1, 16)
            for i in range(SLOTS, 7):
                load(sp, i, in_w[i])
            flow(C_HIN + 7, W_HIN + 7, HIN - 7)
            flow(C_HOUT, W_HOUT, OUTB)
            flow(C_F0, W_F0, FIN)
            flow_out(0)
            sp.wait_ge(s_g, FB)
            sp.dma_start(AW2[0:16, :], in_aw2).then_inc(s_aw, 16)
            flow(C_GIN, W_GIN, GIN, 1)
            flow(C_GOUT, W_GOUT, OUTB)
            flow(C_F1, W_F1, FIN)
            flow_out(1)
            for a in range(2):
                for d in range(DB):
                    x_updated(sp, 7, d, a)
                    sp.dma_start(out_x[:, d, half(a)], x[:, d, half(a)]).then_inc(s_out, 16)
            sp.wait_ge(s_out, 16 * 2 * DB)

        @block.tensor
        def _(pe):
            pe.wait_ge(s_cst, CONSTS)
            pe_sum_all(pe, 0)
            project(pe, C_HIN, O_HIN, 2 + 2 * SLOTS, 0)
            for o in range(2 + 2 * SLOTS, HIN):
                if o == H_AT:
                    pe_compress_in(pe)
                if o == H_AT + 2:
                    pe_compress_out(pe)
                if S_AT <= o < S_AT + 2:
                    pe_cmp_scores(pe, o - S_AT)
                pe_early(pe, o)
                chunk(pe, o, o, hh, hl)
            pe_cmp(pe)
            pe_attention(pe)
            pe_gdn_prep(pe)
            pe_inverse(pe)
            pe_gdn_scan(pe)
            for a in range(2):
                pe.wait_ge(s_om, NT + (a + 1) * NT // 2)
                for h in range(H):
                    two_block(pe, C_HOUT, O_HOUT, h, False, a == 1 and h == H - 1, half(a))
            pe_outproj(pe, C_HOUT, O_HOUT, 1)
            pe_sum(pe, 2)
            pe_ffn(pe, 0)
            pe_sum(pe, 4)
            pe_gla(pe)
            two_start(pe, C_GOUT, O_GOUT)
            for k in range(DB):
                pe.wait_ge(s_om, DB + k + 1)
                two_block(pe, C_GOUT, O_GOUT, k, k == 0, k == DB - 1)
            pe_outproj(pe, C_GOUT, O_GOUT, 5)
            pe_sum(pe, 6)
            pe_ffn(pe, 1)

        @block.scalar
        def _(act):
            act.wait_ge(s_cst, CONSTS)
            act_pre(act, 0)
            act_hybrid_in(act)
            act_attention(act)
            act_gdn_prep(act)
            act_inverse(act)
            act_gdn_scan(act)
            act_outproj(act, C_HOUT, O_HOUT)
            act_post(act, 1)
            act_pre(act, 2)
            act_ffn(act, 0)
            act_post(act, 3)
            act_pre(act, 4)
            act_gla(act)
            act_outproj(act, C_GOUT, O_GOUT)
            act_post(act, 5)
            act_pre(act, 6)
            act_ffn(act, 1)
            act_post(act, 7)

        @block.gpsimd
        def _(pool):
            pool_gdn(pool)
            pool_post(pool, 1)
            pool_post(pool, 3)
            pool_gla(pool)
            pool_post(pool, 5)
            pool_post(pool, 7)

        @block.vector
        def _(dve):
            dve.memset(ones, 1.0).then_inc(s_cst, 1)
            dve.memset(epsc[:, 0:1], D * EPS).then_inc(s_cst, 1)
            dve.memset(epsc[:, 1:2], EPS).then_inc(s_cst, 1)
            dve.memset(epsc[:, 2:3], P * EPS).then_inc(s_cst, 1)
            dve.memset(epsc[:, 3:4], 2 * P * EPS).then_inc(s_cst, 1)
            dve.memset(onec[:, :], 1.0).then_inc(s_cst, 1)
            dve_sum_start(dve, 0)
            for d in range(DB):
                dve_sum_block(dve, 0, d)
            dve.wait_ge(s_par, 16)
            dve.tensor_scalar(gain[:, :], pr("gain", 0, 8 * DB), D ** 0.5, None, ALU.mult).then_inc(s_cst, 1)
            dve.tensor_scalar(fcw[:, :], pr("fcw", 0, 2 * FIN * FC), 1 / WS, None, ALU.mult).then_inc(s_cst, 1)
            dve.tensor_scalar(gcw[:, :], pr("gcw", 0, 12 * GC), 1 / WS, None, ALU.mult).then_inc(s_cst, 1)
            dve.tensor_scalar(hon[:, 0:1], pr("gon"), P ** 0.5, None, ALU.mult).then_inc(s_cst, 1)
            dve.tensor_scalar(hon[:, 1:3], pr("lon", 0, 2), (2 * P) ** 0.5, None, ALU.mult).then_inc(s_cst, 1)
            dve.memset(cu[:, 0, 0:1], 0.0).then_inc(s_prod, 1)
            dve.memset(cu[:, 0, 1:2], 0.0).then_inc(s_prod, 1)
            for c in range(LEAD):
                split_lo(dve, c)
            dve.wait_ge(s_cst, CONSTS + LATER)
            for a in range(XP):
                dve.wait_ge(s_x[a], 16)
            dve_pre(dve, 0)
            dve_hybrid_in(dve)
            dve_cmp(dve)
            dve_attention(dve)
            dve_gdn_prep(dve)
            dve_inverse(dve)
            dve_gdn_scan(dve)
            dve_outproj(dve, C_HOUT, 1)
            dve_post(dve, 1)
            dve_pre(dve, 2)
            dve_ffn(dve, 0)
            dve_post(dve, 3)
            dve_pre(dve, 4)
            dve_gla(dve)
            dve_outproj(dve, C_GOUT, 5)
            dve_post(dve, 5)
            dve_pre(dve, 6)
            dve_ffn(dve, 1)
            dve_post(dve, 7)


def host_layout(i):
    import numpy as np

    i = {k: np.asarray(v) for k, v in i.items()}

    def cols(w):
        k, n = w.shape
        return w.reshape(k // P, P, n // P, P).transpose(2, 1, 0, 3).reshape(n // P, P, k)

    def rows(a):
        return a.reshape(-1, P).T

    w = i["hyb_w_in"][0]
    at = np.cumsum([0, 3 * H * P, H, H, H * P, NH * DH, 6 * 2 * DH, 3 * NH])
    qkv, beta, dec, gate, qb, kv, gb = (w[:, at[j]:at[j + 1]] for j in range(7))
    small = np.zeros((D, P), w.dtype)
    small[:, 0:H], small[:, 32:32 + H], small[:, 64:64 + 3 * NH] = dec, beta, gb
    qb = qb.reshape(D, 2, 4, DH).transpose(0, 2, 1, 3).reshape(D, NH * DH)
    kv = kv.reshape(D, 6, 2 * DH)[:, [0, 1, 2, 4, 3, 5]].reshape(D, 12 * DH)
    hin = np.concatenate([small, qkv, kv[:, :2 * P], gate, qb, kv[:, 2 * P:]], 1)
    g = i["gla_w_in"][0]
    alr = np.zeros((D, P), g.dtype)
    alr[:, 0:16] = g[:, 3 * D:]
    gin = np.concatenate([alr, g[:, 0:3 * D]], 1)

    def pairs(a):
        return a.reshape(a.shape[:-1] + (2, FB, P)).swapaxes(-3, -2).reshape(a.shape)

    fin = pairs(i["ffn_w_in"])
    in_w = np.concatenate([cols(hin), cols(i["hyb_w_out"][0]), cols(fin[0]), cols(gin), cols(i["gla_w_out"][0]), cols(fin[1])])
    in_fo = np.concatenate([cols(i["ffn_w_out"][0]), cols(i["ffn_w_out"][1])])
    par = np.zeros((P, NPAR), np.float32)

    def put(name, a):
        a = a.reshape(a.shape[0], -1)
        par[0:a.shape[0], PARAM[name][0]:PARAM[name][0] + a.shape[1]] = a

    put("gain", rows(i["norm_gains"]))
    put("fcw", rows(pairs(i["ffn_conv_w"]).transpose(1, 0, 2)))
    put("fcb", rows(pairs(i["ffn_conv_b"])))
    put("gcw", i["gdn_conv_w"][0].reshape(GC, 12, P).transpose(2, 1, 0))
    put("alog", i["gdn_A_log"][0][:, None])
    put("dtb", i["gdn_dt_bias"][0][:, None])
    put("gon", rows(i["gdn_o_norm"]))
    put("b1", rows(i["nsa_cmp_b1"]))
    put("pe", np.concatenate([i["nsa_cmp_pe"][0].transpose(2, 0, 1)] * 2))
    put("lon", rows(i["gla_o_norm"]))
    put("lab", rows(i["gla_a_b"]))
    w2 = i["nsa_cmp_w2"][0]
    return {
        "in_x": i["x"][0].T.reshape(DB, P, S).transpose(1, 0, 2),
        "in_par": par, "in_msk": masks(), "in_w": in_w, "in_fo": in_fo,
        "in_w1": i["nsa_cmp_w1"][0].reshape(2, CL, DH, P).transpose(0, 2, 1, 3).reshape(2, DH, 4, 8 * P),
        "in_w2": np.concatenate([w2, w2], 2),
        "in_aw2": i["gla_a_w2"][0],
    }


def masks():
    import numpy as np

    m = np.zeros((P, NMASK), np.float32)

    def put(name, a):
        m[0:a.shape[0], MASKS[name][0]:MASKS[name][1]] = a

    r = np.arange(P)
    put("ident", np.eye(P))
    put("strict", r[:, None] > r[None, :])
    put("incl", r[:, None] <= r[None, :])
    put("lev", np.concatenate([(r[:, None] >> l + 1 == r[None, :] >> l + 1) & (r[:, None] >> l & 1 == 1)
                               & (r[None, :] >> l & 1 == 0) for l in range(7)], 1))
    neg = np.zeros((P, S))
    neg[:, S - P:] = np.where(r[None, :] > r[:, None], NEG, 0.0)
    put("neg", neg)
    put("seg", np.tile(np.arange(S) % DH != 0, (P, 1)))
    t = r[:, None, None] + P * np.arange(NT)[None, :, None]
    c = np.arange(NCP)[None, None, :]
    ok = ((c * CS + CL - 1 <= t) & (c < NC)).reshape(P, -1)
    put("cadd", np.where(ok, 0.0, NEG))
    put("c01", ok)
    put("sel", np.kron(np.eye(H), np.ones((1, P))))
    return m


def kernel(**inputs):
    import numpy as np
    import concourse.bacc as bacc
    from concourse.bass_utils import run_bass_kernel_spmd

    nc = bacc.Bacc("TRN2", target_bir_lowering=False, num_devices=1)
    arrays = {k: np.ascontiguousarray(a) for k, a in host_layout(inputs).items()}
    aps = {k: nc.dram_tensor(k, a.shape, mybir.dt.from_np(a.dtype), kind="ExternalInput").ap() for k, a in arrays.items()}
    out = nc.dram_tensor("out_x", (P, DB, S), F32, kind="ExternalOutput").ap()
    build(nc, out, **aps)
    r = run_bass_kernel_spmd(nc, [arrays], core_ids=[0])
    o = np.asarray(r.results[0]["out_x"])
    return o.transpose(2, 1, 0).reshape(1, S, D)
```
